# Optimizing a Trainium2 kernel written in Bass

```python
import math
import jax
import jax.numpy as jnp
from jax import lax
import numpy as np

D_MODEL = 1024
BATCH = 1
SEQ = 256
DEPTH = 2

RWKV_HEAD = 64
RWKV_HEADS = D_MODEL // RWKV_HEAD
RWKV_DIM = RWKV_HEADS * RWKV_HEAD
W_LORA = max(32, int(round(1.8 * D_MODEL ** 0.5 / 32)) * 32)
A_LORA = max(32, int(round(1.8 * D_MODEL ** 0.5 / 32)) * 32)
V_LORA = max(32, int(round(1.3 * D_MODEL ** 0.5 / 32)) * 32)
G_LORA = max(32, int(round(0.6 * D_MODEL ** 0.8 / 32)) * 32)
RWKV_GN_EPS = 64e-5
RWKV_COLS = 3 * RWKV_DIM + 2 * W_LORA + 2 * A_LORA + G_LORA

M_EXPAND = 2
M_INNER = M_EXPAND * D_MODEL
M_HEADDIM = 64
M_HEADS = M_INNER // M_HEADDIM
M_GROUPS = 4
M_STATE = 128
M_CONV = 5
M_CHUNK = 128
M_XBC = M_INNER + 2 * M_GROUPS * M_STATE
MAMBA_COLS = M_INNER + M_XBC + 2 * M_HEADS

DIFF_HEADS = D_MODEL // 128
DIFF_HEAD = 64
DIFF_V = 2 * DIFF_HEAD
DIFF_COLS = 3 * DIFF_HEADS * 2 * DIFF_HEAD
Q_BLOCK = 128

N_BRANCH = 3
GATE_COLS = N_BRANCH * D_MODEL
N_IN = RWKV_COLS + MAMBA_COLS + DIFF_COLS + GATE_COLS
D_FF = 256 * ((8 * D_MODEL // 3 + 255) // 256)
N_SUB = 3
EPS = 1e-6

kernel_name = "hybrid_rwkv7_mamba2_diffattn_macaron_encoder"

def _split_points(sizes):
    return [int(s) for s in np.cumsum(sizes)[:-1]]

def rmsnorm(x, w, eps=EPS):
    xf = x.astype(jnp.float32)
    y = xf * lax.rsqrt(jnp.mean(xf * xf, axis=-1, keepdims=True) + eps)
    return (y * w.astype(jnp.float32)).astype(x.dtype)

def modulated_norm(x, w, m):
    return rmsnorm(x, w) * (1.0 + m[:, 1, None]) + m[:, 0, None]

def swiglu(h, w13, w2):
    g, u = jnp.split(h @ w13, 2, axis=-1)
    return (jax.nn.silu(g) * u) @ w2

def centred_shift(s):
    pad = jnp.pad(s, ((0, 0), (1, 1), (0, 0)))
    return 0.5 * (pad[:, :-2] + pad[:, 2:])

def depthwise_conv_centred(x, w):
    k, ch = w.shape
    return lax.conv_general_dilated(
        x, w[:, None, :].astype(x.dtype), window_strides=(1,),
        padding=[((k - 1) // 2, (k - 1) // 2)],
        dimension_numbers=("NWC", "WIO", "NWC"), feature_group_count=ch)

def alibi_slopes(n_heads):
    return jnp.asarray(2.0 ** (-8.0 * np.arange(1, n_heads + 1) / n_heads), jnp.float32)

def rwkv7_scan(r, w, k, v, a, b, reverse):
    bsz, _, h, n = r.shape

    def step(state, inp):
        r_t, w_t, k_t, v_t, a_t, b_t = inp
        sa = jnp.einsum("bhij,bhj->bhi", state, a_t)
        state = (state * w_t[:, :, None, :] + sa[..., None] * b_t[:, :, None, :]
                 + v_t[..., None] * k_t[:, :, None, :])
        return state, jnp.einsum("bhij,bhj->bhi", state, r_t)

    xs = tuple(jnp.moveaxis(t, 1, 0) for t in (r, w, k, v, a, b))
    s0 = jnp.zeros((bsz, h, n, n), jnp.float32)
    _, y = lax.scan(step, s0, xs, reverse=reverse)
    return jnp.moveaxis(y, 0, 1)

def rwkv7_branch(p, w0, w2, a0, a2, g2, k_k, k_a, r_k, ln_w, ln_b, v_first, vres):
    bsz, s, _ = p.shape
    f32 = jnp.float32
    r, k, v, cw, ca, cg = jnp.split(
        p, _split_points([RWKV_DIM, RWKV_DIM, RWKV_DIM, 2 * W_LORA, 2 * A_LORA, G_LORA]), axis=-1)
    if vres is None:
        v_first = v
    else:
        v0, v1, v2 = vres
        v = v + (v_first - v) * jax.nn.sigmoid(v0 + (v @ v1) @ v2)
    w_log = -jax.nn.softplus(-(w0 + jnp.einsum("bsdr,drc->bsdc", jnp.tanh(cw.reshape(bsz, s, 2, W_LORA)), w2))) - 0.5
    decay = jnp.exp(-jnp.exp(w_log.astype(f32)))
    iclr = jax.nn.sigmoid(a0 + jnp.einsum("bsdr,drc->bsdc", ca.reshape(bsz, s, 2, A_LORA), a2)).astype(f32)
    gate = jax.nn.sigmoid(cg) @ g2

    def heads(t):
        return t.reshape(t.shape[:2] + (RWKV_HEADS, RWKV_HEAD)).astype(f32)

    kk = heads(k * k_k)
    kk = kk * lax.rsqrt(jnp.sum(kk * kk, axis=-1, keepdims=True) + 1e-12)
    k_dir = k.astype(f32)[:, :, None] * (1.0 + (iclr - 1.0) * k_a.astype(f32))
    rh, vh = heads(r), heads(v)
    y_fwd = rwkv7_scan(rh, heads(decay[:, :, 0]), heads(k_dir[:, :, 0]), vh, -kk,
                       kk * heads(iclr[:, :, 0]), reverse=False)
    y_bwd = rwkv7_scan(rh, heads(decay[:, :, 1]), heads(k_dir[:, :, 1]), vh, -kk,
                       kk * heads(iclr[:, :, 1]), reverse=True)
    y = y_fwd + y_bwd
    mu = jnp.mean(y, axis=-1, keepdims=True)
    var = jnp.mean(jnp.square(y - mu), axis=-1, keepdims=True)
    yn = ((y - mu) * lax.rsqrt(var + RWKV_GN_EPS)).reshape(bsz, s, RWKV_DIM) * ln_w + ln_b
    bonus = jnp.sum(rh * heads(k_dir[:, :, 0] + k_dir[:, :, 1]) * r_k, axis=-1, keepdims=True) * vh
    out = (yn + bonus.reshape(bsz, s, RWKV_DIM)) * gate
    return out.astype(p.dtype), v_first

def ssd_chunked(xdt, da, bg, cg):
    bsz, s, h, p = xdt.shape
    g, n = bg.shape[2], bg.shape[3]
    r = h // g
    nc = s // M_CHUNK
    xc = xdt.reshape(bsz, nc, M_CHUNK, g, r, p)
    ac = da.reshape(bsz, nc, M_CHUNK, g, r)
    bc = bg.reshape(bsz, nc, M_CHUNK, g, n)
    cc = cg.reshape(bsz, nc, M_CHUNK, g, n)
    a_cs = jnp.cumsum(ac, axis=2)
    lower = jnp.tril(jnp.ones((M_CHUNK, M_CHUNK), bool))[None, None, :, :, None, None]
    seg = a_cs[:, :, :, None] - a_cs[:, :, None, :]
    lmat = jnp.exp(jnp.where(lower, seg, -jnp.inf))
    cb = jnp.einsum("bclgn,bcsgn->bclsg", cc, bc)
    y_diag = jnp.einsum("bclsgr,bcsgrp->bclgrp", cb[..., None] * lmat, xc)
    decay_to_end = jnp.exp(a_cs[:, :, -1:] - a_cs)
    states = jnp.einsum("bclgn,bclgrp->bcgrpn", bc, xc * decay_to_end[..., None])
    chunk_decay = jnp.exp(a_cs[:, :, -1])

    def carry_step(hs, inp):
        dec, st = inp
        return hs * dec[..., None, None] + st, hs

    h0 = jnp.zeros((bsz, g, r, p, n), xdt.dtype)
    _, h_prev = lax.scan(carry_step, h0, (jnp.moveaxis(chunk_decay, 1, 0), jnp.moveaxis(states, 1, 0)))
    h_prev = jnp.moveaxis(h_prev, 0, 1)
    y_off = jnp.einsum("bclgn,bcgrpn->bclgrp", cc, h_prev) * jnp.exp(a_cs)[..., None]
    return (y_diag + y_off).reshape(bsz, s, h, p)

def mamba2_branch(p, conv_w, conv_b, dt_bias, a_log, d_skip, norm_w):
    bsz, s, _ = p.shape
    f32 = jnp.float32
    z, xbc, dt_raw = jnp.split(p, _split_points([M_INNER, M_XBC, 2 * M_HEADS]), axis=-1)
    xbc = jax.nn.silu(depthwise_conv_centred(xbc, conv_w) + conv_b)
    xm, bm, cm = jnp.split(xbc, _split_points([M_INNER, M_GROUPS * M_STATE, M_GROUPS * M_STATE]), axis=-1)
    xh = xm.reshape(bsz, s, M_HEADS, M_HEADDIM).astype(f32)
    bg = bm.reshape(bsz, s, M_GROUPS, M_STATE).astype(f32)
    cg = cm.reshape(bsz, s, M_GROUPS, M_STATE).astype(f32)
    dt = jax.nn.softplus(dt_raw.reshape(bsz, s, 2, M_HEADS).astype(f32) + dt_bias)
    a = -jnp.exp(a_log.astype(f32))
    y_fwd = ssd_chunked(xh * dt[:, :, 0, :, None], dt[:, :, 0] * a[0], bg, cg)
    y_bwd = jnp.flip(ssd_chunked(jnp.flip(xh * dt[:, :, 1, :, None], 1), jnp.flip(dt[:, :, 1] * a[1], 1),
                                 jnp.flip(bg, 1), jnp.flip(cg, 1)), 1)
    y = y_fwd + y_bwd + d_skip.astype(f32)[:, None] * xh
    y = y.reshape(bsz, s, M_INNER) * jax.nn.silu(z.astype(f32))
    y = rmsnorm(y.reshape(bsz, s, M_GROUPS, M_INNER // M_GROUPS),
                norm_w.reshape(M_GROUPS, M_INNER // M_GROUPS), 1e-5)
    return y.reshape(bsz, s, M_INNER).astype(p.dtype)

def diff_attention_branch(p, lam_vecs, subln_w, lambda_init):
    bsz, s, _ = p.shape
    q, k, v = jnp.split(p, 3, axis=-1)
    q = q.reshape(bsz, s, DIFF_HEADS, 2, DIFF_HEAD)
    k = k.reshape(bsz, s, DIFF_HEADS, 2, DIFF_HEAD)
    v = v.reshape(bsz, s, DIFF_HEADS, DIFF_V)
    lv = lam_vecs.astype(jnp.float32)
    lam = jnp.exp(jnp.sum(lv[0] * lv[1])) - jnp.exp(jnp.sum(lv[2] * lv[3])) + lambda_init
    slopes = alibi_slopes(DIFF_HEADS)
    pos = jnp.arange(s, dtype=jnp.int32)
    nb = s // Q_BLOCK
    qb = jnp.moveaxis(q.reshape(bsz, nb, Q_BLOCK, DIFF_HEADS, 2, DIFF_HEAD), 1, 0)
    pb = pos.reshape(nb, Q_BLOCK)
    scale = DIFF_HEAD ** -0.5

    def block(args):
        qi, pi = args
        sc = jnp.einsum("bqhmd,bkhmd->bhmqk", qi, k).astype(jnp.float32) * scale
        dist = jnp.abs(pi[:, None] - pos[None, :]).astype(jnp.float32)
        sc = sc - slopes[None, :, None, None, None] * dist[None, None, None]
        pm = jax.nn.softmax(sc, axis=-1)
        amap = pm[:, :, 0] - lam * pm[:, :, 1]
        return jnp.einsum("bhqk,bkhe->bqhe", amap.astype(v.dtype), v)

    o = lax.map(block, (qb, pb))
    o = jnp.moveaxis(o, 0, 1).reshape(bsz, s, DIFF_HEADS, DIFF_V)
    o = rmsnorm(o, subln_w, 1e-5) * (1.0 - lambda_init)
    return o.reshape(bsz, s, DIFF_HEADS * DIFF_V)

def token_mixer(h, w_in, rwkv_mu, rwkv_params, vres, v_first, mamba_params,
                lam_vecs, subln_w, lambda_init, w_br_r, w_br_m, w_br_d, w_out):
    bsz, s, _ = h.shape
    proj = h @ w_in
    p_r, p_m, p_d, p_g = jnp.split(proj, _split_points([RWKV_COLS, MAMBA_COLS, DIFF_COLS, GATE_COLS]), axis=-1)
    p_r = p_r + rwkv_mu * (centred_shift(p_r) - p_r)
    y_r, v_first = rwkv7_branch(p_r, *rwkv_params, v_first, vres)
    y_m = mamba2_branch(p_m, *mamba_params)
    y_d = diff_attention_branch(p_d, lam_vecs, subln_w, lambda_init)
    g = jax.nn.sigmoid(p_g).reshape(bsz, s, N_BRANCH, D_MODEL)
    merged = g[:, :, 0] * (y_r @ w_br_r) + g[:, :, 1] * (y_m @ w_br_m) + g[:, :, 2] * (y_d @ w_br_d)
    return merged @ w_out, v_first

def setup_inputs(seed: int = 0) -> dict:
    key = jax.random.key(seed)
    ks = iter(jax.random.split(key, 64))
    f32 = jnp.float32

    def nrm(shape, scale):
        return scale * jax.random.normal(next(ks), shape, f32)

    def unif(shape, lo, hi):
        return jax.random.uniform(next(ks), shape, f32, minval=lo, maxval=hi)

    x = nrm((BATCH, SEQ, D_MODEL), 1.0)
    c = nrm((BATCH, D_MODEL), 1.0)
    ada_w = nrm((DEPTH, D_MODEL, N_SUB * 3 * D_MODEL), D_MODEL ** -0.5)
    ada_b = nrm((DEPTH, N_SUB * 3 * D_MODEL), 0.02)
    norm_w = 1.0 + nrm((DEPTH, 2 * N_SUB, D_MODEL), 0.05)
    ffn_w13 = nrm((DEPTH, 2, D_MODEL, 2 * D_FF), D_MODEL ** -0.5)
    ffn_w2 = nrm((DEPTH, 2, D_FF, D_MODEL), D_FF ** -0.5)
    w_in = nrm((DEPTH, D_MODEL, N_IN), D_MODEL ** -0.5)
    rwkv_mu = unif((DEPTH, RWKV_COLS), 0.0, 1.0)
    rwkv_w0 = unif((DEPTH, 2, RWKV_DIM), -3.0, 0.0)
    rwkv_w2 = nrm((DEPTH, 2, W_LORA, RWKV_DIM), W_LORA ** -0.5)
    rwkv_a0 = nrm((DEPTH, 2, RWKV_DIM), 0.1)
    rwkv_a2 = nrm((DEPTH, 2, A_LORA, RWKV_DIM), A_LORA ** -0.5)
    rwkv_g2 = nrm((DEPTH, G_LORA, RWKV_DIM), G_LORA ** -0.5)
    rwkv_k_k = 0.85 + nrm((DEPTH, RWKV_DIM), 0.05)
    rwkv_k_a = 1.0 + nrm((DEPTH, RWKV_DIM), 0.05)
    rwkv_r_k = nrm((DEPTH, RWKV_HEADS, RWKV_HEAD), 0.1)
    rwkv_ln_w = 1.0 + nrm((DEPTH, RWKV_DIM), 0.05)
    rwkv_ln_b = nrm((DEPTH, RWKV_DIM), 0.02)
    rwkv_v0 = nrm((DEPTH - 1, RWKV_DIM), 0.1)
    rwkv_v1 = nrm((DEPTH - 1, RWKV_DIM, V_LORA), RWKV_DIM ** -0.5)
    rwkv_v2 = nrm((DEPTH - 1, V_LORA, RWKV_DIM), V_LORA ** -0.5)
    mamba_conv_w = nrm((DEPTH, M_CONV, M_XBC), M_CONV ** -0.5)
    mamba_conv_b = nrm((DEPTH, M_XBC), 0.02)
    dt0 = jnp.exp(unif((DEPTH, 2, M_HEADS), math.log(1e-3), math.log(1e-1)))
    mamba_dt_bias = dt0 + jnp.log(-jnp.expm1(-dt0))
    mamba_a_log = jnp.log(unif((DEPTH, 2, M_HEADS), 1.0, 16.0))
    mamba_d = 1.0 + nrm((DEPTH, M_HEADS), 0.1)
    mamba_norm_w = 1.0 + nrm((DEPTH, M_INNER), 0.05)
    diff_lambda = nrm((DEPTH, 4, DIFF_HEAD), 0.1)
    diff_subln_w = 1.0 + nrm((DEPTH, DIFF_V), 0.05)
    w_branch_rwkv = nrm((DEPTH, RWKV_DIM, D_MODEL), RWKV_DIM ** -0.5)
    w_branch_mamba = nrm((DEPTH, M_INNER, D_MODEL), M_INNER ** -0.5)
    w_branch_diff = nrm((DEPTH, DIFF_HEADS * DIFF_V, D_MODEL), (DIFF_HEADS * DIFF_V) ** -0.5)
    w_out = nrm((DEPTH, D_MODEL, D_MODEL), D_MODEL ** -0.5)
    return {"x": x, "c": c, "ada_w": ada_w, "ada_b": ada_b, "norm_w": norm_w,
            "ffn_w13": ffn_w13, "ffn_w2": ffn_w2, "w_in": w_in, "rwkv_mu": rwkv_mu,
            "rwkv_w0": rwkv_w0, "rwkv_w2": rwkv_w2, "rwkv_a0": rwkv_a0, "rwkv_a2": rwkv_a2,
            "rwkv_g2": rwkv_g2, "rwkv_k_k": rwkv_k_k, "rwkv_k_a": rwkv_k_a, "rwkv_r_k": rwkv_r_k,
            "rwkv_ln_w": rwkv_ln_w, "rwkv_ln_b": rwkv_ln_b, "rwkv_v0": rwkv_v0, "rwkv_v1": rwkv_v1,
            "rwkv_v2": rwkv_v2, "mamba_conv_w": mamba_conv_w, "mamba_conv_b": mamba_conv_b,
            "mamba_dt_bias": mamba_dt_bias, "mamba_a_log": mamba_a_log, "mamba_d": mamba_d,
            "mamba_norm_w": mamba_norm_w, "diff_lambda": diff_lambda, "diff_subln_w": diff_subln_w,
            "w_branch_rwkv": w_branch_rwkv, "w_branch_mamba": w_branch_mamba,
            "w_branch_diff": w_branch_diff, "w_out": w_out}

def reference(x, c, ada_w, ada_b, norm_w, ffn_w13, ffn_w2, w_in, rwkv_mu,
              rwkv_w0, rwkv_w2, rwkv_a0, rwkv_a2, rwkv_g2, rwkv_k_k, rwkv_k_a, rwkv_r_k,
              rwkv_ln_w, rwkv_ln_b, rwkv_v0, rwkv_v1, rwkv_v2, mamba_conv_w, mamba_conv_b,
              mamba_dt_bias, mamba_a_log, mamba_d, mamba_norm_w, diff_lambda, diff_subln_w,
              w_branch_rwkv, w_branch_mamba, w_branch_diff, w_out):
    bsz = x.shape[0]
    c_act = jax.nn.silu(c)
    v_first = None
    for l in range(DEPTH):
        mod = (c_act @ ada_w[l] + ada_b[l]).reshape(bsz, N_SUB, 3, D_MODEL)
        h = modulated_norm(x, norm_w[l, 0], mod[:, 0])
        x = x + 0.5 * mod[:, 0, 2, None] * rmsnorm(swiglu(h, ffn_w13[l, 0], ffn_w2[l, 0]), norm_w[l, 1])
        h = modulated_norm(x, norm_w[l, 2], mod[:, 1])
        vres = None if l == 0 else (rwkv_v0[l - 1], rwkv_v1[l - 1], rwkv_v2[l - 1])
        rwkv_params = (rwkv_w0[l], rwkv_w2[l], rwkv_a0[l], rwkv_a2[l], rwkv_g2[l], rwkv_k_k[l],
                       rwkv_k_a[l], rwkv_r_k[l], rwkv_ln_w[l], rwkv_ln_b[l])
        mamba_params = (mamba_conv_w[l], mamba_conv_b[l], mamba_dt_bias[l], mamba_a_log[l],
                        mamba_d[l], mamba_norm_w[l])
        lambda_init = 0.8 - 0.6 * math.exp(-0.3 * l)
        y, v_first = token_mixer(h, w_in[l], rwkv_mu[l], rwkv_params, vres, v_first, mamba_params,
                                 diff_lambda[l], diff_subln_w[l], lambda_init,
                                 w_branch_rwkv[l], w_branch_mamba[l], w_branch_diff[l], w_out[l])
        x = x + mod[:, 1, 2, None] * rmsnorm(y, norm_w[l, 3])
        h = modulated_norm(x, norm_w[l, 4], mod[:, 2])
        x = x + 0.5 * mod[:, 2, 2, None] * rmsnorm(swiglu(h, ffn_w13[l, 1], ffn_w2[l, 1]), norm_w[l, 5])
    return x


_drawn_inputs = setup_inputs


def setup_inputs(seed=0):
    import zlib

    import numpy as np

    out = dict(_drawn_inputs(seed))
    spreads = {}
    factors = {'rwkv_a0': 4.617,
     'rwkv_ln_w': 4.103,
     'rwkv_ln_b': 23.772,
     'rwkv_v0': 6.859,
     'mamba_conv_b': 15.115,
     'mamba_d': 24.172,
     'diff_subln_w': 3.251,
     'mamba_norm_w': 5.656}
    for name, (base, spread) in spreads.items():
        noise = np.random.default_rng([zlib.crc32(name.encode()), seed]).standard_normal(out[name].shape)
        drawn = base * np.exp(spread * noise) if base else spread * noise
        out[name] = jnp.asarray(drawn.astype(out[name].dtype))
    for name, factor in factors.items():
        out[name] = (out[name] * factor).astype(out[name].dtype)
    return out
```

```python
from contextlib import ExitStack, contextmanager
import math

import concourse.bass as bass
from concourse import mybir

F32 = mybir.dt.float32
I32 = mybir.dt.int32
ALU = mybir.AluOpType
ACT = mybir.ActivationFunctionType
AX = mybir.AxisListType.X
ds = bass.ds

P = 128
D = 1024
KT = D // P
S = 256
TT = S // P
DEPTH = 2
FF = 2816
FJ = FF // 256
RW = 3488
MB0 = RW
XBC0 = MB0 + 2048
DT0 = XBC0 + 3072
DF0 = DT0 + 64
GT0 = DF0 + 3072
NIN = GT0 + 3072
PAIRS = 8
L = 64
CH = S // L
LV = 5

IT_ADA, IT_FFA, IT_RW, IT_MR, IT_Z, IT_XBC, IT_MM, IT_DF, IT_MD, IT_OUT, IT_FFB, N_ITEM = (
    0, 18, 29, 37, 41, 45, 51, 57, 63, 67, 69, 80)


def group_of(item):
    return item - (item > 52) - (item > 55)


N_GROUP = group_of(N_ITEM)


def loads_before(item, parity):
    return sum(2 if IT_FFA <= n < IT_RW or n >= IT_FFB else 1 for n in range(item) if n % 2 == parity)

C_CONVW, C_V0 = 0, 120
C_ADAB, C_NORM, C_KK = 128, 200, 248
C_W0, C_A0, C_KA, C_RK, C_LNW, C_LNB, C_MNW, C_CONVB, C_SUB = 256, 272, 288, 296, 304, 312, 320, 336, 360
C_MU = 384
E_OMU, E_HMU, E_W0H, E_A0H, E_KA1, E_SUB, N_DER = 0, 28, 56, 72, 88, 96, 97

SCRATCH = 28400
NEG_EXP_HALF = -0.5 * math.exp(-0.5)


class Signal:

    def __init__(self, sem, per_layer, by=1):
        self.sem, self.per_layer, self.by = sem, per_layer, by

    def __call__(self, l, k):
        return self.sem, (l * self.per_layer + k) * self.by


class Serial:

    def __init__(self, eng, sem, settled):
        self.eng, self.sem, self.settled, self.n = eng, sem, settled, 0

    def step(self, ins):
        self.n += 1
        ins.then_inc(self.sem, 1)
        self.eng.wait_ge(self.sem, self.n)

    def raise_(self, ins, sem, value):
        ins.then_inc(sem, 1)
        self.eng.wait_ge(sem, value)

    def restart(self):
        if self.n:
            self.eng.wait_ge(self.sem, self.n)
            self.eng.sem_inc(self.settled, 1)
            self.eng.sem_clear(self.sem)
        self.n = 0


def build(nc, a, out):
    with ExitStack() as ctx:
        def sb(name, shape):
            return ctx.enter_context(nc.sbuf_tensor(name, shape, F32))

        def signal(name, per_layer, by=1):
            return Signal(ctx.enter_context(nc.semaphore(name)), per_layer, by)

        ring = sb("ring", [P, 2, 4096])
        x = sb("x", [P, TT, D])
        hT = sb("hT", [P, KT, S])
        gbc = sb("gbc", [P, 3, D])
        prow = sb("prow", [P, 4, P])
        prm = sb("prm", [P, 512])
        der = sb("der", [P, N_DER])
        modc = sb("modc", [P, 48])
        vfirst = sb("vfirst", [P, KT, S])
        merged = sb("merged", [P, TT, D])
        ident = sb("ident", [P, P])
        ones = sb("ones", [P, P])
        onesblk = sb("onesblk", [P, 2, L])
        stack_i = sb("stack_i", [P, L])
        tri = sb("tri", [P, 2, P])
        rmask = sb("rmask", [P, 2, 2, P])
        lvl = sb("lvl", [P, 2, LV + 1, P])
        reset = sb("reset", [P, 2 * CH, L])
        dist = sb("dist", [P, TT, S])
        slopes = sb("slopes", [P, 8])
        halfc = sb("halfc", [P, 3])
        laminit = sb("laminit", [P, DEPTH, 2])
        mhalf = sb("mhalf", [P, 8])
        ccol = sb("ccol", [P, KT])
        crow = sb("crow", [8, P])
        stat = sb("stat", [P, 16])
        U = sb("scratch", [P, SCRATCH])

        def carver():
            at = [0]

            def carve(shape, parts=P):
                n = 1
                for s in shape:
                    n *= s
                v = U[0:parts, at[0]:at[0] + n]
                at[0] += n
                assert at[0] <= SCRATCH, at[0]
                names = "abcde"[:len(shape)]
                if len(shape) == 1:
                    return v
                return v.rearrange("p (%s) -> p %s" % (" ".join(names), " ".join(names)),
                                   **{c: s for c, s in zip(names, shape)})
            return carve, at

        carve, at = carver()
        xn = carve([TT, D])
        w2s = carve([2, 2, D])
        sgm = carve([2, 512])
        actT = carve([2, 2, S])
        yt = carve([D])
        nbc = carve([3, D])

        carve, at = carver()
        rkv = carve([24, S])
        cw = carve([S])
        ca = carve([S])
        cg = carve([S])
        cg2 = carve([S], 32)
        kkT = carve([PAIRS, S])
        lora = carve([3, P])
        g2b = carve([P], 32)
        vfd_at = at[0]
        lwb = carve([2, CH, L])
        icl = carve([2, CH, L])
        gi = carve([2, CH, L])
        ge = carve([2, CH, L])
        kdir = carve([2, S])
        kb = carve([2, CH, L])
        etot = carve([2, CH])
        bprod = carve([S])
        bonus = carve([S])
        gate = carve([S])
        vX = carve([CH, 2, L])
        vtm = carve([CH, L])
        arX = carve([2, CH, 2, 2, L])
        btX = carve([2, CH, 2, L])
        ktX = carve([2, CH, 2, L])
        btm_at = at[0]
        btm = carve([2, CH, P])
        ktm = carve([2, CH, P])
        mb_at = at[0]
        mb = carve([2, CH, 2, P])
        mk = carve([2, CH, 2, P])
        dd = carve([2, CH, 2, P])
        ee_at = at[0]
        ee = carve([2, CH, P])
        rs = carve([2, L])
        yX = carve([CH, 2, L])
        gstat = carve([4, CH])
        st8 = U[:, ee_at:ee_at + 512].rearrange("p (j d v) -> p j d v", j=CH, d=2)
        us = U[:, ee_at + 512:ee_at + 1024].rearrange("p (j d v) -> p j d v", j=CH, d=2)
        yy = U[:, btm_at:btm_at + S].rearrange("p (c v) -> p c v", c=CH)
        ysq = U[:, btm_at + S:btm_at + 2 * S].rearrange("p (c v) -> p c v", c=CH)
        ege, egi, eni = ge, gi, lwb
        v1s = U[:, mb_at:mb_at + 256].rearrange("p (k n) -> p k n", k=KT)
        v2s = U[0:32, mb_at + 256:mb_at + 1280]
        vrs = U[0:32, mb_at + 1280:mb_at + 1536]
        vtmp = U[:, mb_at + 1536:mb_at + 2048]
        vfd = U[:, vfd_at:vfd_at + KT * S].rearrange("p (k s) -> p k s", k=KT)
        kk_sq_buf = merged[:, :, :].rearrange("p t (k s) -> p (t k) s", s=S)

        sg = U[:, 20480:21504].rearrange("p (a b) -> p a b", a=TT)

        carve, at = carver()
        zy = carve([4, TT, 512])
        xtm = carve([TT, 2048])
        bcT = carve([8, S])
        btk = carve([TT, 512])
        wdt = carve([KT, 64])
        dtb = carve([64])
        alog = carve([64])
        dskip = carve([32])
        dts = carve([8, TT, 64])
        acsT = carve([S], 64)
        bg = carve([S])
        cgm = carve([S])
        btg = carve([TT, P])
        cbm = carve([2, TT, P])
        bca = carve([2, 8, P])
        wx_at = at[0]
        wx = carve([4, 8, P])
        cv = U[:, wx_at:wx_at + 2048].rearrange("p (i m s) -> p i m s", i=2, m=4)
        cvs = U[:, wx_at + 2048:wx_at + 3072]
        xdt = carve([4, 8, 64])
        xs = carve([8, 64])
        h0 = carve([512])
        ym = carve([TT, 512])
        ytmp = carve([512])
        mstat = carve([16])

        carve, at = carver()
        qkT = carve([16, S])
        vdm = carve([TT, D])
        qX = carve([2, S])
        sc = carve([TT, 2, S])
        pr = carve([TT, 2, S])
        am = carve([TT, S])
        amT = carve([TT, S])
        on = carve([TT, P])
        ydT = carve([8, S])
        dlam = carve([4, 64])
        dstat = carve([32])

        ps = ctx.enter_context(nc.psum_tensor("ps", [P, 8, 512], F32))
        disti = U[:, TT * S:2 * TT * S].bitcast(I32).rearrange("p (t s) -> p t s", t=TT)
        sc_const = U[:, 0:TT * S].rearrange("p (t s) -> p t s", t=TT)
        acs_dram = nc.dram_tensor("acs_scratch", (64, S), F32).ap()

        consts_ready = signal("consts_ready", 0)
        x_loaded = signal("x_loaded", 0, 16)
        c_loaded = signal("c_loaded", 0, 16)
        c_turned = signal("c_turned", 0)
        c_sig = signal("c_sig", 0)
        c_ready = signal("c_ready", 0)
        out_stored = signal("out_stored", 0, 16)
        dve_own = ctx.enter_context(nc.semaphore("dve_own"))
        act_own = ctx.enter_context(nc.semaphore("act_own"))
        pool_own = ctx.enter_context(nc.semaphore("pool_own"))
        settled = ctx.enter_context(nc.semaphore("settled"))

        layer_open = signal("layer_open", 1)
        params_loaded = signal("params_loaded", 15, 16)
        params_turned = signal("params_turned", 1)
        bc_loaded = signal("bc_loaded", 3, 16)
        slot_loaded = [signal(f"slot_loaded{i}", loads_before(N_ITEM, i), 16) for i in range(2)]
        group_done = signal("group_done", N_GROUP)
        group_evacuated = signal("group_evacuated", N_GROUP)
        sumsq_done = signal("sumsq_done", 6)
        mean_ready = signal("mean_ready", 6)
        rstd_ready = signal("rstd_ready", 6)
        xn_ready = signal("xn_ready", 3)
        x_updated = signal("x_updated", 3)
        xn_turned = signal("xn_turned", 3)
        hT_ready = signal("hT_ready", 4)
        ffn_sig = signal("ffn_sig", 2 * FJ)
        w2_loaded = [signal("w2_loaded0", 12, 16), signal("w2_loaded1", 10, 16)]
        down_done = signal("down_done", 2 * FJ)
        shift_scaled = signal("shift_scaled", 8)
        lora_act = signal("lora_act", 1)
        vlow_done = signal("vlow_done", 1)
        vlow_evac = signal("vlow_evac", 1)
        vmix_done = signal("vmix_done", 4)
        vmix_sig = signal("vmix_sig", 4)
        v_final = signal("v_final", 4)
        kk_sq = signal("kk_sq", 1)
        kk_sum = signal("kk_sum", 1)
        kk_root = signal("kk_root", 1)
        kk_eps = signal("kk_eps", 1)
        vfirst_kept = signal("vfirst_kept", 0)
        rwkv_w_loaded = signal("rwkv_w_loaded", 2, 16)
        pair_w_loaded = signal("pair_w_loaded", 4 * PAIRS, 16)
        lora_done = signal("lora_done", PAIRS)
        lora_evac = signal("lora_evac", PAIRS)
        decay_ready = signal("decay_ready", PAIRS)
        exps_ready = signal("exps_ready", PAIRS)
        bonus_done = signal("bonus_done", PAIRS)
        bonus_evac = signal("bonus_evac", PAIRS)
        ops_ready = signal("ops_ready", 2 * PAIRS)
        turned_done = signal("turned_done", 2 * PAIRS)
        m1_done = signal("m1_done", 2 * PAIRS)
        turned_evac = signal("turned_evac", 2 * PAIRS)
        m2_done = signal("m2_done", 2 * PAIRS)
        m2_evac = signal("m2_evac", 2 * PAIRS)
        f_done = signal("f_done", 2 * LV * PAIRS)
        e_ready = signal("e_ready", 2 * LV * PAIRS)
        de_done = signal("de_done", 2 * LV * PAIRS)
        dd_ready = signal("dd_ready", 2 * LV * PAIRS)
        r_done = signal("r_done", 4 * PAIRS)
        r_evac = signal("r_evac", 4 * PAIRS)
        u_done = signal("u_done", 4 * PAIRS)
        u_evac = signal("u_evac", 4 * PAIRS)
        s_done = signal("s_done", 3 * PAIRS)
        s_evac = signal("s_evac", 3 * PAIRS)
        y_done = signal("y_done", PAIRS)
        gn_var = signal("gn_var", PAIRS)
        gn_rstd = signal("gn_rstd", PAIRS)
        yx_ready = signal("yx_ready", PAIRS)
        yt_done = signal("yt_done", PAIRS)
        yr_ready = signal("yr_ready", PAIRS)
        gate_sig = signal("gate_sig", 6)
        z_sig = signal("z_sig", 4)
        conv_scaled = signal("conv_scaled", 6)
        conv_raw = signal("conv_raw", 6)
        conv_sig = signal("conv_sig", 6)
        conv_turned = signal("conv_turned", 5)
        conv_evac = signal("conv_evac", 5)
        mamba_w_loaded = signal("mamba_w_loaded", 4, 16)
        dt_done = signal("dt_done", 1)
        dt_raw = signal("dt_raw", 1)
        dt_exp = signal("dt_exp", 1)
        da_ready = signal("da_ready", 1)
        acs_done = signal("acs_done", 1)
        acs_evac = signal("acs_evac", 1)
        acs_turned = signal("acs_turned", 1)
        acs_diff = signal("acs_diff", 1)
        acs_exp = signal("acs_exp", 1)
        acs_stored = signal("acs_stored", 1, 16)
        acs_bc = [signal(f"acs_bc{i}", 8, 16) for i in range(2)]
        group_staged = signal("group_staged", 4)
        cb_done = signal("cb_done", 4)
        cb_evac = signal("cb_evac", 4)
        seg_ready = signal("seg_ready", 16)
        seg_exp = signal("seg_exp", 16)
        wx_ready = signal("wx_ready", 8)
        ydiag_done = signal("ydiag_done", 8)
        ydiag_evac = signal("ydiag_evac", 8)
        xs_ready = signal("xs_ready", 8)
        state_done = signal("state_done", 8)
        state_evac = signal("state_evac", 8)
        yoff_done = signal("yoff_done", 8)
        yoff_evac = signal("yoff_evac", 8)
        msq_ready = signal("msq_ready", 4)
        mrstd_ready = signal("mrstd_ready", 4)
        ym_ready = signal("ym_ready", 4)
        ym_turned = signal("ym_turned", 4)
        ymT_ready = signal("ymT_ready", 4)
        diff_w_loaded = signal("diff_w_loaded", 1, 16)
        lam_raw = signal("lam_raw", 1)
        lam_exp = signal("lam_exp", 1)
        qx_ready = signal("qx_ready", 8)
        sc_done = signal("sc_done", 8)
        smax_ready = signal("smax_ready", 8)
        p_ready = signal("p_ready", 8)
        am_ready = signal("am_ready", 8)
        am_turned = signal("am_turned", 8)
        amT_ready = signal("amT_ready", 8)
        o_done = signal("o_done", 8)
        o_sq = signal("o_sq", 8)
        o_mean = signal("o_mean", 8)
        o_rstd = signal("o_rstd", 8)
        on_ready = signal("on_ready", 8)
        on_turned = signal("on_turned", 8)
        yd_ready = signal("yd_ready", 8)
        merged_turned = signal("merged_turned", 1)

        def settle(eng):
            eng.sem_inc(settled, 1)

        @contextmanager
        def loop(eng, first, end):
            settle(eng)
            with eng.Fori(first, end) as i:
                yield i
                settle(eng)

        @contextmanager
        def when(eng, condition):
            settle(eng)
            with eng.If(condition):
                yield
                settle(eng)

        block = ctx.enter_context(nc.Block())

        def halves(pair):
            return ps[:, 2 * pair:2 * pair + 2, :]

        def row(dram, l):
            return dram[ds(l, 1)]

        @block.sync
        def _(sp):
            sp.dma_start(x[:, :, :], a["x"].rearrange("a (t p) n -> p (a t) n", p=P)).then_inc(x_loaded.sem, 16)

            def load(l, item, parity, src, cols=512, free_after=None):
                dst = ring[:, parity, 0:KT * cols].rearrange("p (k n) -> p k n", k=KT)
                if free_after is not None:
                    sp.wait_ge(*group_done(l, free_after))
                sp.dma_start(dst, src).then_inc(slot_loaded[parity].sem, 16)

            def kmaj(ap):
                return ap.rearrange("a (k p) n -> p (a k) n", p=P)

            def feed_forward(l, f, first):
                def step(j, parity, wait_down):
                    par = (first + parity) % 2
                    w13 = row(a["ffn_w13"], l)[:, f, :, :].rearrange("a (k p) (u n) -> p (a k) u n", p=P, u=2)
                    dst = ring[:, par, :].rearrange("p (k u n) -> p k u n", k=KT, u=2)
                    sp.wait_ge(*group_done(l, group_of(first) + j - 1))
                    for u in range(2):
                        sp.dma_start(dst[:, :, u, :], w13[:, :, u, ds(j * 256, 256)]).then_inc(
                            slot_loaded[par].sem, 16)
                    if wait_down:
                        sp.wait_ge(*down_done(l, f * FJ + j - 1))
                    w2 = row(a["ffn_w2"], l)[:, f, ds(j * 256, 256), :].rearrange("a (k p) n -> p (a k) n", p=P)
                    sp.dma_start(w2s[:, parity, :, :], w2).then_inc(w2_loaded[parity].sem, 16)
                sp.wait_ge(*xn_ready(l, 3 if f else 1))
                settle(sp)
                step(0, 0, False)
                step(1, 1, False)
                with loop(sp, 0, 4) as i:
                    step(2 * i + 2, 0, True)
                    step(2 * i + 3, 1, True)
                step(10, 0, True)

            with loop(sp, 0, DEPTH) as l:
                sp.wait_ge(*layer_open(l, 1))
                ada = row(a["ada_w"], l)
                load(l, 0, 0, kmaj(ada[:, :, 0:512]))
                load(l, 1, 1, kmaj(ada[:, :, 512:1024]))
                with loop(sp, 1, 9) as i:
                    load(l, 2 * i, 0, kmaj(ada[:, :, ds(i * 1024, 512)]), free_after=2 * i - 1)
                    load(l, 2 * i + 1, 1, kmaj(ada[:, :, ds(i * 1024 + 512, 512)]), free_after=2 * i)
                feed_forward(l, 0, IT_FFA)
                w_in = row(a["w_in"], l)
                par = IT_RW % 2
                with loop(sp, 0, 3) as i:
                    for j in range(2):
                        load(l, IT_RW, (par + j) % 2, kmaj(w_in[:, :, ds(i * 1024 + j * 512, 512)]),
                             free_after=group_of(IT_RW) + 2 * i + j - 1)
                load(l, IT_RW + 6, par, kmaj(w_in[:, :, 3072:3328]), 256, group_of(IT_RW) + 5)
                load(l, IT_RW + 7, 1 - par, kmaj(w_in[:, :, 3328:RW]), 160, group_of(IT_RW) + 6)

                def merge(first, b, src, ks):
                    item = first
                    for h in range(2):
                        c0 = GT0 + b * D + h * 512
                        load(l, item, item % 2, kmaj(w_in[:, :, c0:c0 + 512]), free_after=group_of(item - 2) + 1)
                        item += 1
                        for k in range(ks):
                            load(l, item, item % 2, kmaj(src[:, k * D:(k + 1) * D, h * 512:h * 512 + 512]),
                                 free_after=group_of(item - 2) + 1)
                            item += 1

                merge(IT_MR, 0, row(a["w_branch_rwkv"], l), 1)
                for first, c0, n in ((IT_Z, MB0, 2), (IT_XBC, XBC0, 3)):
                    with loop(sp, 0, n) as i:
                        for j in range(2):
                            load(l, first, (first + j) % 2, kmaj(w_in[:, :, ds(i * 1024 + c0 + j * 512, 512)]),
                                 free_after=group_of(first) + 2 * i + j - 1)
                merge(IT_MM, 1, row(a["w_branch_mamba"], l), 2)
                sp.wait_ge(*group_done(l, group_of(IT_DF)))
                with loop(sp, 0, 3) as i:
                    for j in range(2):
                        load(l, IT_DF, (IT_DF + j) % 2, kmaj(w_in[:, :, ds(i * 1024 + DF0 + j * 512, 512)]),
                             free_after=group_of(IT_DF) + 2 * i + j - 1)
                merge(IT_MD, 2, row(a["w_branch_diff"], l), 1)
                for h in range(2):
                    load(l, IT_OUT + h, (IT_OUT + h) % 2, kmaj(row(a["w_out"], l)[:, :, h * 512:h * 512 + 512]),
                         free_after=group_of(IT_OUT + h - 2) + 1)
                feed_forward(l, 1, IT_FFB)
            sp.wait_ge(*layer_open(DEPTH, 1))
            sp.dma_start(out.rearrange("a (t p) n -> p (a t) n", p=P), x[:, :, :]).then_inc(out_stored.sem, 16)
            sp.wait_ge(*out_stored(0, 1))

        @block.gpsimd
        def _(pool):
            own = Serial(pool, pool_own, settled)

            def keep(m, pattern, base, mult, op=ALU.is_ge, fill=0.0):
                own.step(pool.affine_select(out=m, in_=m, compare_op=op, fill=fill, base=base,
                                            pattern=pattern, channel_multiplier=mult))
            own.step(pool.memset(ident[:, :], 0.0))
            keep(ident[:, :], [[-1, P]], 0, 1, ALU.not_equal, 1.0)
            own.step(pool.memset(ones[:, :], 1.0))
            own.step(pool.memset(onesblk[:, :, :], 1.0))
            keep(onesblk[:, :, :], [[-L, 2], [0, L]], 0, 1)
            keep(onesblk[:, :, :], [[L, 2], [0, L]], L - 1, -1)
            own.step(pool.memset(stack_i[:, :], 0.0))
            keep(stack_i[:, :], [[-1, L]], 0, 1, ALU.not_equal, 1.0)
            keep(stack_i[:, :], [[-1, L]], -L, 1, ALU.not_equal, 1.0)
            own.step(pool.memset(tri[:, :, :], 1.0))
            keep(tri[:, 0, :], [[1, P]], 0, -1)
            keep(tri[:, 1, :], [[-1, P]], 0, 1)
            for d in range(2):
                for incl in range(2):
                    m = rmask[:, d, incl, :]
                    own.step(pool.tensor_copy(m, onesblk[:, :, :].rearrange("p a b -> p (a b)")))
                    keep(m, [[1 if d == 0 else -1, P]], incl - 1, -1 if d == 0 else 1)
            own.step(pool.memset(lvl[:, :, :, :], 0.0))
            for k in range(LV + 1):
                h = 1 << k
                nb = P // (2 * h)
                for d in range(2):
                    m = lvl[:, d, k, :].rearrange("p (b u i) -> p b u i", u=2, i=h)
                    own.step(pool.memset(m[:, :, d, :], 1.0))
                    keep(m[:, :, :, :], [[-2 * h, nb], [0, 2], [0, h]], -h if d == 0 else 0, 1)
                    keep(m[:, :, :, :], [[2 * h, nb], [0, 2], [0, h]], (2 * h if d == 0 else h) - 1, -1)
            own.step(pool.memset(reset[:, :, :], 1.0))
            own.step(pool.memset(reset[:, :, 0:1], 0.0))
            own.step(pool.iota(disti[:, :, :], pattern=[[P, TT], [-1, S]], base=0, channel_multiplier=1))
            own.step(pool.tensor_copy(dist[:, :, :], disti[:, :, :]))
            for h in range(8):
                own.step(pool.memset(slopes[:, h:h + 1], -(2.0 ** -(h + 1)) * 8.0))
            own.step(pool.memset(halfc[:, :], 0.5))
            own.step(pool.memset(halfc[:, 1:2], 1.0))
            own.step(pool.memset(mhalf[:, :], -0.5))
            for l in range(DEPTH):
                li = 0.8 - 0.6 * math.exp(-0.3 * l)
                own.step(pool.memset(laminit[:, l, 0:1], li))
                own.step(pool.memset(laminit[:, l, 1:2], 1.0 - li))
            own.step(pool.memset(vfirst[:, :, :], 0.0))
            own.step(pool.memset(prow[:, :, :], 0.0))
            pool.memset(stat[:, :], 0.0).then_inc(consts_ready.sem, 1)
            pool.wait_ge(*consts_ready(0, 1))
            pool.dma_start(crow[:, :], a["c"].rearrange("a (k p) -> (a k) p", p=P)).then_inc(c_loaded.sem, 16)
            own.restart()

            def rstd(l, k, n):
                pool.wait_ge(*mean_ready(l, k))
                pool.tensor_tensor(stat[:, 4:4 + n], stat[:, 2:2 + n], mhalf[:, 0:n], ALU.pow).then_inc(rstd_ready.sem, 1)

            with loop(pool, 0, DEPTH) as l:
                pool.wait_ge(*layer_open(l, 1))
                rows = [("mamba_conv_w", 0, 0, 120, "a k (c p) -> (a k c) p"),
                        ("ada_b", 1, 0, 72, "a (c p) -> (a c) p"),
                        ("norm_w", 1, 72, 48, "a k (c p) -> (a k c) p"),
                        ("rwkv_k_k", 1, 120, 8, "a (c p) -> (a c) p"),
                        ("rwkv_w0", 2, 0, 16, "a k (c p) -> (a k c) p"),
                        ("rwkv_a0", 2, 16, 16, "a k (c p) -> (a k c) p"),
                        ("rwkv_k_a", 2, 32, 8, "a (c p) -> (a c) p"),
                        ("rwkv_ln_w", 2, 48, 8, "a (c p) -> (a c) p"),
                        ("rwkv_ln_b", 2, 56, 8, "a (c p) -> (a c) p"),
                        ("mamba_norm_w", 2, 64, 16, "a (c p) -> (a c) p"),
                        ("mamba_conv_b", 2, 80, 24, "a (c p) -> (a c) p"),
                        ("diff_subln_w", 2, 104, 1, None)]
                for name, t, r0, n, how in rows:
                    src = row(a[name], l)
                    if how:
                        src = src.rearrange(how, p=P)
                    pool.dma_start(prow[r0:r0 + n, t, :], src).then_inc(params_loaded.sem, 16)
                pool.dma_start(prow[40:48, 2, :],
                               row(a["rwkv_r_k"], l).rearrange("a (c h) p -> (a c) h p", h=2)).then_inc(params_loaded.sem, 16)
                pool.dma_start(prow[120:128, 0, :],
                               a["rwkv_v0"].rearrange("a (c p) -> (a c) p", p=P)).then_inc(params_loaded.sem, 16)
                mu = row(a["rwkv_mu"], l)
                pool.dma_start(prow[0:27, 3, :], mu[:, 0:27 * P].rearrange("a (c p) -> (a c) p", p=P)
                               ).then_inc(params_loaded.sem, 16)
                pool.dma_start(prow[27:28, 3, 0:32], mu[:, 27 * P:RW]).then_inc(bc_loaded.sem, 16)
                adab = row(a["ada_b"], l).rearrange("a (i w n) -> a i w n", i=3, w=3)
                pool.dma_start(gbc[:, :, :], adab[:, :, 2, :].to_broadcast([P, 3, D])).then_inc(bc_loaded.sem, 16)
                nw = row(a["norm_w"], l).rearrange("a (i w) n -> a i w n", w=2)
                pool.dma_start(nbc[:, :, :], nw[:, :, 1, :].to_broadcast([P, 3, D])).then_inc(bc_loaded.sem, 16)

                rstd(l, 1, 2)
                rstd(l, 2, 2)
                rstd(l, 3, 2)
                pool.wait_ge(*xn_ready(l, 2))
                pool.wait_ge(*hT_ready(l, 2))
                settle(pool)
                pool.dma_start(v1s[:, :, :], a["rwkv_v1"].rearrange("a (k p) n -> p (a k) n", p=P)).then_inc(rwkv_w_loaded.sem, 16)
                pool.dma_start(v2s[:, :], a["rwkv_v2"].rearrange("a p n -> (a p) n")).then_inc(rwkv_w_loaded.sem, 16)
                for t in (vX, arX, btX, ktX, yX):
                    own.step(pool.memset(t, 0.0))
                own.restart()
                with loop(pool, 0, PAIRS) as p:
                    pool.wait_ge(*hT_ready(l, 2))
                    with when(pool, p > 0):
                        pool.wait_ge(*lora_done(l, p))
                    c = ds(p * P, P)
                    pool.dma_start(lora[:, 0, :], row(a["rwkv_w2"], l)[:, :, :, c].rearrange("a d r n -> (a d r) n")).then_inc(pair_w_loaded.sem, 16)
                    pool.dma_start(lora[:, 1, :], row(a["rwkv_a2"], l)[:, :, :, c].rearrange("a d r n -> (a d r) n")).then_inc(pair_w_loaded.sem, 16)
                    pool.dma_start(lora[:, 2, :], row(a["rwkv_g2"], l)[:, 0:P, c].rearrange("a r n -> (a r) n")).then_inc(pair_w_loaded.sem, 16)
                    pool.dma_start(g2b[:, :], row(a["rwkv_g2"], l)[:, P:160, c].rearrange("a r n -> (a r) n")).then_inc(pair_w_loaded.sem, 16)
                    pool.wait_ge(*gn_var(l, p + 1))
                    pool.tensor_tensor(gstat[:, 3, :], gstat[:, 2, :], mhalf[:, 0:CH], ALU.pow).then_inc(gn_rstd.sem, 1)
                pool.wait_ge(*group_evacuated(l, group_of(IT_Z)))
                pool.dma_start(wdt[:, :, :], row(a["w_in"], l)[:, :, DT0:DT0 + 64].rearrange("a (k p) n -> p (a k) n", p=P)).then_inc(mamba_w_loaded.sem, 16)
                pool.dma_start(dtb[:, :], row(a["mamba_dt_bias"], l).rearrange("a d h -> a (d h)").to_broadcast([P, 64])).then_inc(mamba_w_loaded.sem, 16)
                pool.dma_start(alog[:, :], row(a["mamba_a_log"], l).rearrange("a d h -> a (d h)").to_broadcast([P, 64])).then_inc(mamba_w_loaded.sem, 16)
                pool.dma_start(dskip[:, :], row(a["mamba_d"], l).to_broadcast([P, 32])).then_inc(mamba_w_loaded.sem, 16)
                pool.wait_ge(*acs_evac(l, 1))
                settle(pool)
                pool.dma_start(acs_dram, acsT[:, :]).then_inc(acs_stored.sem, 16)
                pool.wait_ge(*acs_stored(l, 1))
                with loop(pool, 0, 4) as g:
                    with when(pool, g > 0):
                        pool.wait_ge(*yoff_evac(l, 2 * g))
                    own.step(pool.tensor_copy(bg[:, :], bcT[:, ds(g, 1), :]))
                    own.step(pool.tensor_copy(cgm[:, :], bcT[:, ds(g + 4, 1), :]))
                    pool.tensor_copy(btg[:, :, :], btk[:, :, ds(g * P, P)]).then_inc(group_staged.sem, 1)
                    for n in range(4):
                        c, d = n // 2, n % 2
                        i = n % 2
                        if n >= 2:
                            pool.wait_ge(*seg_ready(l, 4 * g + n - 1))
                        src = acs_dram[ds(g * 8 + d * 32, 8), c * P:(c + 1) * P].rearrange("(a h) n -> a h n", a=1)
                        pool.dma_start(bca[:, i, :, :], src.to_broadcast([P, 8, P])).then_inc(acs_bc[i].sem, 16)
                    pool.wait_ge(*msq_ready(l, g + 1))
                    pool.tensor_tensor(mstat[:, 4:6], mstat[:, 2:4], mhalf[:, 0:2], ALU.pow).then_inc(mrstd_ready.sem, 1)
                    own.restart()
                pool.wait_ge(*group_evacuated(l, group_of(IT_DF)))
                pool.dma_start(dlam[:, :, :], row(a["diff_lambda"], l).to_broadcast([P, 4, 64])).then_inc(diff_w_loaded.sem, 16)
                own.step(pool.memset(qX[:, :, :], 0.0))
                pool.wait_ge(*diff_w_loaded(l, 1))
                own.restart()
                with loop(pool, 0, 8) as h:
                    pool.wait_ge(*group_evacuated(l, group_of(IT_DF) + 4))
                    with when(pool, h > 0):
                        pool.wait_ge(*sc_done(l, h))
                    own.step(pool.tensor_copy(qX[0:64, 0, :], qkT[0:64, ds(h, 1), :]))
                    pool.tensor_copy(qX[64:P, 1, :], qkT[64:P, ds(h, 1), :]).then_inc(qx_ready.sem, 1)
                    pool.wait_ge(*o_mean(l, h + 1))
                    pool.tensor_tensor(dstat[:, 20:22], dstat[:, 18:20], mhalf[:, 0:2], ALU.pow).then_inc(o_rstd.sem, 1)
                    own.restart()
                rstd(l, 4, 2)
                rstd(l, 5, 2)
                rstd(l, 6, 2)

        @block.tensor
        def _(pe):
            def mm(o, lhsT, rhs, start=True, stop=True):
                return pe.matmul(o, lhsT, rhs, start=start, stop=stop)

            def slot(parity, cols=512):
                return ring[:, parity, 0:KT * cols].rearrange("p (k n) -> p k n", k=KT)

            def bank_free(l, group):
                pe.wait_ge(*group_evacuated(l, group - 1))

            def to_channels(pair, w, src, n_mt=4, last=P, k0=0):
                for m in range(n_mt):
                    cols = last if m == n_mt - 1 else P
                    o = ps[0:cols, 2 * pair + m // 2, (m % 2) * S:(m % 2 + 1) * S]
                    for k in range(KT):
                        ins = mm(o, w[:, k, m * P:m * P + cols], src[:, k, :], k == 0, k == KT - 1)
                return ins

            def to_tokens(pair, w, src, k0=0, nk=KT, first=True, final=True):
                for t in range(TT):
                    for k in range(nk):
                        ins = mm(ps[:, 2 * pair + t, :], src[:, k0 + k, t * P:(t + 1) * P], w[:, k, :],
                                 first and k == 0, final and k == nk - 1)
                return ins

            def turn_norm(l, k):
                pe.wait_ge(*xn_ready(l, k))
                for kt in range(KT):
                    for t in range(TT):
                        o = ps[:, 4 + kt // 2, (kt % 2) * S + t * P:(kt % 2) * S + (t + 1) * P]
                        ins = pe.transpose(o, xn[:, t, kt * P:(kt + 1) * P], ident[:, :])
                ins.then_inc(xn_turned.sem, 1)

            def feed_forward(l, f, first):
                g0 = group_of(first)

                def up(j, half_item, parity):
                    item_par = (first + parity) % 2
                    pe.wait_ge(*ffn_arrival(l, f, first, half_item, parity))
                    bank_free(l, g0 + j)
                    w = ring[:, item_par, :].rearrange("p (k u n) -> p k u n", k=KT, u=2)
                    pair = (g0 + parity) % 2
                    for u in range(2):
                        for m in range(2):
                            for k in range(KT):
                                ins = mm(ps[:, 2 * pair + u, m * S:(m + 1) * S], w[:, k, u, m * P:(m + 1) * P],
                                         hT[:, k, :], k == 0, k == KT - 1)
                    ins.then_inc(group_done.sem, 1)

                def down(j, half_item, parity, start=False, stop=False):
                    pe.wait_ge(*w2_loaded[parity](l, f * (6 if parity == 0 else 5) + half_item + 1))
                    pe.wait_ge(*group_evacuated(l, g0 + j + 1))
                    for t in range(TT):
                        for h in range(2):
                            for k in range(2):
                                ins = mm(ps[:, 4 + 2 * t + h, :], actT[:, parity, k, t * P:(t + 1) * P],
                                         w2s[:, parity, k, h * 512:(h + 1) * 512],
                                         start and k == 0, stop and k == 1)
                    ins.then_inc(down_done.sem, 1)

                pe.wait_ge(*hT_ready(l, 4 if f else 1))
                up(0, 0, 0)
                up(1, 0, 1)
                down(0, 0, 0, start=True)
                with loop(pe, 0, 4) as i:
                    up(2 * i + 2, i + 1, 0)
                    down(2 * i + 1, i, 1)
                    up(2 * i + 3, i + 1, 1)
                    down(2 * i + 2, i + 1, 0)
                up(10, 5, 0)
                down(9, 4, 1)
                down(10, 5, 0, stop=True)

            def ffn_arrival(l, f, first, half_item, parity):
                par = (first + parity) % 2
                return slot_loaded[par](l, loads_before(first + parity, par) + 2 * (half_item + 1))

            pe.wait_ge(*consts_ready(0, 1))
            pe.wait_ge(*c_loaded(0, 1))
            pe.transpose(ps[:, 4, 0:8], crow[:, :], ident[0:8, 0:8]).then_inc(c_turned.sem, 1)
            pe.wait_ge(*c_ready(0, 1))

            with loop(pe, 0, DEPTH) as l:
                pe.wait_ge(*layer_open(l, 1))
                pe.wait_ge(*params_loaded(l, 15))
                pe.wait_ge(*bc_loaded(l, 3))
                for t in range(4):
                    ins = pe.transpose(ps[:, 4, t * P:(t + 1) * P], prow[:, t, :], ident[:, :])
                ins.then_inc(params_turned.sem, 1)

                def ada(i, b):
                    par = b % 2
                    g = i * 6 + b
                    pe.wait_ge(*slot_loaded[par](l, i * 3 + b // 2 + 1))
                    if b >= 2:
                        bank_free(l, g)
                    w = slot(par)
                    if b < 4:
                        for m in range(4):
                            for k in range(KT):
                                ins = mm(ps[:, 2 * par, m:m + 1], w[:, k, m * P:(m + 1) * P], ccol[:, k:k + 1],
                                         k == 0, k == KT - 1)
                    else:
                        for k in range(KT):
                            ins = mm(ps[:, 2 * par, :], ccol[:, k:k + 1].to_broadcast([P, P]), w[:, k, :],
                                     k == 0, k == KT - 1)
                    ins.then_inc(group_done.sem, 1)
                with loop(pe, 0, 3) as i:
                    for b in range(6):
                        ada(i, b)
                    pe.wait_ge(*group_evacuated(l, 6 * i + 6))

                turn_norm(l, 1)
                feed_forward(l, 0, IT_FFA)
                turn_norm(l, 2)
                pe.wait_ge(*hT_ready(l, 2))

                def project(item, i, run, parity, kind, **kw):
                    g = group_of(item)
                    par = (item + parity) % 2
                    pe.wait_ge(*slot_loaded[par](l, loads_before(item + parity, par) + run + 1))
                    bank_free(l, g + i)
                    pair = (g + parity) % 2
                    ins = kind(pair, slot(par, kw.pop("cols", 512)), hT, **kw)
                    ins.then_inc(group_done.sem, 1)

                with loop(pe, 0, 3) as i:
                    for j in range(2):
                        project(IT_RW, 2 * i + j, i, j, to_channels)
                project(IT_RW + 6, 0, 0, 0, to_channels, n_mt=2, cols=256)
                project(IT_RW + 7, 0, 0, 0, to_channels, n_mt=2, last=32, cols=160)

                pe.wait_ge(*group_evacuated(l, group_of(IT_RW) + 8))
                pe.wait_ge(*rwkv_w_loaded(l, 2))
                for k in range(KT):
                    ins = mm(ps[0:32, 4, 0:S], v1s[:, k, :], rkv[:, 16 + k, :], k == 0, k == KT - 1)
                ins.then_inc(vlow_done.sem, 1)
                pe.wait_ge(*vlow_evac(l, 1))
                for n in range(4):
                    if n >= 2:
                        pe.wait_ge(*v_final(l, n - 1))
                    for m in range(2):
                        kt = 2 * n + m
                        ins = mm(ps[:, 4 + n % 2, m * S:(m + 1) * S], v2s[:, kt * P:(kt + 1) * P], vrs[:, :])
                    ins.then_inc(vmix_done.sem, 1)
                pe.wait_ge(*v_final(l, 4))
                pe.wait_ge(*kk_sq(l, 1))
                for n in range(4):
                    ins = mm(ps[:, 4 + n, :], onesblk[:, :, :].rearrange("p a b -> p (a b)"),
                             kk_sq_buf[:, 2 * n:2 * n + 2, :])
                ins.then_inc(kk_sum.sem, 1)
                pe.wait_ge(*kk_root(l, 1))

                with loop(pe, 0, PAIRS) as p:
                    pe.wait_ge(*pair_w_loaded(l, 4 * p + 4))
                    with when(pe, p > 0):
                        pe.wait_ge(*yr_ready(l, p))
                    for d in range(2):
                        rr = slice(d * 64, d * 64 + 64)
                        mm(ps[:, 4 + d, 0:S], lora[rr, 0, :], cw[rr, :])
                        mm(ps[:, 4 + d, S:2 * S], lora[rr, 1, :], ca[rr, :])
                    mm(ps[:, 6, 0:S], lora[:, 2, :], cg[:, :], True, False)
                    mm(ps[:, 6, 0:S], g2b[:, :], cg2[:, :], False, True).then_inc(lora_done.sem, 1)
                    pe.wait_ge(*decay_ready(l, p + 1))
                    mm(ps[:, 6, S:2 * S], onesblk[:, :, :].rearrange("p a b -> p (a b)"), bprod[:, :])
                    for c in range(CH):
                        ins = mm(ps[:, 7, c * L:(c + 1) * L], vX[:, c, :, :].rearrange("p a b -> p (a b)"), stack_i[:, :])
                    ins.then_inc(bonus_done.sem, 1)
                    pe.wait_ge(*bonus_evac(l, p + 1))
                    def flat(t):
                        return t.rearrange("p a b -> p (a b)")

                    def by_all(o, t, d, c):
                        return mm(o, flat(t[:, d, c, :, :]), arX[:, d, c, :, :, :].rearrange("p u a b -> p (u a b)"))

                    for d in range(2):
                        u = 2 * p + d
                        pe.wait_ge(*ops_ready(l, u + 1))
                        if d:
                            pe.wait_ge(*m2_evac(l, u))
                        for c in range(CH):
                            pe.transpose(ps[:, 2, c * P:(c + 1) * P], flat(btX[:, d, c, :, :]), ident[:, :])
                        for c in range(CH):
                            ins = pe.transpose(ps[:, 3, c * P:(c + 1) * P], flat(ktX[:, d, c, :, :]), ident[:, :])
                        ins.then_inc(turned_done.sem, 1)
                        for c in range(CH):
                            mm(ps[:, 4, c * P:(c + 1) * P], flat(arX[:, d, c, 0, :, :]), flat(btX[:, d, c, :, :]))
                        for c in range(CH):
                            ins = by_all(ps[:, 5 + c // 2, (c % 2) * S:(c % 2 + 1) * S], btX, d, c)
                        ins.then_inc(m1_done.sem, 1)
                        pe.wait_ge(*turned_evac(l, u + 1))
                        for c in range(CH):
                            ins = by_all(ps[:, (7, 2)[c // 2], (c % 2) * S:(c % 2 + 1) * S], ktX, d, c)
                        ins.then_inc(m2_done.sem, 1)
                    pe.wait_ge(*m2_evac(l, 2 * p + 2))
                    for k in range(LV):
                        w = p * 2 * LV + 2 * k
                        for d in range(2):
                            if k:
                                pe.wait_ge(*dd_ready(l, w - 1 + d))
                            for c in range(CH):
                                ins = mm(ps[:, 2 + d, c * P:(c + 1) * P], mb[:, d, c, 0, :], dd[:, d, c, 0, :])
                            ins.then_inc(f_done.sem, 1)
                        for d in range(2):
                            pe.wait_ge(*e_ready(l, w + d + 1))
                            for c in range(CH):
                                if k < LV - 1:
                                    mm(ps[:, 4 + 2 * d, c * P:(c + 1) * P], dd[:, d, c, 1, :], ee[:, d, c, :])
                                ins = mm(ps[:, 5 + 2 * d, c * P:(c + 1) * P], ee[:, d, c, :], dd[:, d, c, 1, :])
                            ins.then_inc(de_done.sem, 1)
                    pe.wait_ge(*dd_ready(l, (p + 1) * 2 * LV))
                    def chunk(d, j):
                        return j if d == 0 else CH - 1 - j

                    for j in range(CH):
                        if j:
                            pe.wait_ge(*s_evac(l, 3 * p + j))
                        for d in range(2):
                            c = chunk(d, j)
                            ins = mm(ps[:, 4, d * L:(d + 1) * L], mk[:, d, c, 0, :], vtm[:, c, :], True, j == 0)
                            if j:
                                ins = mm(ps[:, 4, d * L:(d + 1) * L], flat(arX[:, d, c, 0, :, :]), st8[:, j, d, :], False, True)
                        ins.then_inc(r_done.sem, 1)
                        pe.wait_ge(*r_evac(l, 4 * p + j + 1))
                        for d in range(2):
                            ins = mm(ps[:, 5, d * L:(d + 1) * L], dd[:, d, chunk(d, j), 1, :], rs[:, d, :])
                        ins.then_inc(u_done.sem, 1)
                        pe.wait_ge(*u_evac(l, 4 * p + j + 1))
                        if j < CH - 1:
                            for d in range(2):
                                c = chunk(d, j)
                                mm(ps[:, 6, d * L:(d + 1) * L], btm[:, d, c, :], us[:, j, d, :], True, False)
                                ins = mm(ps[:, 6, d * L:(d + 1) * L], ktm[:, d, c, :], vtm[:, c, :], False, True)
                            ins.then_inc(s_done.sem, 1)
                    for c in range(CH):
                        o = ps[:, 7, c * L:(c + 1) * L]
                        for d in range(2):
                            j = chunk(d, c)
                            mm(o, mb[:, d, c, 1, :], us[:, j, d, :], d == 0, False)
                            if j:
                                mm(o, flat(arX[:, d, c, 1, :, :]), st8[:, j, d, :], False, False)
                            ins = mm(o, mk[:, d, c, 1, :], vtm[:, c, :], False, d == 1)
                    ins.then_inc(y_done.sem, 1)
                    pe.wait_ge(*yx_ready(l, p + 1))
                    for c in range(CH):
                        ins = mm(ps[:, 4, c * L:(c + 1) * L], yX[:, c, :, :].rearrange("p a b -> p (a b)"), stack_i[:, :])
                    ins.then_inc(yt_done.sem, 1)
                pe.wait_ge(*yr_ready(l, PAIRS))

                def merge(first, yT, ks):
                    item = first
                    for h in range(2):
                        for kind in range(2):
                            g = group_of(item)
                            n = ks if kind else 1
                            for kk in range(n):
                                par = item % 2
                                pe.wait_ge(*slot_loaded[par](l, loads_before(item, par) + 1))
                                if kk == 0:
                                    bank_free(l, g)
                                if n == 1:
                                    ins = to_tokens(g % 2, slot(par), yT if kind else hT)
                                else:
                                    ins = to_tokens(g % 2, slot(par), yT, 8 * kk, KT, kk == 0, kk == n - 1)
                                item += 1
                            ins.then_inc(group_done.sem, 1)

                merge(IT_MR, rkv, 1)

                with loop(pe, 0, 2) as i:
                    for j in range(2):
                        project(IT_Z, 2 * i + j, i, j, to_tokens)

                def turn_conv(k, parity, later=None):
                    pe.wait_ge(*group_evacuated(l, group_of(IT_XBC) + k + 1))
                    if later is None:
                        pe.wait_ge(*conv_evac(l, k))
                    else:
                        with when(pe, later > 0):
                            pe.wait_ge(*conv_evac(l, k))
                    for t in range(TT):
                        for m in range(4):
                            ins = pe.transpose(ps[:, 4 + t, m * P:(m + 1) * P], cv[:, parity, m, t * P:(t + 1) * P], ident[:, :])
                    ins.then_inc(conv_turned.sem, 1)
                with loop(pe, 0, 2) as i:
                    for j in range(2):
                        project(IT_XBC, 2 * i + j, i, j, to_channels)
                        turn_conv(2 * i + j, j, None if j else i)
                project(IT_XBC, 4, 2, 0, to_channels)
                turn_conv(4, 0)
                project(IT_XBC, 5, 2, 1, to_channels)
                pe.wait_ge(*mamba_w_loaded(l, 4))
                for t in range(TT):
                    for k in range(KT):
                        ins = mm(ps[:, 6, t * 64:(t + 1) * 64], hT[:, k, t * P:(t + 1) * P], wdt[:, k, :], k == 0, k == KT - 1)
                ins.then_inc(dt_done.sem, 1)
                pe.wait_ge(*da_ready(l, 1))
                for c in range(TT):
                    for d in range(2):
                        mm(ps[d * 32:d * 32 + 32, 7, c * P:(c + 1) * P], dts[:, 6, c, d * 32:d * 32 + 32], tri[:, d, :])
                for c in range(TT):
                    ins = mm(ps[:, 6, c * 64:(c + 1) * 64], ones[:, :], dts[:, 6, c, :])
                ins.then_inc(acs_done.sem, 1)
                pe.wait_ge(*acs_evac(l, 1))
                settle(pe)
                for c in range(TT):
                    ins = pe.transpose(ps[:, 7, 256 + c * 64:256 + (c + 1) * 64], acsT[:, c * P:(c + 1) * P], ident[0:64, 0:64])
                ins.then_inc(acs_turned.sem, 1)
                pe.wait_ge(*acs_exp(l, 1))
                pe.wait_ge(*group_evacuated(l, group_of(IT_MM)))

                with loop(pe, 0, 4) as g:
                    pe.wait_ge(*group_staged(l, g + 1))
                    with when(pe, g > 0):
                        pe.wait_ge(*ymT_ready(l, g))
                    for c in range(TT):
                        ins = mm(ps[:, 4, c * P:(c + 1) * P], bg[:, c * P:(c + 1) * P], cgm[:, c * P:(c + 1) * P])
                    ins.then_inc(cb_done.sem, 1)
                    for c in range(TT):
                        pe.wait_ge(*wx_ready(l, 2 * g + c + 1))
                        for h in range(8):
                            for d in range(2):
                                ins = mm(ps[:, 5 + c, h * 64:(h + 1) * 64], wx[:, 2 * c + d, h, :], xdt[:, 2 * c + d, h, :],
                                         d == 0, d == 1)
                        ins.then_inc(ydiag_done.sem, 1)
                    for d in range(2):
                        pe.wait_ge(*xs_ready(l, 2 * g + d + 1))
                        mm(ps[:, 7, :], btg[:, d, :], xs[:, :, :].rearrange("p a b -> p (a b)")).then_inc(state_done.sem, 1)
                        pe.wait_ge(*state_evac(l, 2 * g + d + 1))
                        if d:
                            pe.wait_ge(*yoff_evac(l, 2 * g + 1))
                        mm(ps[:, 4, :], cgm[:, (1 - d) * P:(2 - d) * P], h0[:, :]).then_inc(yoff_done.sem, 1)
                    pe.wait_ge(*ym_ready(l, g + 1))
                    for m in range(4):
                        for c in range(TT):
                            o = ps[:, 5 + m // 2, (m % 2) * S + c * P:(m % 2) * S + (c + 1) * P]
                            ins = pe.transpose(o, ym[:, c, m * P:(m + 1) * P], ident[:, :])
                    ins.then_inc(ym_turned.sem, 1)
                pe.wait_ge(*ymT_ready(l, 4))
                merge(IT_MM, zy.rearrange("p g t c -> p (g t c)").rearrange("p (k s) -> p k s", s=S), 2)

                with loop(pe, 0, 2) as i:
                    for j in range(2):
                        project(IT_DF, 2 * i + j, i, j, to_channels)
                for j in range(2):
                    project(IT_DF, 4 + j, 2, j, to_tokens)
                pe.wait_ge(*group_evacuated(l, group_of(IT_DF) + 6))
                with loop(pe, 0, 8) as h:
                    pe.wait_ge(*qx_ready(l, h + 1))
                    with when(pe, h > 0):
                        pe.wait_ge(*yd_ready(l, h))
                    for t in range(TT):
                        for m in range(2):
                            ins = mm(ps[:, 4 + t, m * S:(m + 1) * S], qX[:, m, t * P:(t + 1) * P], qkT[:, ds(h + 8, 1), :])
                    ins.then_inc(sc_done.sem, 1)
                    pe.wait_ge(*am_ready(l, h + 1))
                    for kt in range(TT):
                        for t in range(TT):
                            ins = pe.transpose(ps[:, 6, kt * S + t * P:kt * S + (t + 1) * P], am[:, t, kt * P:(kt + 1) * P], ident[:, :])
                    ins.then_inc(am_turned.sem, 1)
                    pe.wait_ge(*amT_ready(l, h + 1))
                    for t in range(TT):
                        for kt in range(TT):
                            ins = mm(ps[:, 7, t * P:(t + 1) * P], amT[:, kt, t * P:(t + 1) * P], vdm[:, kt, ds(h * P, P)],
                                     kt == 0, kt == 1)
                    ins.then_inc(o_done.sem, 1)
                    pe.wait_ge(*on_ready(l, h + 1))
                    for t in range(TT):
                        ins = pe.transpose(ps[:, 6, t * P:(t + 1) * P], on[:, t, :], ident[:, :])
                    ins.then_inc(on_turned.sem, 1)
                pe.wait_ge(*yd_ready(l, 8))
                merge(IT_MD, ydT, 1)

                pe.wait_ge(*group_evacuated(l, group_of(IT_OUT)))
                for kt in range(KT):
                    for t in range(TT):
                        o = ps[:, 4 + kt // 2, (kt % 2) * S + t * P:(kt % 2) * S + (t + 1) * P]
                        ins = pe.transpose(o, merged[:, t, kt * P:(kt + 1) * P], ident[:, :])
                ins.then_inc(merged_turned.sem, 1)
                pe.wait_ge(*hT_ready(l, 3))
                for h in range(2):
                    item = IT_OUT + h
                    par = item % 2
                    pe.wait_ge(*slot_loaded[par](l, loads_before(item, par) + 1))
                    bank_free(l, group_of(item))
                    to_tokens(group_of(item) % 2, slot(par), hT).then_inc(group_done.sem, 1)
                turn_norm(l, 3)
                feed_forward(l, 1, IT_FFB)

        @block.scalar
        def _(act):
            own = Serial(act, act_own, settled)

            def sumsq(l, k, src, into):
                for t in range(TT):
                    own.step(act.activation(yt[:, :], src[t], ACT.Square, accum_out=stat[:, t:t + 1]))
                act.sem_inc(sumsq_done.sem, 1)

            def ffn(l, f, first):
                g0 = group_of(first)

                def gate_of(j, parity):
                    act.wait_ge(*group_done(l, g0 + j + 1))
                    pair = (g0 + parity) % 2
                    act.activation(sgm[:, parity, :], ps[:, 2 * pair, :], ACT.Sigmoid).then_inc(ffn_sig.sem, 1)
                for j in range(2):
                    gate_of(j, j)
                with loop(act, 0, 4) as i:
                    for j in range(2):
                        act.wait_ge(*group_evacuated(l, g0 + 2 * i + 1 + j))
                        gate_of(2 * i + 2 + j, j)
                act.wait_ge(*group_evacuated(l, g0 + 9))
                gate_of(10, 0)
                act.wait_ge(*down_done(l, (f + 1) * FJ))

            act.wait_ge(*c_turned(0, 1))
            act.activation(stat[:, 8:16], ps[:, 4, 0:8], ACT.Sigmoid).then_inc(c_sig.sem, 1)
            act.wait_ge(*x_loaded(0, 1))
            own.restart()
            with loop(act, 0, DEPTH) as l:
                act.wait_ge(*layer_open(l, 1))
                xs_ = [x[:, t, :] for t in range(TT)]
                sumsq(l, 1, xs_, 0)
                ffn(l, 0, IT_FFA)
                sumsq(l, 2, [ps[:, 4 + 2 * t:6 + 2 * t, :] for t in range(TT)], 0)
                act.wait_ge(*x_updated(l, 1))
                sumsq(l, 3, xs_, 0)

                act.wait_ge(*hT_ready(l, 2))

                def scaled(g, pair, mt0, n, last=P):
                    act.wait_ge(*group_done(l, g + 1))
                    for m in range(n):
                        cols = last if m == n - 1 else P
                        dst, mcol = mt0(m)
                        own.step(act.activation(dst, ps[0:cols, 2 * pair + m // 2, (m % 2) * S:(m % 2 + 1) * S],
                                                ACT.Identity, scale=der[0:cols, ds(mcol, 1)]))
                    act.sem_inc(shift_scaled.sem, 1)
                own.restart()
                with loop(act, 0, 3) as i:
                    for j in range(2):
                        g = group_of(IT_RW)
                        scaled(g + 2 * i + j, (g + j) % 2,
                               lambda m: (rkv[:, ds(i * 8 + j * 4 + m, 1), :], i * 8 + j * 4 + m + E_OMU), 4)
                    own.restart()
                g = group_of(IT_RW)
                scaled(g + 6, g % 2, lambda m: ((cw, ca)[m], 24 + m + E_OMU), 2)
                scaled(g + 7, (g + 1) % 2, lambda m: ((cg, cg2)[m], 26 + m + E_OMU), 2, 32)
                act.wait_ge(*group_evacuated(l, g + 8))
                own.step(act.activation(cw, cw, ACT.Tanh))
                own.step(act.activation(cg, cg, ACT.Sigmoid))
                act.activation(cg2, cg2, ACT.Sigmoid).then_inc(lora_act.sem, 1)
                act.wait_ge(*vlow_done(l, 1))
                act.activation(vrs, ps[0:32, 4, 0:S], ACT.Identity).then_inc(vlow_evac.sem, 1)
                for n in range(4):
                    act.wait_ge(*vmix_done(l, n + 1))
                    if n:
                        act.wait_ge(*v_final(l, n))
                    for m in range(2):
                        own.step(act.activation(vtmp[:, m * S:(m + 1) * S], ps[:, 4 + n % 2, m * S:(m + 1) * S], ACT.Sigmoid,
                                                bias=prm[:, C_V0 + 2 * n + m:C_V0 + 2 * n + m + 1]))
                    act.sem_inc(vmix_sig.sem, 1)
                act.wait_ge(*kk_eps(l, 1))
                act.activation(kk_sq_buf, kk_sq_buf, ACT.Sqrt).then_inc(kk_root.sem, 1)
                own.restart()
                with loop(act, 0, PAIRS) as p:
                    act.wait_ge(*lora_done(l, p + 1))
                    for d in range(2):
                        own.step(act.activation(lwb[:, d, :, :], ps[:, 4 + d, 0:S], ACT.Tanh, scale=0.5,
                                                bias=der[:, ds(p + E_W0H + 8 * d, 1)]))
                        own.step(act.activation(icl[:, d, :, :], ps[:, 4 + d, S:2 * S], ACT.Tanh, scale=0.5,
                                                bias=der[:, ds(p + E_A0H + 8 * d, 1)]))
                    act.activation(gate, ps[:, 6, 0:S], ACT.Identity).then_inc(lora_evac.sem, 1)
                    act.wait_ge(*decay_ready(l, p + 1))
                    own.step(act.activation(etot[:, 0, :], gi[:, 0, :, L - 1], ACT.Exp))
                    own.step(act.activation(etot[:, 1, :], gi[:, 1, :, 0], ACT.Exp))
                    own.step(act.activation(ege, ge, ACT.Exp))
                    own.step(act.activation(eni, gi, ACT.Exp, scale=-1.0))
                    act.activation(egi, gi, ACT.Exp).then_inc(exps_ready.sem, 1)
                    for d in range(2):
                        u = 2 * p + d
                        act.wait_ge(*turned_done(l, u + 1))
                        own.step(act.activation(btm[:, d], ps[:, 2, :], ACT.Identity))
                        act.activation(ktm[:, d], ps[:, 3, :], ACT.Identity).then_inc(turned_evac.sem, 1)
                    own.restart()

                def gates(first):
                    for item in (first, first + (3 if first == IT_MM else 2)):
                        g = group_of(item)
                        act.wait_ge(*group_done(l, g + 1))
                        act.wait_ge(*group_evacuated(l, g))
                        act.activation(sg, halves(g % 2), ACT.Sigmoid).then_inc(gate_sig.sem, 1)

                act.wait_ge(*yr_ready(l, PAIRS))
                gates(IT_MR)

                g = group_of(IT_Z)
                act.wait_ge(*group_evacuated(l, g))
                with loop(act, 0, 2) as i:
                    for j in range(2):
                        act.wait_ge(*group_done(l, g + 2 * i + j + 1))
                        act.activation(zy[:, ds(2 * i + j, 1), :, :], halves((g + j) % 2), ACT.Sigmoid).then_inc(z_sig.sem, 1)
                g = group_of(IT_XBC)

                def conv(k, parity, turned_free, to_tok):
                    act.wait_ge(*group_done(l, g + k + 1))
                    if turned_free is not None:
                        act.wait_ge(*conv_turned(l, turned_free))
                    for m in range(4):
                        own.step(act.activation(cv[:, parity, m, :], ps[:, 2 * ((g + parity) % 2) + m // 2, (m % 2) * S:(m % 2 + 1) * S],
                                                ACT.Identity, scale=prm[:, ds(k * 4 + m + C_CONVW + 48, 1)],
                                                bias=prm[:, ds(k * 4 + m + C_CONVB, 1)]))
                    act.sem_inc(conv_scaled.sem, 1)
                    act.wait_ge(*conv_raw(l, k + 1))
                    act.activation(cvs, cv[:, parity, :, :], ACT.Sigmoid).then_inc(conv_sig.sem, 1)
                    if to_tok:
                        act.wait_ge(*conv_turned(l, k + 1))
                        for t in range(TT):
                            dst = xtm[:, t, ds(k * 512, 512)] if to_tok == 1 else btk[:, t, :]
                            own.step(act.activation(dst, ps[:, 4 + t, :], ACT.Identity))
                        act.sem_inc(conv_evac.sem, 1)
                own.restart()
                with loop(act, 0, 2) as i:
                    for j in range(2):
                        conv(2 * i + j, j, None, 1)
                    own.restart()
                conv(4, 0, None, 2)
                conv(5, 1, None, 0)
                act.wait_ge(*dt_raw(l, 1))
                own.step(act.activation(alog, alog, ACT.Exp))
                act.activation(dts[:, 1, :, :], dts[:, 1, :, :], ACT.Exp).then_inc(dt_exp.sem, 1)
                act.wait_ge(*acs_diff(l, 1))
                own.step(act.activation(dts[:, 4, :, :], dts[:, 4, :, :], ACT.Exp))
                act.activation(dts[:, 5, :, :], dts[:, 3, :, :], ACT.Exp).then_inc(acs_exp.sem, 1)
                with loop(act, 0, 4) as gg:
                    for n in range(4):
                        act.wait_ge(*seg_ready(l, 4 * gg + n + 1))
                        act.activation(wx[:, n, :, :], wx[:, n, :, :], ACT.Exp).then_inc(seg_exp.sem, 1)
                    for d in range(2):
                        act.wait_ge(*state_done(l, 2 * gg + d + 1))
                        with when(act, gg * 2 + d > 0):
                            act.wait_ge(*yoff_done(l, 2 * gg + d))
                        act.activation(h0, ps[:, 7, :], ACT.Identity).then_inc(state_evac.sem, 1)
                act.wait_ge(*ymT_ready(l, 4))
                gates(IT_MM)

                own.restart()
                act.wait_ge(*lam_raw(l, 1))
                act.activation(dstat[:, 26:28], dstat[:, 24:26], ACT.Exp).then_inc(lam_exp.sem, 1)
                with loop(act, 0, 8) as h:
                    act.wait_ge(*smax_ready(l, h + 1))
                    for t in range(TT):
                        for m in range(2):
                            own.step(act.activation(pr[:, t, m, :], sc[:, t, m, :], ACT.Exp, scale=0.125,
                                                    bias=dstat[:, 4 + 2 * t + m:5 + 2 * t + m],
                                                    accum_out=dstat[:, 8 + 2 * t + m:9 + 2 * t + m]))
                    act.sem_inc(p_ready.sem, 1)
                    act.wait_ge(*o_done(l, h + 1))
                    for t in range(TT):
                        own.step(act.activation(on[:, t, :], ps[:, 7, t * P:(t + 1) * P], ACT.Square,
                                                accum_out=dstat[:, 16 + t:17 + t]))
                    act.sem_inc(o_sq.sem, 1)
                    own.restart()
                gates(IT_MD)
                act.wait_ge(*group_evacuated(l, group_of(IT_OUT) + 2))
                sumsq(l, 4, [merged[:, t, :] for t in range(TT)], 0)
                act.wait_ge(*x_updated(l, 2))
                sumsq(l, 5, xs_, 0)
                ffn(l, 1, IT_FFB)
                sumsq(l, 6, [ps[:, 4 + 2 * t:6 + 2 * t, :] for t in range(TT)], 0)
                own.restart()

        @block.vector
        def _(dve):
            own = Serial(dve, dve_own, settled)

            def tt(o, i0, i1, op):
                return dve.tensor_tensor(o, i0, i1, op)

            def ts(o, i0, s1, s2, op0, op1=ALU.bypass):
                return dve.tensor_scalar(o, i0, s1, s2, op0, op1)

            def stt(o, i0, s, i1, op0, op1):
                return dve.scalar_tensor_tensor(out=o, in0=i0, scalar=s, in1=i1, op0=op0, op1=op1)

            def evacuated(l, ins, group):
                own.raise_(ins, *group_evacuated(l, group + 1))

            def raised(ins, pair):
                own.raise_(ins, *pair)

            def make_rstd(l, k):
                dve.wait_ge(*sumsq_done(l, k))
                raised(ts(stat[:, 2:4], stat[:, 0:2], 1.0 / D, 1e-6, ALU.mult, ALU.add), mean_ready(l, k))
                dve.wait_ge(*rstd_ready(l, k))

            def norm_in(l, k, n, i):
                make_rstd(l, k)
                own.step(ts(xn[:, 0, :], x[:, 0, :], stat[:, 4:5], None, ALU.mult))
                raised(ts(xn[:, 1, :], x[:, 1, :], stat[:, 5:6], None, ALU.mult), xn_ready(l, n))
                dve.wait_ge(*xn_turned(l, n))
                for kt in range(KT):
                    ins = ts(hT[:, kt, :], ps[:, 4 + kt // 2, (kt % 2) * S:(kt % 2 + 1) * S],
                             modc[:, 16 * i + 8 + kt:16 * i + 9 + kt], modc[:, 16 * i + kt:16 * i + kt + 1],
                             ALU.mult, ALU.add)
                    if kt < KT - 1:
                        own.step(ins)
                raised(ins, hT_ready(l, n if n < 3 else 4))

            def residual(l, k, src, i, n):
                make_rstd(l, k)
                for t in range(TT):
                    own.step(stt(yt, src[t], stat[:, 4 + t:5 + t], gbc[:, i, :], ALU.mult, ALU.mult))
                    ins = tt(x[:, t, :], x[:, t, :], yt, ALU.add)
                    if t == 0:
                        own.step(ins)
                raised(ins, x_updated(l, n))

            def ffn(l, f, first):
                g0 = group_of(first)

                def hidden(j, parity, down_free):
                    pair = (g0 + parity) % 2
                    dve.wait_ge(*ffn_sig(l, f * FJ + j + 1))
                    own.step(tt(sgm[:, parity, :], sgm[:, parity, :], ps[:, 2 * pair, :], ALU.mult))
                    if down_free:
                        dve.wait_ge(*down_done(l, f * FJ + j - 1))
                    evacuated(l, tt(actT[:, parity, :, :], sgm[:, parity, :], ps[:, 2 * pair + 1, :], ALU.mult), g0 + j)
                hidden(0, 0, False)
                hidden(1, 1, False)
                own.restart()
                with loop(dve, 0, 4) as i:
                    hidden(2 * i + 2, 0, True)
                    hidden(2 * i + 3, 1, True)
                    own.restart()
                hidden(10, 0, True)

            dve.wait_ge(*consts_ready(0, 1))
            own.step(ts(sc_const, dist[:, :, :], -1.0, None, ALU.mult))
            own.step(tt(dist[:, :, :], dist[:, :, :], sc_const, ALU.max))
            dve.wait_ge(*c_sig(0, 1))
            raised(tt(ccol[:, :], stat[:, 8:16], ps[:, 4, 0:8], ALU.mult), c_ready(0, 1))
            own.restart()
            dve.wait_ge(*x_loaded(0, 1))
            dve.sem_inc(layer_open.sem, 1)

            with loop(dve, 0, DEPTH) as l:
                dve.wait_ge(*params_turned(l, 1))
                own.step(dve.tensor_copy(prm[:, :], ps[:, 4, :]))
                own.step(ts(der[:, E_OMU:E_OMU + 28], prm[:, C_MU:C_MU + 28], -1.0, 1.0, ALU.mult, ALU.add))
                own.step(ts(der[:, E_HMU:E_HMU + 28], prm[:, C_MU:C_MU + 28], 0.5, None, ALU.mult))
                own.step(ts(der[:, E_W0H:E_W0H + 32], prm[:, C_W0:C_W0 + 32], 0.5, None, ALU.mult))
                own.step(ts(der[:, E_KA1:E_KA1 + 8], prm[:, C_KA:C_KA + 8], -1.0, 1.0, ALU.mult, ALU.add))
                own.step(tt(der[:, E_SUB:E_SUB + 1], prm[:, C_SUB:C_SUB + 1],
                            laminit[:, ds(l, 1), 1:2].rearrange("p a b -> p (a b)"), ALU.mult))
                own.restart()
                with loop(dve, 0, 3) as i:
                    for b in range(6):
                        dve.wait_ge(*group_done(l, i * 6 + b + 1))
                        par = b % 2
                        if b < 4:
                            ins = tt(modc[:, ds(i * 16 + b * 4, 4)], ps[:, 2 * par, 0:4],
                                     prm[:, ds(i * 24 + C_ADAB + b * 4, 4)], ALU.add)
                        else:
                            o = gbc[:, ds(i, 1), (b - 4) * 512:(b - 3) * 512]
                            ins = tt(o, o, ps[:, 2 * par:2 * par + 1, :], ALU.add)
                        evacuated(l, ins, i * 6 + b)
                for i in range(3):
                    own.step(stt(modc[:, 16 * i + 8:16 * i + 16], modc[:, 16 * i + 8:16 * i + 16], 1.0,
                                 prm[:, C_NORM + 16 * i:C_NORM + 16 * i + 8], ALU.add, ALU.mult))
                    own.step(stt(gbc[:, i, :], gbc[:, i, :], halfc[:, i:i + 1], nbc[:, i, :], ALU.mult, ALU.mult))

                norm_in(l, 1, 1, 0)
                ffn(l, 0, IT_FFA)
                dve.wait_ge(*down_done(l, FJ))
                residual(l, 2, [ps[:, 4 + 2 * t:6 + 2 * t, :].rearrange("p a b -> p (a b)") for t in range(TT)], 0, 1)
                norm_in(l, 3, 2, 1)

                own.restart()
                g = group_of(IT_RW)

                def neighbours(gi_, pair, where, n, last=P):
                    dve.wait_ge(*shift_scaled(l, gi_ - g + 1))
                    for m in range(n):
                        cols = last if m == n - 1 else P
                        dst, mcol = where(m)
                        src = ps[0:cols, 2 * pair + m // 2, (m % 2) * S:(m % 2 + 1) * S]
                        h = der[0:cols, ds(mcol, 1)]
                        own.step(stt(dst[..., 1:S], src[:, 0:S - 1], h, dst[..., 1:S], ALU.mult, ALU.add))
                        ins = stt(dst[..., 0:S - 1], src[:, 1:S], h, dst[..., 0:S - 1], ALU.mult, ALU.add)
                        if m < n - 1:
                            own.step(ins)
                    evacuated(l, ins, gi_)
                with loop(dve, 0, 3) as i:
                    for j in range(2):
                        neighbours(g + 2 * i + j, (g + j) % 2,
                                   lambda m: (rkv[:, ds(i * 8 + j * 4 + m, 1), :].rearrange("p a s -> p (a s)"),
                                              i * 8 + j * 4 + m + E_HMU), 4)
                    own.restart()
                neighbours(g + 6, g % 2, lambda m: ((cw, ca)[m], 24 + m + E_HMU), 2)
                neighbours(g + 7, (g + 1) % 2, lambda m: ((cg, cg2)[m], 26 + m + E_HMU), 2, 32)

                with when(dve, l < 1):
                    dve.tensor_copy(vfirst[:, :, :], rkv[:, 16:24, :]).then_inc(vfirst_kept.sem, 1)
                    dve.wait_ge(*vfirst_kept(0, 1))
                own.step(tt(vfd, vfirst[:, :, :], rkv[:, 16:24, :], ALU.subtract))
                for kt in range(KT):
                    own.step(ts(kkT[:, kt, :], rkv[:, 8 + kt, :], prm[:, C_KK + kt:C_KK + kt + 1], None, ALU.mult))
                raised(tt(kk_sq_buf, kkT, kkT, ALU.mult), kk_sq(l, 1))
                for n in range(4):
                    dve.wait_ge(*vmix_sig(l, n + 1))
                    d2 = vfd[:, 2 * n:2 * n + 2, :]
                    own.step(tt(d2, d2, vtmp.rearrange("p (a s) -> p a s", a=2), ALU.mult))
                    v2 = rkv[:, 16 + 2 * n:18 + 2 * n, :]
                    raised(tt(v2, v2, d2, ALU.add), v_final(l, n + 1))
                dve.wait_ge(*kk_sum(l, 1))
                raised(ts(kk_sq_buf, ps[:, 4:8, :], 1e-12, None, ALU.add), kk_eps(l, 1))
                dve.wait_ge(*kk_root(l, 1))
                own.step(dve.reciprocal(kk_sq_buf, kk_sq_buf))
                own.step(stt(kkT, kkT, -1.0, kk_sq_buf, ALU.mult, ALU.mult))
                own.restart()

                with loop(dve, 0, PAIRS) as p:
                    r_ = rkv[:, ds(p, 1), :]
                    k_ = rkv[:, ds(p + 8, 1), :]
                    v_ = rkv[:, ds(p + 16, 1), :]
                    dve.wait_ge(*lora_evac(l, p + 1))
                    own.step(ts(lwb, lwb, 1.0, NEG_EXP_HALF, ALU.add, ALU.mult))
                    own.step(ts(icl, icl, 1.0, 0.5, ALU.add, ALU.mult))
                    f512 = "p d c t -> p (d c t)"
                    own.step(dve.tensor_tensor_scan(gi.rearrange(f512), reset[:, :, :].rearrange("p a b -> p (a b)"),
                                                    lwb.rearrange(f512), 0.0, ALU.mult, ALU.add))
                    own.step(tt(ge[:, 0], gi[:, 0], lwb[:, 0], ALU.subtract))
                    own.step(tt(ge[:, 1], gi[:, 1, :, L - 1:L].to_broadcast([P, CH, L]), gi[:, 1], ALU.subtract))
                    own.step(tt(gi[:, 1], ge[:, 1], lwb[:, 1], ALU.add))
                    ic2 = icl.rearrange("p d c t -> p d (c t)")
                    own.step(ts(kdir, ic2, prm[:, ds(p + C_KA, 1)], der[:, ds(p + E_KA1, 1)], ALU.mult, ALU.add))
                    own.step(tt(kdir, kdir, k_.to_broadcast([P, 2, S]), ALU.mult))
                    own.step(tt(bprod, kdir[:, 0, :], kdir[:, 1, :], ALU.add))
                    own.step(stt(bprod, bprod, prm[:, ds(p + C_RK, 1)], r_.rearrange("p a s -> p (a s)"), ALU.mult, ALU.mult))
                    for h in range(2):
                        hh = slice(64 * h, 64 * h + 64)
                        own.step(dve.tensor_copy(vX[hh, :, h, :], rkv[hh, ds(p + 16, 1), :].rearrange("p a (c t) -> p (a c) t", c=CH)))
                    kk_ = kkT[:, ds(p, 1), :]
                    raised(stt(kb.rearrange("p d c t -> p d (c t)"), ic2, -1.0, kk_.to_broadcast([P, 2, S]), ALU.mult, ALU.mult),
                           decay_ready(l, p + 1))
                    dve.wait_ge(*bonus_done(l, p + 1))
                    own.step(tt(bonus, ps[:, 6, S:2 * S], v_.rearrange("p a s -> p (a s)"), ALU.mult))
                    raised(dve.tensor_copy(vtm, ps[:, 7, 0:S]), bonus_evac(l, p + 1))
                    dve.wait_ge(*exps_ready(l, p + 1))
                    for d in range(2):
                        u = 2 * p + d
                        for h in range(2):
                            hh = slice(64 * h, 64 * h + 64)

                            def chunks(t, q):
                                return t[hh, ds(q, 1), :].rearrange("p a (c t) -> p (a c) t", c=CH)
                            own.step(tt(arX[hh, d, :, 0, h, :], chunks(kkT, p), ege[hh, d], ALU.mult))
                            own.step(tt(arX[hh, d, :, 1, h, :], chunks(rkv, p), egi[hh, d], ALU.mult))
                            own.step(tt(btX[hh, d, :, h, :], kb[hh, d], eni[hh, d], ALU.mult))
                            ins = tt(ktX[hh, d, :, h, :], kdir[hh, d, :].rearrange("p (c t) -> p c t", c=CH), eni[hh, d], ALU.mult)
                            if h == 0:
                                own.step(ins)
                        raised(ins, ops_ready(l, u + 1))
                    b4 = [P, CH, P]
                    eye = ident[:, :].rearrange("p (a b) -> p a b", a=1).to_broadcast(b4)
                    for d in range(2):
                        u = 2 * p + d
                        dve.wait_ge(*m1_done(l, u + 1))
                        ddn = dd[:, d, :, 0, :]
                        ddt = dd[:, d, :, 1, :]
                        lm, lt = lvl[:, d], lvl[:, 1 - d]
                        rm = rmask[:, d, :, :].rearrange("p u t -> p (u t)").rearrange("p (a t) -> p a t", a=1).to_broadcast([P, 2, 2 * P])

                        def two(t, c):
                            return t[:, d, c:c + 2, :, :].rearrange("p c u t -> p c (u t)")
                        own.step(tt(ddn, ps[:, 4, :].rearrange("p (c t) -> p c t", c=CH), lm[:, 0:1, :].to_broadcast(b4), ALU.mult))
                        own.step(tt(two(mb, 0), ps[:, 5, :].rearrange("p (c t) -> p c t", c=2), rm, ALU.mult))
                        own.step(tt(two(mb, 2), ps[:, 6, :].rearrange("p (c t) -> p c t", c=2), rm, ALU.mult))
                        own.step(tt(ddn, ddn, eye, ALU.add))
                        own.step(tt(ddt, mb[:, d, :, 0, :], lt[:, 0:1, :].to_broadcast(b4), ALU.mult))
                        own.step(tt(ddt, ddt, eye, ALU.add))
                        dve.wait_ge(*m2_done(l, u + 1))
                        own.step(tt(two(mk, 0), ps[:, 7, :].rearrange("p (c t) -> p c t", c=2), rm, ALU.mult))
                        raised(tt(two(mk, 2), ps[:, 2, :].rearrange("p (c t) -> p c t", c=2), rm, ALU.mult), m2_evac(l, u + 1))
                    for k in range(LV):
                        w = p * 2 * LV + 2 * k
                        for d in range(2):
                            dve.wait_ge(*f_done(l, w + d + 1))
                            raised(tt(ee[:, d], ps[:, 2 + d, :].rearrange("p (c t) -> p c t", c=CH),
                                      lvl[:, d, k + 1:k + 2, :].to_broadcast(b4), ALU.mult), e_ready(l, w + d + 1))
                        for d in range(2):
                            dve.wait_ge(*de_done(l, w + d + 1))
                            if k < LV - 1:
                                src = ps[:, 4 + 2 * d:6 + 2 * d, :].rearrange("p u (c t) -> p u c t", c=CH)
                                dst = dd[:, d].rearrange("p c u t -> p u c t")
                            else:
                                src = ps[:, 5 + 2 * d, :].rearrange("p (c t) -> p c t", c=CH)
                                dst = dd[:, d, :, 1, :]
                            raised(tt(dst, dst, src, ALU.add), dd_ready(l, w + d + 1))
                    for j in range(CH):
                        dve.wait_ge(*r_done(l, 4 * p + j + 1))
                        raised(dve.tensor_copy(rs, ps[:, 4, 0:2 * L].rearrange("p (d v) -> p d v", d=2)), r_evac(l, 4 * p + j + 1))
                        dve.wait_ge(*u_done(l, 4 * p + j + 1))
                        raised(dve.tensor_copy(us[:, j, :, :], ps[:, 5, 0:2 * L].rearrange("p (d v) -> p d v", d=2)), u_evac(l, 4 * p + j + 1))
                        if j < CH - 1:
                            dve.wait_ge(*s_done(l, 3 * p + j + 1))
                            src = ps[:, 6, 0:2 * L].rearrange("p (d v) -> p d v", d=2)
                            if j:
                                own.step(tt(st8[:, j + 1, :, :], st8[:, j, :, :], src, ALU.add))
                                src = st8[:, j + 1, :, :]
                            own.step(ts(st8[:, j + 1, 0, :], src[:, 0, :], etot[:, 0, j:j + 1], None, ALU.mult))
                            raised(ts(st8[:, j + 1, 1, :], src[:, 1, :], etot[:, 1, CH - 1 - j:CH - j], None, ALU.mult), s_evac(l, 3 * p + j + 1))
                    dve.wait_ge(*y_done(l, p + 1))
                    yps = ps[:, 7, 0:S].rearrange("p (c t) -> p c t", c=CH)
                    own.step(dve.tensor_reduce(out=gstat[:, 0, :], in_=yps, op=ALU.add, axis=AX))
                    own.step(ts(gstat[:, 0, :], gstat[:, 0, :], 1.0 / L, None, ALU.mult))
                    own.step(tt(yy, yps, gstat[:, 0, :].rearrange("p (c a) -> p c a", a=1).to_broadcast([P, CH, L]), ALU.subtract))
                    own.step(tt(ysq, yy, yy, ALU.mult))
                    own.step(dve.tensor_reduce(out=gstat[:, 1, :], in_=ysq, op=ALU.add, axis=AX))
                    raised(ts(gstat[:, 2, :], gstat[:, 1, :], 1.0 / L, 64e-5, ALU.mult, ALU.add), gn_var(l, p + 1))
                    dve.wait_ge(*gn_rstd(l, p + 1))
                    for h in range(2):
                        hh = slice(64 * h, 64 * h + 64)
                        ins = tt(yX[hh, :, h, :], yy[hh], gstat[hh, 3, :].rearrange("p (c a) -> p c a", a=1).to_broadcast([64, CH, L]), ALU.mult)
                        if h == 0:
                            own.step(ins)
                    raised(ins, yx_ready(l, p + 1))
                    dve.wait_ge(*yt_done(l, p + 1))
                    own.step(ts(bprod, ps[:, 4, 0:S], prm[:, ds(p + C_LNW, 1)], prm[:, ds(p + C_LNB, 1)], ALU.mult, ALU.add))
                    own.step(tt(bprod, bprod, bonus, ALU.add))
                    raised(tt(r_.rearrange("p a s -> p (a s)"), bprod, gate, ALU.mult), yr_ready(l, p + 1))
                    own.restart()

                def merge(first, b, ks, n0):
                    for h in range(2):
                        gg = group_of(first + h * (1 + ks))
                        dve.wait_ge(*gate_sig(l, n0 + h + 1))
                        dve.sem_inc(group_evacuated.sem, 1)
                        dve.wait_ge(*group_done(l, gg + 2))
                        dst = merged[:, :, h * 512:(h + 1) * 512]
                        if b == 0:
                            evacuated(l, tt(dst, sg, halves((gg + 1) % 2), ALU.mult), gg + 1)
                        else:
                            own.step(tt(sg, sg, halves((gg + 1) % 2), ALU.mult))
                            evacuated(l, tt(dst, dst, sg, ALU.add), gg + 1)

                merge(IT_MR, 0, 1, 0)

                g = group_of(IT_Z)
                with loop(dve, 0, 2) as i:
                    for j in range(2):
                        dve.wait_ge(*z_sig(l, 2 * i + j + 1))
                        zz = zy[:, ds(2 * i + j, 1), :, :].rearrange("p a t c -> p (a t) c")
                        evacuated(l, tt(zz, zz, halves((g + j) % 2), ALU.mult), g + 2 * i + j)
                gx = group_of(IT_XBC)

                def conv(k, parity, dst, copy_to=None):
                    dve.wait_ge(*conv_scaled(l, k + 1))
                    for m in range(4):
                        src = ps[:, 2 * ((gx + parity) % 2) + m // 2, (m % 2) * S:(m % 2 + 1) * S]
                        c = cv[:, parity, m, :]
                        for tap in (0, 1, 3, 4):
                            s = tap - 2
                            w = prm[:, ds(k * 4 + m + C_CONVW + 24 * tap, 1)]
                            o = c[:, -s:S] if s < 0 else c[:, 0:S - s]
                            i0 = src[:, 0:S + s] if s < 0 else src[:, s:S]
                            ins = stt(o, i0, w, o, ALU.mult, ALU.add)
                            if m < 3 or tap < 4:
                                own.step(ins)
                    raised(ins, conv_raw(l, k + 1))
                    dve.wait_ge(*conv_sig(l, k + 1))
                    sig = cvs.rearrange("p (a s) -> p a s", a=4)
                    if copy_to is not None:
                        own.step(tt(copy_to, cv[:, parity, :, :], sig, ALU.mult))
                    evacuated(l, tt(dst, cv[:, parity, :, :], sig, ALU.mult), gx + k)
                own.restart()
                with loop(dve, 0, 2) as i:
                    for j in range(2):
                        conv(2 * i + j, j, cv[:, j, :, :])
                    own.restart()
                conv(4, 0, cv[:, 0, :, :], bcT[:, 0:4, :])
                conv(5, 1, bcT[:, 4:8, :])

                T0, T1, T2, T3, T4, T5, T6, T7 = (dts[:, n, :, :] for n in range(8))
                b64 = [P, TT, 64]

                def rowbc(v):
                    return v.rearrange("p (a b) -> p a b", a=1).to_broadcast(b64)
                dve.wait_ge(*dt_done(l, 1))
                own.step(tt(T0, ps[:, 6, 0:128].rearrange("p (a b) -> p a b", a=TT), rowbc(dtb), ALU.add))
                own.step(ts(T1, T0, -1.0, None, ALU.mult))
                raised(tt(T1, T0, T1, ALU.min), dt_raw(l, 1))
                dve.wait_ge(*dt_exp(l, 1))
                own.step(ts(T2, T1, 2.0, None, ALU.add))
                own.step(dve.reciprocal(T2, T2))
                own.step(tt(T1, T1, T2, ALU.mult))
                own.step(tt(T2, T1, T1, ALU.mult))
                own.step(ts(T7, T2, 1.0 / 15, None, ALU.mult))
                for n in (13, 11, 9, 7, 5, 3):
                    own.step(stt(T7, T7, 1.0 / n, T2, ALU.add, ALU.mult))
                own.step(stt(T7, T7, 1.0, T1, ALU.add, ALU.mult))
                own.step(ts(T0, T0, 0.0, None, ALU.max))
                own.step(stt(T0, T7, 2.0, T0, ALU.mult, ALU.add))
                raised(stt(T6, T0, -1.0, rowbc(alog), ALU.mult, ALU.mult), da_ready(l, 1))
                dve.wait_ge(*acs_done(l, 1))
                own.step(dve.tensor_copy(T4, ps[:, 6, 0:128].rearrange("p (a b) -> p a b", a=TT)))
                raised(dve.tensor_copy(acsT, ps[0:64, 7, 0:S]), acs_evac(l, 1))
                dve.wait_ge(*acs_turned(l, 1))
                own.step(dve.tensor_copy(T3, ps[:, 7, 256:384].rearrange("p (a b) -> p a b", a=TT)))
                raised(tt(T4, T4, T3, ALU.subtract), acs_diff(l, 1))
                dve.wait_ge(*acs_exp(l, 1))
                own.restart()

                def heads(t, c, h0):
                    return t[:, c, h0].rearrange("p (h a) -> p h a", a=1).to_broadcast([P, 8, 64])

                with loop(dve, 0, 4) as gg:
                    dve.wait_ge(*cb_done(l, gg + 1))
                    for d in range(2):
                        ins = tt(cbm[:, d, :, :], ps[:, 4, 0:256].rearrange("p (c t) -> p c t", c=TT),
                                 tri[:, d:d + 1, :].to_broadcast([P, TT, P]), ALU.mult)
                        if d == 0:
                            own.step(ins)
                    raised(ins, cb_evac(l, gg + 1))
                    for n in range(4):
                        c, d = n // 2, n % 2
                        dve.wait_ge(*acs_bc[n % 2](l, 2 * gg + n // 2 + 1))
                        a_s = dts[:, 3, c, ds(gg * 8 + d * 32, 8)].rearrange("p (h a) -> p h a", a=1).to_broadcast([P, 8, P])
                        own.step(tt(wx[:, n, :, :], bca[:, n % 2, :, :], a_s, ALU.subtract))
                        raised(ts(wx[:, n, :, :], wx[:, n, :, :], 0.0, None, ALU.min), seg_ready(l, 4 * gg + n + 1))
                    xg = [xtm[:, c, ds(gg * 512, 512)].rearrange("p (h q) -> p h q", h=8) for c in range(TT)]
                    for c in range(TT):
                        for d in range(2):
                            n = 2 * c + d
                            own.step(tt(xdt[:, n, :, :], xg[c], heads(dts[:, 0], c, ds(gg * 8 + d * 32, 8)), ALU.mult))
                            dve.wait_ge(*seg_exp(l, 4 * gg + n + 1))
                            ins = tt(wx[:, n, :, :], wx[:, n, :, :], cbm[:, d, c:c + 1, :].to_broadcast([P, 8, P]), ALU.mult)
                            if d == 0:
                                own.step(ins)
                        raised(ins, wx_ready(l, 2 * gg + c + 1))
                    for c in range(TT):
                        dsk = dskip[:, ds(gg * 8, 8)].rearrange("p (h a) -> p h a", a=1).to_broadcast([P, 8, 64])
                        ymc = ym[:, c, :].rearrange("p (h q) -> p h q", h=8)
                        own.step(tt(ymc, xg[c], dsk, ALU.mult))
                        dve.wait_ge(*ydiag_done(l, 2 * gg + c + 1))
                        raised(tt(ym[:, c, :], ym[:, c, :], ps[:, 5 + c, :], ALU.add), ydiag_evac(l, 2 * gg + c + 1))
                    for d in range(2):
                        hcol = ds(gg * 8 + d * 32, 8)
                        if d:
                            dve.wait_ge(*state_done(l, 2 * gg + 1))
                        raised(tt(xs, xdt[:, 3 * d, :, :], heads(dts[:, 4], d, hcol), ALU.mult), xs_ready(l, 2 * gg + d + 1))
                        dve.wait_ge(*yoff_done(l, 2 * gg + d + 1))
                        raised(tt(ytmp.rearrange("p (h q) -> p h q", h=8), ps[:, 4, :].rearrange("p (h q) -> p h q", h=8),
                                  heads(dts[:, 5], 1 - d, hcol), ALU.mult), yoff_evac(l, 2 * gg + d + 1))
                        own.step(tt(ym[:, 1 - d, :], ym[:, 1 - d, :], ytmp, ALU.add))
                    zz = zy[:, ds(gg, 1), :, :].rearrange("p a t c -> p (a t) c")
                    own.step(tt(ym, ym, zz, ALU.mult))
                    for c in range(TT):
                        own.step(tt(ytmp, ym[:, c, :], ym[:, c, :], ALU.mult))
                        own.step(dve.tensor_reduce(out=mstat[:, c:c + 1], in_=ytmp, op=ALU.add, axis=AX))
                    raised(ts(mstat[:, 2:4], mstat[:, 0:2], 1.0 / 512, 1e-5, ALU.mult, ALU.add), msq_ready(l, gg + 1))
                    dve.wait_ge(*mrstd_ready(l, gg + 1))
                    own.step(ts(ym[:, 0, :], ym[:, 0, :], mstat[:, 4:5], None, ALU.mult))
                    raised(ts(ym[:, 1, :], ym[:, 1, :], mstat[:, 5:6], None, ALU.mult), ym_ready(l, gg + 1))
                    dve.wait_ge(*ym_turned(l, gg + 1))
                    for m in range(4):
                        dst = zy[:, ds(gg, 1), m // 2, (m % 2) * S:(m % 2 + 1) * S]
                        ins = ts(dst, ps[:, 5 + m // 2:6 + m // 2, (m % 2) * S:(m % 2 + 1) * S], prm[:, ds(gg * 4 + m + C_MNW, 1)], None, ALU.mult)
                        if m < 3:
                            own.step(ins)
                    raised(ins, ymT_ready(l, gg + 1))
                    own.restart()
                merge(IT_MM, 1, 2, 2)

                g = group_of(IT_DF)
                own.restart()
                with loop(dve, 0, 2) as i:
                    for j in range(2):
                        dve.wait_ge(*group_done(l, g + 2 * i + j + 1))
                        evacuated(l, dve.tensor_copy(qkT[:, ds(i * 8 + j * 4, 4), :].rearrange("p a s -> p (a s)"),
                                                     halves((g + j) % 2).rearrange("p a s -> p (a s)")), g + 2 * i + j)
                for j in range(2):
                    dve.wait_ge(*group_done(l, g + 4 + j + 1))
                    evacuated(l, dve.tensor_copy(vdm[:, :, j * 512:(j + 1) * 512], halves((g + j) % 2)), g + 4 + j)
                dve.wait_ge(*diff_w_loaded(l, 1))
                for n in range(2):
                    own.step(tt(dlam[:, 2 * n, :], dlam[:, 2 * n, :], dlam[:, 2 * n + 1, :], ALU.mult))
                    ins = dve.tensor_reduce(out=dstat[:, 24 + n:25 + n], in_=dlam[:, 2 * n, :], op=ALU.add, axis=AX)
                    if n == 0:
                        own.step(ins)
                raised(ins, lam_raw(l, 1))
                dve.wait_ge(*lam_exp(l, 1))
                own.step(tt(dstat[:, 28:29], dstat[:, 27:28], dstat[:, 26:27], ALU.subtract))
                own.step(tt(dstat[:, 28:29], dstat[:, 28:29], laminit[:, ds(l, 1), 0:1].rearrange("p a b -> p (a b)"), ALU.subtract))
                own.restart()
                with loop(dve, 0, 8) as h:
                    dve.wait_ge(*sc_done(l, h + 1))
                    for t in range(TT):
                        own.step(stt(sc[:, t, :, :], dist[:, t:t + 1, :].to_broadcast([P, 2, S]), slopes[:, ds(h, 1)],
                                     ps[:, 4 + t, :].rearrange("p (m s) -> p m s", m=2), ALU.mult, ALU.add))
                    own.step(dve.tensor_reduce(out=dstat[:, 0:4], in_=sc.rearrange("p t m s -> p (t m) s"), op=ALU.max, axis=AX))
                    raised(ts(dstat[:, 4:8], dstat[:, 0:4], -0.125, None, ALU.mult), smax_ready(l, h + 1))
                    dve.wait_ge(*p_ready(l, h + 1))
                    own.step(dve.reciprocal(dstat[:, 12:16], dstat[:, 8:12]))
                    for t in range(TT):
                        own.step(tt(dstat[:, 13 + 2 * t:14 + 2 * t], dstat[:, 13 + 2 * t:14 + 2 * t], dstat[:, 28:29], ALU.mult))
                        own.step(ts(am[:, t, :], pr[:, t, 0, :], dstat[:, 12 + 2 * t:13 + 2 * t], None, ALU.mult))
                        ins = stt(am[:, t, :], pr[:, t, 1, :], dstat[:, 13 + 2 * t:14 + 2 * t], am[:, t, :], ALU.mult, ALU.add)
                        if t == 0:
                            own.step(ins)
                    raised(ins, am_ready(l, h + 1))
                    dve.wait_ge(*am_turned(l, h + 1))
                    raised(dve.tensor_copy(amT.rearrange("p a s -> p (a s)"), ps[:, 6, :]), amT_ready(l, h + 1))
                    dve.wait_ge(*o_sq(l, h + 1))
                    raised(ts(dstat[:, 18:20], dstat[:, 16:18], 1.0 / P, 1e-5, ALU.mult, ALU.add), o_mean(l, h + 1))
                    dve.wait_ge(*o_rstd(l, h + 1))
                    own.step(ts(on[:, 0, :], ps[:, 7, 0:P], dstat[:, 20:21], None, ALU.mult))
                    raised(ts(on[:, 1, :], ps[:, 7, P:2 * P], dstat[:, 21:22], None, ALU.mult), on_ready(l, h + 1))
                    dve.wait_ge(*on_turned(l, h + 1))
                    raised(ts(ydT[:, ds(h, 1), :].rearrange("p a s -> p (a s)"), ps[:, 6, 0:S], der[:, E_SUB:E_SUB + 1], None, ALU.mult), yd_ready(l, h + 1))
                    own.restart()
                merge(IT_MD, 2, 1, 4)

                dve.wait_ge(*merged_turned(l, 1))
                raised(dve.tensor_copy(hT[:, :, :].rearrange("p a s -> p (a s)"), ps[:, 4:8, :].rearrange("p a s -> p (a s)")), hT_ready(l, 3))
                for h in range(2):
                    g = group_of(IT_OUT + h)
                    dve.wait_ge(*group_done(l, g + 1))
                    evacuated(l, dve.tensor_copy(merged[:, :, h * 512:(h + 1) * 512], halves(g % 2)), g)
                residual(l, 4, [merged[:, t, :] for t in range(TT)], 1, 2)
                norm_in(l, 5, 3, 2)
                ffn(l, 1, IT_FFB)
                dve.wait_ge(*down_done(l, 2 * FJ))
                residual(l, 6, [ps[:, 4 + 2 * t:6 + 2 * t, :].rearrange("p a b -> p (a b)") for t in range(TT)], 2, 3)
                own.restart()
                dve.sem_inc(layer_open.sem, 1)


INPUTS = ["x", "c", "ada_w", "ada_b", "norm_w", "ffn_w13", "ffn_w2", "w_in", "rwkv_mu", "rwkv_w0", "rwkv_w2",
          "rwkv_a0", "rwkv_a2", "rwkv_g2", "rwkv_k_k", "rwkv_k_a", "rwkv_r_k", "rwkv_ln_w", "rwkv_ln_b", "rwkv_v0",
          "rwkv_v1", "rwkv_v2", "mamba_conv_w", "mamba_conv_b", "mamba_dt_bias", "mamba_a_log", "mamba_d",
          "mamba_norm_w", "diff_lambda", "diff_subln_w", "w_branch_rwkv", "w_branch_mamba", "w_branch_diff", "w_out"]


def kernel(**inputs):
    import numpy as np
    import concourse.bacc as bacc
    from concourse.bass_utils import run_bass_kernel_spmd

    nc = bacc.Bacc("TRN2", target_bir_lowering=False, num_devices=1)
    arrays, args = {}, {}
    for name in INPUTS:
        v = np.ascontiguousarray(inputs[name])
        arrays[f"in_{name}"] = v
        args[name] = nc.dram_tensor(f"in_{name}", v.shape, mybir.dt.from_np(v.dtype), kind="ExternalInput").ap()
    out = nc.dram_tensor("out", (1, S, D), F32, kind="ExternalOutput").ap()
    build(nc, args, out)
    return run_bass_kernel_spmd(nc, [arrays], core_ids=[0]).results[0]["out"]
```

```python
from contextlib import ExitStack, contextmanager
import math

import concourse.bass as bass
from concourse import mybir

F32 = mybir.dt.float32
I32 = mybir.dt.int32
ALU = mybir.AluOpType
ACT = mybir.ActivationFunctionType
AX = mybir.AxisListType.X
ds = bass.ds

P = 128
D = 1024
KT = D // P
S = 256
TT = S // P
DEPTH = 2
FF = 2816
FJ = FF // 256
RW = 3488
MB0 = RW
XBC0 = MB0 + 2048
DT0 = XBC0 + 3072
DF0 = DT0 + 64
GT0 = DF0 + 3072
NIN = GT0 + 3072
HEADS = 8
PAIRS = 8
L = 64
CH = S // L
LV = 5

IT_ADA, IT_FFA, IT_RW, IT_LATE, IT_MR, IT_Z, IT_XBC, IT_MM, IT_DF, IT_MD, IT_OUT, IT_FFB, N_ITEM = (
    0, 12, 23, 31, 37, 41, 45, 51, 57, 63, 67, 69, 80)


def group_of(item):
    return item - (item > 52) - (item > 55)


N_GROUP = group_of(N_ITEM)


def loads_before(item, parity):
    return sum(2 if IT_FFA <= n < IT_RW or n >= IT_FFB else 1 for n in range(item) if n % 2 == parity)

C_CONVW, C_V0 = 0, 120
C_ADAB, C_NORM, C_KK = 128, 200, 248
C_W0, C_A0, C_KA, C_RK, C_LNW, C_LNB, C_MNW, C_CONVB, C_SUB = 256, 272, 288, 296, 304, 312, 320, 336, 360
C_MU = 384
E_OMU, E_HMU, E_W0H, E_A0H, E_KA1, E_SUB, N_DER = 0, 28, 56, 72, 88, 96, 97

SCRATCH = 28400
NEG_EXP_HALF = -0.5 * math.exp(-0.5)


class Signal:

    def __init__(self, sem, per_layer, by=1):
        self.sem, self.per_layer, self.by = sem, per_layer, by

    def __call__(self, l, k):
        return self.sem, (l * self.per_layer + k) * self.by


class Serial:

    def __init__(self, eng, sem, settled):
        self.eng, self.sem, self.settled, self.n = eng, sem, settled, 0

    def step(self, ins):
        self.n += 1
        ins.then_inc(self.sem, 1)
        self.eng.wait_ge(self.sem, self.n)

    def raise_(self, ins, sem, value):
        ins.then_inc(sem, 1)
        self.eng.wait_ge(sem, value)

    def restart(self):
        if self.n:
            self.eng.wait_ge(self.sem, self.n)
            self.eng.sem_inc(self.settled, 1)
            self.eng.sem_clear(self.sem)
        self.n = 0


def build(nc, a, out):
    with ExitStack() as ctx:
        def sb(name, shape):
            return ctx.enter_context(nc.sbuf_tensor(name, shape, F32))

        def signal(name, per_layer, by=1):
            return Signal(ctx.enter_context(nc.semaphore(name)), per_layer, by)

        ring = sb("ring", [P, 2, 4096])
        x = sb("x", [P, TT, D])
        hT = sb("hT", [P, KT, S])
        gbc = sb("gbc", [P, 3, D])
        prow = sb("prow", [P, 4, P])
        prm = sb("prm", [P, 512])
        der = sb("der", [P, N_DER])
        modc = sb("modc", [P, 48])
        vfirst = sb("vfirst", [P, KT, S])
        merged = sb("merged", [P, TT, D])
        ident = sb("ident", [P, P])
        ones = sb("ones", [P, P])
        onesblk = sb("onesblk", [P, 2, L])
        stack_i = sb("stack_i", [P, L])
        tri = sb("tri", [P, 2, P])
        rmask = sb("rmask", [P, 2, 2, P])
        lvl = sb("lvl", [P, 2, LV + 1, P])
        reset = sb("reset", [P, 2 * CH, L])
        dist = sb("dist", [P, TT, S])
        slopes = sb("slopes", [P, 8])
        halfc = sb("halfc", [P, 3])
        laminit = sb("laminit", [P, DEPTH, 2])
        mhalf = sb("mhalf", [P, 8])
        ccol = sb("ccol", [P, KT])
        crow = sb("crow", [8, P])
        stat = sb("stat", [P, 16])
        U = sb("scratch", [P, SCRATCH])

        def carver():
            at = [0]

            def carve(shape, parts=P):
                n = 1
                for s in shape:
                    n *= s
                v = U[0:parts, at[0]:at[0] + n]
                at[0] += n
                assert at[0] <= SCRATCH, at[0]
                names = "abcde"[:len(shape)]
                if len(shape) == 1:
                    return v
                return v.rearrange("p (%s) -> p %s" % (" ".join(names), " ".join(names)),
                                   **{c: s for c, s in zip(names, shape)})
            return carve, at

        carve, at = carver()
        xn = carve([TT, D])
        w2s = carve([2, 2, D])
        sgm = carve([2, 512])
        actT = carve([2, 2, S])
        yt = carve([D])
        nbc = carve([2, D])

        carve, at = carver()
        rkv = carve([24, S])
        cw = carve([S])
        ca = carve([S])
        cg = carve([S])
        cg2 = carve([S], 32)
        kkT = carve([PAIRS, S])
        lora = carve([3, P])
        g2b = carve([P], 32)
        vfd_at = at[0]
        lwb = carve([2, CH, L])
        icl = carve([2, CH, L])
        gi = carve([2, CH, L])
        ge = carve([2, CH, L])
        kdir = carve([2, S])
        kb = carve([2, CH, L])
        etot = carve([2, CH])
        bprod = carve([S])
        bonus = carve([S])
        gate = carve([S])
        vX = carve([CH, 2, L])
        vtm = carve([CH, L])
        arX = carve([2, CH, 2, 2, L])
        btX = carve([2, CH, 2, L])
        ktX = carve([2, CH, 2, L])
        btm_at = at[0]
        btm = carve([2, CH, P])
        ktm = carve([2, CH, P])
        mb_at = at[0]
        mb = carve([2, CH, 2, P])
        mk = carve([2, CH, 2, P])
        dd = carve([2, CH, 2, P])
        ee_at = at[0]
        ee = carve([2, CH, P])
        yy = ee[:, 0, 0:2, :].rearrange("p a b -> p (a b)").rearrange("p (c v) -> p c v", c=CH)
        ysq = ee[:, 0, 2:4, :].rearrange("p a b -> p (a b)").rearrange("p (c v) -> p c v", c=CH)
        rs = carve([2, L])
        yX = carve([CH, 2, L])
        gstat = carve([4, CH])
        st8 = U[:, ee_at:ee_at + 512].rearrange("p (j d v) -> p j d v", j=CH, d=2)
        us = U[:, ee_at + 512:ee_at + 1024].rearrange("p (j d v) -> p j d v", j=CH, d=2)
        ege, egi, eni = ge, gi, lwb
        v1s = U[:, mb_at:mb_at + 256].rearrange("p (k n) -> p k n", k=KT)
        v2s = U[0:32, mb_at + 256:mb_at + 1280]
        vrs = U[0:32, mb_at + 1280:mb_at + 1536]
        vtmp = U[:, mb_at + 1536:mb_at + 2048]
        vfd = U[:, vfd_at:vfd_at + KT * S].rearrange("p (k s) -> p k s", k=KT)
        kk_sq_buf = merged[:, :, :].rearrange("p t (k s) -> p (t k) s", s=S)

        sg = U[:, 20480:21504].rearrange("p (a b) -> p a b", a=TT)

        carve, at = carver()
        zy = carve([4, TT, 512])
        xtm = carve([TT, 2048])
        bcT = carve([8, S])
        btk = carve([TT, 512])
        wdt = carve([KT, 64])
        dtb = carve([64])
        alog = carve([64])
        dskip = carve([32])
        dts = carve([8, TT, 64])
        acsT = carve([S], 64)
        bg = carve([S])
        cgm = carve([S])
        btg = carve([TT, P])
        cbm = carve([2, TT, P])
        bca = carve([2, 8, P])
        wx_at = at[0]
        wx = carve([4, 8, P])
        cv = U[:, wx_at:wx_at + 2048].rearrange("p (i m s) -> p i m s", i=2, m=4)
        cvs = U[:, wx_at + 2048:wx_at + 3072]
        xdt = carve([4, 8, 64])
        xs = carve([8, 64])
        h0 = carve([512])
        ym = carve([TT, 512])
        ytmp = carve([512])
        mstat = carve([16])

        carve, at = carver()
        qkT = carve([16, S])
        vdm = carve([TT, D])
        qX = carve([2, S])
        sc = carve([TT, 2, S])
        pr = carve([TT, 2, S])
        am = carve([TT, S])
        amT = carve([TT, S])
        on = carve([TT, P])
        ydT = carve([8, S])
        dlam = carve([4, 64])
        dstat = carve([32])

        ps = ctx.enter_context(nc.psum_tensor("ps", [P, 8, 512], F32))
        disti = U[:, TT * S:2 * TT * S].bitcast(I32).rearrange("p (t s) -> p t s", t=TT)
        sc_const = U[:, 0:TT * S].rearrange("p (t s) -> p t s", t=TT)
        acs_dram = nc.dram_tensor("acs_scratch", (64, S), F32).ap()

        consts_ready = signal("consts_ready", 0)
        x_loaded = signal("x_loaded", 0, 16)
        c_loaded = signal("c_loaded", 0, 16)
        c_turned = signal("c_turned", 0)
        c_sig = signal("c_sig", 0)
        c_ready = signal("c_ready", 0)
        out_stored = signal("out_stored", 0, 16)
        dve_own = ctx.enter_context(nc.semaphore("dve_own"))
        act_own = ctx.enter_context(nc.semaphore("act_own"))
        pool_own = ctx.enter_context(nc.semaphore("pool_own"))
        settled = ctx.enter_context(nc.semaphore("settled"))

        layer_open = signal("layer_open", 1)
        params_loaded = signal("params_loaded", 15, 16)
        params_turned = signal("params_turned", 1)
        bc_loaded = signal("bc_loaded", 3, 16)
        slot_loaded = [signal(f"slot_loaded{i}", loads_before(N_ITEM, i), 16) for i in range(2)]
        group_done = signal("group_done", N_GROUP)
        group_evacuated = signal("group_evacuated", N_GROUP)
        sumsq_done = signal("sumsq_done", 6)
        mean_ready = signal("mean_ready", 6)
        rstd_ready = signal("rstd_ready", 6)
        xn_ready = signal("xn_ready", 3)
        x_updated = signal("x_updated", 3)
        xn_turned = signal("xn_turned", 3)
        hT_ready = signal("hT_ready", 4)
        ffn_sig = signal("ffn_sig", 2 * FJ)
        w2_loaded = [signal("w2_loaded0", 12, 16), signal("w2_loaded1", 10, 16)]
        down_done = signal("down_done", 2 * FJ)
        shift_scaled = signal("shift_scaled", 8)
        lora_act = signal("lora_act", 1)
        vlow_done = signal("vlow_done", 1)
        vlow_evac = signal("vlow_evac", 1)
        vmix_done = signal("vmix_done", 4)
        vmix_sig = signal("vmix_sig", 4)
        v_final = signal("v_final", 4)
        kk_sq = signal("kk_sq", 1)
        kk_sum = signal("kk_sum", 1)
        kk_root = signal("kk_root", 1)
        kk_eps = signal("kk_eps", 1)
        vfirst_kept = signal("vfirst_kept", 0)
        rwkv_w_loaded = signal("rwkv_w_loaded", 2, 16)
        pair_w_loaded = signal("pair_w_loaded", 4 * PAIRS, 16)
        lora_done = signal("lora_done", PAIRS)
        lora_evac = signal("lora_evac", PAIRS)
        cum_ready = signal("cum_ready", PAIRS)
        decay_ready = signal("decay_ready", PAIRS)
        vx_ready = signal("vx_ready", PAIRS)
        etot_ready = signal("etot_ready", PAIRS)
        vtm_ready = signal("vtm_ready", PAIRS)
        gate_kept = signal("gate_kept", PAIRS)
        late_weights_loaded = signal("late_weights_loaded", 1, 16)
        exps_ready = signal("exps_ready", PAIRS)
        bonus_done = signal("bonus_done", PAIRS)
        bonus_evac = signal("bonus_evac", PAIRS)
        ops_ready = signal("ops_ready", 2 * PAIRS)
        turned_done = signal("turned_done", 2 * PAIRS)
        m1_done = signal("m1_done", 2 * PAIRS)
        turned_evac = signal("turned_evac", 2 * PAIRS)
        m2_done = signal("m2_done", 2 * PAIRS)
        m2_evac = signal("m2_evac", 2 * PAIRS)
        f_done = signal("f_done", 2 * LV * PAIRS)
        e_ready = signal("e_ready", 2 * LV * PAIRS)
        de_done = signal("de_done", 2 * LV * PAIRS)
        dd_ready = signal("dd_ready", 2 * LV * PAIRS)
        r_done = signal("r_done", 4 * PAIRS)
        r_evac = signal("r_evac", 4 * PAIRS)
        u_done = signal("u_done", 4 * PAIRS)
        u_evac = signal("u_evac", 4 * PAIRS)
        s_done = signal("s_done", 3 * PAIRS)
        s_evac = signal("s_evac", 3 * PAIRS)
        y_done = signal("y_done", PAIRS)
        gn_var = signal("gn_var", PAIRS)
        gn_rstd = signal("gn_rstd", PAIRS)
        yx_ready = signal("yx_ready", PAIRS)
        yt_done = signal("yt_done", PAIRS)
        yr_ready = signal("yr_ready", PAIRS)
        gate_sig = signal("gate_sig", 6)
        z_sig = signal("z_sig", 4)
        conv_scaled = signal("conv_scaled", 6)
        conv_raw = signal("conv_raw", 6)
        conv_sig = signal("conv_sig", 6)
        conv_turned = signal("conv_turned", 5)
        conv_evac = signal("conv_evac", 5)
        mamba_w_loaded = signal("mamba_w_loaded", 4, 16)
        dt_done = signal("dt_done", 1)
        dt_raw = signal("dt_raw", 1)
        dt_exp = signal("dt_exp", 1)
        da_ready = signal("da_ready", 1)
        acs_done = signal("acs_done", 1)
        acs_evac = signal("acs_evac", 1)
        acs_turned = signal("acs_turned", 1)
        acs_diff = signal("acs_diff", 1)
        acs_exp = signal("acs_exp", 1)
        acs_stored = signal("acs_stored", 1, 16)
        acs_bc = [signal(f"acs_bc{i}", 8, 16) for i in range(2)]
        group_staged = signal("group_staged", 4)
        cb_done = signal("cb_done", 4)
        cb_evac = signal("cb_evac", 4)
        seg_ready = signal("seg_ready", 16)
        seg_exp = signal("seg_exp", 16)
        wx_ready = signal("wx_ready", 8)
        ydiag_done = signal("ydiag_done", 8)
        ydiag_evac = signal("ydiag_evac", 8)
        xs_ready = signal("xs_ready", 8)
        state_done = signal("state_done", 8)
        state_evac = signal("state_evac", 8)
        yoff_done = signal("yoff_done", 8)
        yoff_evac = signal("yoff_evac", 8)
        msq_ready = signal("msq_ready", 4)
        mrstd_ready = signal("mrstd_ready", 4)
        ym_ready = signal("ym_ready", 4)
        ym_turned = signal("ym_turned", 4)
        ymT_ready = signal("ymT_ready", 4)
        diff_w_loaded = signal("diff_w_loaded", 1, 16)
        lam_raw = signal("lam_raw", 1)
        lam_exp = signal("lam_exp", 1)
        qx_ready = signal("qx_ready", 8)
        sc_done = signal("sc_done", 8)
        smax_ready = signal("smax_ready", 8)
        p_ready = signal("p_ready", 8)
        am_ready = signal("am_ready", 8)
        am_turned = signal("am_turned", 8)
        amT_ready = signal("amT_ready", 8)
        o_done = signal("o_done", 8)
        o_sq = signal("o_sq", 8)
        o_mean = signal("o_mean", 8)
        o_rstd = signal("o_rstd", 8)
        on_ready = signal("on_ready", 8)
        on_turned = signal("on_turned", 8)
        yd_ready = signal("yd_ready", 8)
        merged_turned = signal("merged_turned", 1)

        def settle(eng):
            eng.sem_inc(settled, 1)

        @contextmanager
        def loop(eng, first, end):
            settle(eng)
            with eng.Fori(first, end) as i:
                yield i
                settle(eng)

        @contextmanager
        def when(eng, condition):
            settle(eng)
            with eng.If(condition):
                yield
                settle(eng)

        block = ctx.enter_context(nc.Block())

        def halves(pair):
            return ps[:, 2 * pair:2 * pair + 2, :]

        def row(dram, l):
            return dram[ds(l, 1)]

        @block.sync
        def _(sp):
            sp.dma_start(x[:, :, :], a["x"].rearrange("a (t p) n -> p (a t) n", p=P)).then_inc(x_loaded.sem, 16)

            def load(l, item, parity, src, cols=512, free_after=None):
                dst = ring[:, parity, 0:KT * cols].rearrange("p (k n) -> p k n", k=KT)
                if free_after is not None:
                    sp.wait_ge(*group_done(l, free_after))
                sp.dma_start(dst, src).then_inc(slot_loaded[parity].sem, 16)

            def kmaj(ap):
                return ap.rearrange("a (k p) n -> p (a k) n", p=P)

            def feed_forward(l, f, first):
                def step(j, parity, wait_down):
                    par = (first + parity) % 2
                    w13 = row(a["ffn_w13"], l)[:, f, :, :].rearrange("a (k p) (u n) -> p (a k) u n", p=P, u=2)
                    dst = ring[:, par, :].rearrange("p (k u n) -> p k u n", k=KT, u=2)
                    sp.wait_ge(*group_done(l, group_of(first) + j - 1))
                    for u in range(2):
                        sp.dma_start(dst[:, :, u, :], w13[:, :, u, ds(j * 256, 256)]).then_inc(
                            slot_loaded[par].sem, 16)
                    if wait_down:
                        sp.wait_ge(*down_done(l, f * FJ + j - 1))
                    w2 = row(a["ffn_w2"], l)[:, f, ds(j * 256, 256), :].rearrange("a (k p) n -> p (a k) n", p=P)
                    sp.dma_start(w2s[:, parity, :, :], w2).then_inc(w2_loaded[parity].sem, 16)
                sp.wait_ge(*xn_ready(l, 3 if f else 1))
                settle(sp)
                step(0, 0, False)
                step(1, 1, False)
                with loop(sp, 0, 4) as i:
                    step(2 * i + 2, 0, True)
                    step(2 * i + 3, 1, True)
                step(10, 0, True)

            with loop(sp, 0, DEPTH) as l:
                sp.wait_ge(*layer_open(l, 1))
                ada = row(a["ada_w"], l)
                load(l, 0, 0, kmaj(ada[:, :, 0:512]))
                load(l, 1, 1, kmaj(ada[:, :, 512:1024]))
                with loop(sp, 1, 6) as i:
                    load(l, 2 * i, 0, kmaj(ada[:, :, ds(i * 1024, 512)]), free_after=2 * i - 1)
                    load(l, 2 * i + 1, 1, kmaj(ada[:, :, ds(i * 1024 + 512, 512)]), free_after=2 * i)
                feed_forward(l, 0, IT_FFA)
                w_in = row(a["w_in"], l)
                par = IT_RW % 2
                with loop(sp, 0, 3) as i:
                    for j in range(2):
                        load(l, IT_RW, (par + j) % 2, kmaj(w_in[:, :, ds(i * 1024 + j * 512, 512)]),
                             free_after=group_of(IT_RW) + 2 * i + j - 1)
                load(l, IT_RW + 6, par, kmaj(w_in[:, :, 3072:3328]), 256, group_of(IT_RW) + 5)
                load(l, IT_RW + 7, 1 - par, kmaj(w_in[:, :, 3328:RW]), 160, group_of(IT_RW) + 6)
                with loop(sp, 0, 3) as i:
                    for j in range(2):
                        load(l, IT_LATE, (IT_LATE + j) % 2, kmaj(ada[:, :, ds(i * 1024 + 2 * 3 * D + j * 512, 512)]),
                             free_after=group_of(IT_LATE) + 2 * i + j - 1)

                def merge(first, b, src, ks):
                    item = first
                    for h in range(2):
                        c0 = GT0 + b * D + h * 512
                        load(l, item, item % 2, kmaj(w_in[:, :, c0:c0 + 512]), free_after=group_of(item - 2) + 1)
                        item += 1
                        for k in range(ks):
                            load(l, item, item % 2, kmaj(src[:, k * D:(k + 1) * D, h * 512:h * 512 + 512]),
                                 free_after=group_of(item - 2) + 1)
                            item += 1

                merge(IT_MR, 0, row(a["w_branch_rwkv"], l), 1)
                for first, c0, n in ((IT_Z, MB0, 2), (IT_XBC, XBC0, 3)):
                    with loop(sp, 0, n) as i:
                        for j in range(2):
                            load(l, first, (first + j) % 2, kmaj(w_in[:, :, ds(i * 1024 + c0 + j * 512, 512)]),
                                 free_after=group_of(first) + 2 * i + j - 1)
                merge(IT_MM, 1, row(a["w_branch_mamba"], l), 2)
                sp.wait_ge(*group_done(l, group_of(IT_DF)))
                with loop(sp, 0, 3) as i:
                    for j in range(2):
                        load(l, IT_DF, (IT_DF + j) % 2, kmaj(w_in[:, :, ds(i * 1024 + DF0 + j * 512, 512)]),
                             free_after=group_of(IT_DF) + 2 * i + j - 1)
                merge(IT_MD, 2, row(a["w_branch_diff"], l), 1)
                for h in range(2):
                    load(l, IT_OUT + h, (IT_OUT + h) % 2, kmaj(row(a["w_out"], l)[:, :, h * 512:h * 512 + 512]),
                         free_after=group_of(IT_OUT + h - 2) + 1)
                feed_forward(l, 1, IT_FFB)
            sp.wait_ge(*layer_open(DEPTH, 1))
            sp.dma_start(out.rearrange("a (t p) n -> p (a t) n", p=P), x[:, :, :]).then_inc(out_stored.sem, 16)
            sp.wait_ge(*out_stored(0, 1))

        @block.gpsimd
        def _(pool):
            own = Serial(pool, pool_own, settled)

            def keep(m, pattern, base, mult, op=ALU.is_ge, fill=0.0):
                own.step(pool.affine_select(out=m, in_=m, compare_op=op, fill=fill, base=base,
                                            pattern=pattern, channel_multiplier=mult))
            own.step(pool.memset(ident[:, :], 0.0))
            keep(ident[:, :], [[-1, P]], 0, 1, ALU.not_equal, 1.0)
            own.step(pool.memset(ones[:, :], 1.0))
            own.step(pool.memset(onesblk[:, :, :], 1.0))
            keep(onesblk[:, :, :], [[-L, 2], [0, L]], 0, 1)
            keep(onesblk[:, :, :], [[L, 2], [0, L]], L - 1, -1)
            own.step(pool.memset(stack_i[:, :], 0.0))
            keep(stack_i[:, :], [[-1, L]], 0, 1, ALU.not_equal, 1.0)
            keep(stack_i[:, :], [[-1, L]], -L, 1, ALU.not_equal, 1.0)
            own.step(pool.memset(tri[:, :, :], 1.0))
            keep(tri[:, 0, :], [[1, P]], 0, -1)
            keep(tri[:, 1, :], [[-1, P]], 0, 1)
            for d in range(2):
                for incl in range(2):
                    m = rmask[:, d, incl, :]
                    own.step(pool.tensor_copy(m, onesblk[:, :, :].rearrange("p a b -> p (a b)")))
                    keep(m, [[1 if d == 0 else -1, P]], incl - 1, -1 if d == 0 else 1)
            own.step(pool.memset(lvl[:, :, :, :], 0.0))
            for k in range(LV + 1):
                h = 1 << k
                nb = P // (2 * h)
                for d in range(2):
                    m = lvl[:, d, k, :].rearrange("p (b u i) -> p b u i", u=2, i=h)
                    own.step(pool.memset(m[:, :, d, :], 1.0))
                    keep(m[:, :, :, :], [[-2 * h, nb], [0, 2], [0, h]], -h if d == 0 else 0, 1)
                    keep(m[:, :, :, :], [[2 * h, nb], [0, 2], [0, h]], (2 * h if d == 0 else h) - 1, -1)
            own.step(pool.memset(reset[:, :, :], 1.0))
            own.step(pool.memset(reset[:, :, 0:1], 0.0))
            own.step(pool.iota(disti[:, :, :], pattern=[[P, TT], [-1, S]], base=0, channel_multiplier=1))
            own.step(pool.tensor_copy(dist[:, :, :], disti[:, :, :]))
            for h in range(8):
                own.step(pool.memset(slopes[:, h:h + 1], -(2.0 ** -(h + 1)) * 8.0))
            own.step(pool.memset(halfc[:, :], 0.5))
            own.step(pool.memset(halfc[:, 1:2], 1.0))
            own.step(pool.memset(mhalf[:, :], -0.5))
            for l in range(DEPTH):
                li = 0.8 - 0.6 * math.exp(-0.3 * l)
                own.step(pool.memset(laminit[:, l, 0:1], li))
                own.step(pool.memset(laminit[:, l, 1:2], 1.0 - li))
            own.step(pool.memset(vfirst[:, :, :], 0.0))
            own.step(pool.memset(prow[:, :, :], 0.0))
            pool.memset(stat[:, :], 0.0).then_inc(consts_ready.sem, 1)
            pool.wait_ge(*consts_ready(0, 1))
            pool.dma_start(crow[:, :], a["c"].rearrange("a (k p) -> (a k) p", p=P)).then_inc(c_loaded.sem, 16)
            own.restart()

            def rstd(l, k, n):
                pool.wait_ge(*mean_ready(l, k))
                pool.tensor_tensor(stat[:, 4:4 + n], stat[:, 2:2 + n], mhalf[:, 0:n], ALU.pow).then_inc(rstd_ready.sem, 1)

            with loop(pool, 0, DEPTH) as l:
                pool.wait_ge(*layer_open(l, 1))
                rows = [("mamba_conv_w", 0, 0, 120, "a k (c p) -> (a k c) p"),
                        ("ada_b", 1, 0, 72, "a (c p) -> (a c) p"),
                        ("norm_w", 1, 72, 48, "a k (c p) -> (a k c) p"),
                        ("rwkv_k_k", 1, 120, 8, "a (c p) -> (a c) p"),
                        ("rwkv_w0", 2, 0, 16, "a k (c p) -> (a k c) p"),
                        ("rwkv_a0", 2, 16, 16, "a k (c p) -> (a k c) p"),
                        ("rwkv_k_a", 2, 32, 8, "a (c p) -> (a c) p"),
                        ("rwkv_ln_w", 2, 48, 8, "a (c p) -> (a c) p"),
                        ("rwkv_ln_b", 2, 56, 8, "a (c p) -> (a c) p"),
                        ("mamba_norm_w", 2, 64, 16, "a (c p) -> (a c) p"),
                        ("mamba_conv_b", 2, 80, 24, "a (c p) -> (a c) p"),
                        ("diff_subln_w", 2, 104, 1, None)]
                for name, t, r0, n, how in rows:
                    src = row(a[name], l)
                    if how:
                        src = src.rearrange(how, p=P)
                    pool.dma_start(prow[r0:r0 + n, t, :], src).then_inc(params_loaded.sem, 16)
                pool.dma_start(prow[40:48, 2, :],
                               row(a["rwkv_r_k"], l).rearrange("a (c h) p -> (a c) h p", h=2)).then_inc(params_loaded.sem, 16)
                pool.dma_start(prow[120:128, 0, :],
                               a["rwkv_v0"].rearrange("a (c p) -> (a c) p", p=P)).then_inc(params_loaded.sem, 16)
                mu = row(a["rwkv_mu"], l)
                pool.dma_start(prow[0:27, 3, :], mu[:, 0:27 * P].rearrange("a (c p) -> (a c) p", p=P)
                               ).then_inc(params_loaded.sem, 16)
                pool.dma_start(prow[27:28, 3, 0:32], mu[:, 27 * P:RW]).then_inc(bc_loaded.sem, 16)
                adab = row(a["ada_b"], l).rearrange("a (i w n) -> a i w n", i=3, w=3)
                pool.dma_start(gbc[:, :, :], adab[:, :, 2, :].to_broadcast([P, 3, D])).then_inc(bc_loaded.sem, 16)
                nw = row(a["norm_w"], l).rearrange("a (i w) n -> a i w n", w=2)
                pool.dma_start(nbc[:, :, :], nw[:, 0:2, 1, :].to_broadcast([P, 2, D])).then_inc(bc_loaded.sem, 16)

                rstd(l, 1, 2)
                rstd(l, 2, 2)
                rstd(l, 3, 2)
                pool.wait_ge(*xn_ready(l, 2))
                pool.wait_ge(*hT_ready(l, 2))
                settle(pool)
                pool.dma_start(v1s[:, :, :], a["rwkv_v1"].rearrange("a (k p) n -> p (a k) n", p=P)).then_inc(rwkv_w_loaded.sem, 16)
                pool.dma_start(v2s[:, :], a["rwkv_v2"].rearrange("a p n -> (a p) n")).then_inc(rwkv_w_loaded.sem, 16)
                for t in (vX, arX, btX, ktX, yX):
                    own.step(pool.memset(t, 0.0))
                own.restart()
                def pair_loads(q):
                    c = ds(q * P, P)
                    pool.dma_start(lora[:, 0, :], row(a["rwkv_w2"], l)[:, :, :, c].rearrange("a d r n -> (a d r) n")).then_inc(pair_w_loaded.sem, 16)
                    pool.dma_start(lora[:, 1, :], row(a["rwkv_a2"], l)[:, :, :, c].rearrange("a d r n -> (a d r) n")).then_inc(pair_w_loaded.sem, 16)
                    pool.dma_start(lora[:, 2, :], row(a["rwkv_g2"], l)[:, 0:P, c].rearrange("a r n -> (a r) n")).then_inc(pair_w_loaded.sem, 16)
                    pool.dma_start(g2b[:, :], row(a["rwkv_g2"], l)[:, P:160, c].rearrange("a r n -> (a r) n")).then_inc(pair_w_loaded.sem, 16)

                def pair_values(q):
                    hh = slice(0, 64)
                    own.step(pool.tensor_copy(vX[hh, :, 0, :], rkv[hh, ds(q + 16, 1), :].rearrange("p a (c t) -> p (a c) t", c=CH)))
                    hh = slice(64, 128)
                    pool.tensor_copy(vX[hh, :, 1, :], rkv[hh, ds(q + 16, 1), :].rearrange("p a (c t) -> p (a c) t", c=CH)
                                     ).then_inc(vx_ready.sem, 1)
                    pool.wait_ge(*vx_ready(l, q + 1))

                def group_norm_rstd(q):
                    pool.wait_ge(*gn_var(l, q + 1))
                    pool.tensor_tensor(gstat[:, 3, :], gstat[:, 2, :], mhalf[:, 0:CH], ALU.pow).then_inc(gn_rstd.sem, 1)
                    pool.wait_ge(*gn_rstd(l, q + 1))

                def next_pair(q):
                    pool.wait_ge(*lora_done(l, q))
                    settle(pool)
                    pair_loads(q)
                    pool.wait_ge(*bonus_done(l, q))
                    settle(pool)
                    pair_values(q)

                pair_loads(0)
                pool.wait_ge(*v_final(l, 4))
                settle(pool)
                pair_values(0)
                next_pair(1)
                settle(pool)
                pool.dma_start(merged[:, 0:1, :], nw[:, 2:3, 1, :].to_broadcast([P, 1, D])).then_inc(late_weights_loaded.sem, 16)
                own.restart()
                with loop(pool, 2, PAIRS) as q:
                    next_pair(q)
                    group_norm_rstd(q - 2)
                    own.restart()
                group_norm_rstd(PAIRS - 2)
                group_norm_rstd(PAIRS - 1)
                pool.wait_ge(*group_evacuated(l, group_of(IT_Z)))
                pool.dma_start(wdt[:, :, :], row(a["w_in"], l)[:, :, DT0:DT0 + 64].rearrange("a (k p) n -> p (a k) n", p=P)).then_inc(mamba_w_loaded.sem, 16)
                pool.dma_start(dtb[:, :], row(a["mamba_dt_bias"], l).rearrange("a d h -> a (d h)").to_broadcast([P, 64])).then_inc(mamba_w_loaded.sem, 16)
                pool.dma_start(alog[:, :], row(a["mamba_a_log"], l).rearrange("a d h -> a (d h)").to_broadcast([P, 64])).then_inc(mamba_w_loaded.sem, 16)
                pool.dma_start(dskip[:, :], row(a["mamba_d"], l).to_broadcast([P, 32])).then_inc(mamba_w_loaded.sem, 16)
                pool.wait_ge(*acs_evac(l, 1))
                settle(pool)
                pool.dma_start(acs_dram, acsT[:, :]).then_inc(acs_stored.sem, 16)
                pool.wait_ge(*acs_stored(l, 1))
                def stage_group(g):
                    own.step(pool.tensor_copy(bg[:, :], bcT[:, ds(g, 1), :]))
                    own.step(pool.tensor_copy(cgm[:, :], bcT[:, ds(g + 4, 1), :]))
                    pool.tensor_copy(btg[:, :, :], btk[:, :, ds(g * P, P)]).then_inc(group_staged.sem, 1)
                    pool.wait_ge(*group_staged(l, g + 1))
                    settle(pool)

                def load_decays(g, n):
                    c, d = n // 2, n % 2
                    i = n % 2
                    src = acs_dram[ds(g * 8 + d * 32, 8), c * P:(c + 1) * P].rearrange("(a h) n -> a h n", a=1)
                    pool.dma_start(bca[:, i, :, :], src.to_broadcast([P, 8, P])).then_inc(acs_bc[i].sem, 16)

                def group_rstd(g):
                    pool.wait_ge(*msq_ready(l, g + 1))
                    pool.tensor_tensor(mstat[:, 4:6], mstat[:, 2:4], mhalf[:, 0:2], ALU.pow).then_inc(mrstd_ready.sem, 1)
                    pool.wait_ge(*mrstd_ready(l, g + 1))

                settle(pool)
                stage_group(0)
                for n in range(4):
                    if n >= 2:
                        pool.wait_ge(*seg_ready(l, n - 1))
                        settle(pool)
                    load_decays(0, n)
                own.restart()
                with loop(pool, 0, 3) as g:
                    pool.wait_ge(*yoff_evac(l, 2 * g + 2))
                    settle(pool)
                    stage_group(g + 1)
                    for n in range(2):
                        pool.wait_ge(*seg_ready(l, 4 * g + 3 + n))
                        settle(pool)
                        load_decays(g + 1, n)
                    group_rstd(g)
                    for n in range(2, 4):
                        pool.wait_ge(*seg_ready(l, 4 * g + 3 + n))
                        settle(pool)
                        load_decays(g + 1, n)
                    own.restart()
                group_rstd(3)
                pool.wait_ge(*group_evacuated(l, group_of(IT_DF)))
                pool.dma_start(dlam[:, :, :], row(a["diff_lambda"], l).to_broadcast([P, 4, 64])).then_inc(diff_w_loaded.sem, 16)
                own.step(pool.memset(qX[:, :, :], 0.0))
                pool.wait_ge(*diff_w_loaded(l, 1))
                own.restart()
                def head_queries(h):
                    own.step(pool.tensor_copy(qX[0:64, 0, :], qkT[0:64, ds(h, 1), :]))
                    pool.tensor_copy(qX[64:P, 1, :], qkT[64:P, ds(h, 1), :]).then_inc(qx_ready.sem, 1)
                    pool.wait_ge(*qx_ready(l, h + 1))

                def head_rstd(h):
                    pool.wait_ge(*o_mean(l, h + 1))
                    pool.tensor_tensor(dstat[:, 20:22], dstat[:, 18:20], mhalf[:, 0:2], ALU.pow).then_inc(o_rstd.sem, 1)
                    pool.wait_ge(*o_rstd(l, h + 1))

                pool.wait_ge(*group_evacuated(l, group_of(IT_DF) + 4))
                settle(pool)
                head_queries(0)
                pool.wait_ge(*sc_done(l, 1))
                settle(pool)
                head_queries(1)
                own.restart()
                with loop(pool, 0, HEADS - 2) as h:
                    pool.wait_ge(*sc_done(l, h + 2))
                    settle(pool)
                    head_queries(h + 2)
                    head_rstd(h)
                    own.restart()
                head_rstd(HEADS - 2)
                head_rstd(HEADS - 1)
                rstd(l, 4, 2)
                rstd(l, 5, 2)
                rstd(l, 6, 2)

        @block.tensor
        def _(pe):
            def mm(o, lhsT, rhs, start=True, stop=True):
                return pe.matmul(o, lhsT, rhs, start=start, stop=stop)

            def slot(parity, cols=512):
                return ring[:, parity, 0:KT * cols].rearrange("p (k n) -> p k n", k=KT)

            def bank_free(l, group):
                pe.wait_ge(*group_evacuated(l, group - 1))

            def to_channels(pair, w, src, n_mt=4, last=P, k0=0):
                for m in range(n_mt):
                    cols = last if m == n_mt - 1 else P
                    o = ps[0:cols, 2 * pair + m // 2, (m % 2) * S:(m % 2 + 1) * S]
                    for k in range(KT):
                        ins = mm(o, w[:, k, m * P:m * P + cols], src[:, k, :], k == 0, k == KT - 1)
                return ins

            def to_tokens(pair, w, src, k0=0, nk=KT, first=True, final=True):
                for t in range(TT):
                    for k in range(nk):
                        ins = mm(ps[:, 2 * pair + t, :], src[:, k0 + k, t * P:(t + 1) * P], w[:, k, :],
                                 first and k == 0, final and k == nk - 1)
                return ins

            def turn_norm(l, k):
                pe.wait_ge(*xn_ready(l, k))
                for kt in range(KT):
                    for t in range(TT):
                        o = ps[:, 4 + kt // 2, (kt % 2) * S + t * P:(kt % 2) * S + (t + 1) * P]
                        ins = pe.transpose(o, xn[:, t, kt * P:(kt + 1) * P], ident[:, :])
                ins.then_inc(xn_turned.sem, 1)

            def feed_forward(l, f, first):
                g0 = group_of(first)

                def up(j, half_item, parity):
                    item_par = (first + parity) % 2
                    pe.wait_ge(*ffn_arrival(l, f, first, half_item, parity))
                    bank_free(l, g0 + j)
                    w = ring[:, item_par, :].rearrange("p (k u n) -> p k u n", k=KT, u=2)
                    pair = (g0 + parity) % 2
                    for u in range(2):
                        for m in range(2):
                            for k in range(KT):
                                ins = mm(ps[:, 2 * pair + u, m * S:(m + 1) * S], w[:, k, u, m * P:(m + 1) * P],
                                         hT[:, k, :], k == 0, k == KT - 1)
                    ins.then_inc(group_done.sem, 1)

                def down(j, half_item, parity, start=False, stop=False):
                    pe.wait_ge(*w2_loaded[parity](l, f * (6 if parity == 0 else 5) + half_item + 1))
                    pe.wait_ge(*group_evacuated(l, g0 + j + 1))
                    for t in range(TT):
                        for h in range(2):
                            for k in range(2):
                                ins = mm(ps[:, 4 + 2 * t + h, :], actT[:, parity, k, t * P:(t + 1) * P],
                                         w2s[:, parity, k, h * 512:(h + 1) * 512],
                                         start and k == 0, stop and k == 1)
                    ins.then_inc(down_done.sem, 1)

                pe.wait_ge(*hT_ready(l, 4 if f else 1))
                up(0, 0, 0)
                up(1, 0, 1)
                down(0, 0, 0, start=True)
                with loop(pe, 0, 4) as i:
                    up(2 * i + 2, i + 1, 0)
                    down(2 * i + 1, i, 1)
                    up(2 * i + 3, i + 1, 1)
                    down(2 * i + 2, i + 1, 0)
                up(10, 5, 0)
                down(9, 4, 1)
                down(10, 5, 0, stop=True)

            def ffn_arrival(l, f, first, half_item, parity):
                par = (first + parity) % 2
                return slot_loaded[par](l, loads_before(first + parity, par) + 2 * (half_item + 1))

            pe.wait_ge(*consts_ready(0, 1))
            pe.wait_ge(*c_loaded(0, 1))
            pe.transpose(ps[:, 4, 0:8], crow[:, :], ident[0:8, 0:8]).then_inc(c_turned.sem, 1)
            pe.wait_ge(*c_ready(0, 1))

            with loop(pe, 0, DEPTH) as l:
                pe.wait_ge(*layer_open(l, 1))
                pe.wait_ge(*params_loaded(l, 15))
                pe.wait_ge(*bc_loaded(l, 3))
                for t in range(4):
                    ins = pe.transpose(ps[:, 4, t * P:(t + 1) * P], prow[:, t, :], ident[:, :])
                ins.then_inc(params_turned.sem, 1)

                def modulation(bank, w, columns):
                    if columns:
                        for m in range(4):
                            for k in range(KT):
                                ins = mm(ps[:, bank, m:m + 1], w[:, k, m * P:(m + 1) * P], ccol[:, k:k + 1],
                                         k == 0, k == KT - 1)
                    else:
                        for k in range(KT):
                            ins = mm(ps[:, bank, :], ccol[:, k:k + 1].to_broadcast([P, P]), w[:, k, :],
                                     k == 0, k == KT - 1)
                    ins.then_inc(group_done.sem, 1)

                with loop(pe, 0, 2) as i:
                    for b in range(6):
                        par = b % 2
                        pe.wait_ge(*slot_loaded[par](l, i * 3 + b // 2 + 1))
                        if b >= 2:
                            bank_free(l, i * 6 + b)
                        modulation(2 * par, slot(par), b < 4)
                    pe.wait_ge(*group_evacuated(l, 6 * i + 6))

                turn_norm(l, 1)
                feed_forward(l, 0, IT_FFA)
                turn_norm(l, 2)
                pe.wait_ge(*hT_ready(l, 2))

                def project(item, i, run, parity, kind, **kw):
                    g = group_of(item)
                    par = (item + parity) % 2
                    pe.wait_ge(*slot_loaded[par](l, loads_before(item + parity, par) + run + 1))
                    bank_free(l, g + i)
                    pair = (g + parity) % 2
                    ins = kind(pair, slot(par, kw.pop("cols", 512)), hT, **kw)
                    ins.then_inc(group_done.sem, 1)

                with loop(pe, 0, 3) as i:
                    for j in range(2):
                        project(IT_RW, 2 * i + j, i, j, to_channels)
                project(IT_RW + 6, 0, 0, 0, to_channels, n_mt=2, cols=256)
                project(IT_RW + 7, 0, 0, 0, to_channels, n_mt=2, last=32, cols=160)

                pe.wait_ge(*group_evacuated(l, group_of(IT_RW) + 8))
                pe.wait_ge(*rwkv_w_loaded(l, 2))
                for k in range(KT):
                    ins = mm(ps[0:32, 4, 0:S], v1s[:, k, :], rkv[:, 16 + k, :], k == 0, k == KT - 1)
                ins.then_inc(vlow_done.sem, 1)
                pe.wait_ge(*vlow_evac(l, 1))
                for n in range(4):
                    if n >= 2:
                        pe.wait_ge(*v_final(l, n - 1))
                    for m in range(2):
                        kt = 2 * n + m
                        ins = mm(ps[:, 4 + n % 2, m * S:(m + 1) * S], v2s[:, kt * P:(kt + 1) * P], vrs[:, :])
                    ins.then_inc(vmix_done.sem, 1)
                pe.wait_ge(*v_final(l, 4))
                pe.wait_ge(*kk_sq(l, 1))
                for n in range(4):
                    ins = mm(ps[:, 4 + n, :], onesblk[:, :, :].rearrange("p a b -> p (a b)"),
                             kk_sq_buf[:, 2 * n:2 * n + 2, :])
                ins.then_inc(kk_sum.sem, 1)
                pe.wait_ge(*kk_root(l, 1))

                def flat(t):
                    return t.rearrange("p a b -> p (a b)")

                def by_all(o, t, d, c):
                    return mm(o, flat(t[:, d, c, :, :]), arX[:, d, c, :, :, :].rearrange("p u a b -> p (u a b)"))

                def chunk(d, j):
                    return j if d == 0 else CH - 1 - j

                def pair_lora(q):
                    pe.wait_ge(*pair_w_loaded(l, 4 * q + 4))
                    for d in range(2):
                        rr = slice(d * 64, d * 64 + 64)
                        mm(ps[:, 2 + d, 0:S], lora[rr, 0, :], cw[rr, :])
                        mm(ps[:, 2 + d, S:2 * S], lora[rr, 1, :], ca[rr, :])
                    mm(ps[:, 0, 0:S], lora[:, 2, :], cg[:, :], True, False)
                    mm(ps[:, 0, 0:S], g2b[:, :], cg2[:, :], False, True).then_inc(lora_done.sem, 1)

                def pair_bonus(q):
                    pe.wait_ge(*vx_ready(l, q + 1))
                    for c in range(CH):
                        mm(ps[:, 1, c * L:(c + 1) * L], vX[:, c, :, :].rearrange("p a b -> p (a b)"), stack_i[:, :])
                    pe.wait_ge(*decay_ready(l, q + 1))
                    mm(ps[:, 0, S:2 * S], onesblk[:, :, :].rearrange("p a b -> p (a b)"), bprod[:, :]).then_inc(bonus_done.sem, 1)

                def pair_turn_y(q):
                    pe.wait_ge(*yx_ready(l, q + 1))
                    for c in range(CH):
                        ins = mm(ps[:, 1, S + c * L:S + (c + 1) * L], yX[:, c, :, :].rearrange("p a b -> p (a b)"), stack_i[:, :])
                    ins.then_inc(yt_done.sem, 1)

                def late_modulation(n, j, bank, columns):
                    item = IT_LATE + j
                    par = item % 2
                    pe.wait_ge(*slot_loaded[par](l, loads_before(item, par) + n + 1))
                    modulation(bank, slot(par), columns)

                def pair_body(p, first, last, late=None):
                    late_g = group_of(IT_LATE) + 2 * (p - 1)
                    if late:
                        late_modulation(p - 1, 0, 6, late == "columns")
                    for d in range(2):
                        u = 2 * p + d
                        if d and late:
                            late_modulation(p - 1, 1, 3, late == "columns")
                        pe.wait_ge(*ops_ready(l, u + 1))
                        if d:
                            pe.wait_ge(*m2_evac(l, u))
                            if late:
                                pe.wait_ge(*group_evacuated(l, late_g + 2))
                        for c in range(CH):
                            pe.transpose(ps[:, 2, c * P:(c + 1) * P], flat(btX[:, d, c, :, :]), ident[:, :])
                        for c in range(CH):
                            ins = pe.transpose(ps[:, 3, c * P:(c + 1) * P], flat(ktX[:, d, c, :, :]), ident[:, :])
                        ins.then_inc(turned_done.sem, 1)
                        for c in range(CH):
                            mm(ps[:, 4, c * P:(c + 1) * P], flat(arX[:, d, c, 0, :, :]), flat(btX[:, d, c, :, :]))
                        if late and d == 0:
                            pe.wait_ge(*group_evacuated(l, late_g + 1))
                        for c in range(CH):
                            ins = by_all(ps[:, 5 + c // 2, (c % 2) * S:(c % 2 + 1) * S], btX, d, c)
                        ins.then_inc(m1_done.sem, 1)
                        if d == 0 and not first:
                            pair_turn_y(p - 1)
                        pe.wait_ge(*turned_evac(l, u + 1))
                        for c in range(CH):
                            ins = by_all(ps[:, (7, 2)[c // 2], (c % 2) * S:(c % 2 + 1) * S], ktX, d, c)
                        ins.then_inc(m2_done.sem, 1)
                    pe.wait_ge(*m2_evac(l, 2 * p + 2))
                    for k in range(LV):
                        w = p * 2 * LV + 2 * k
                        for d in range(2):
                            if k:
                                pe.wait_ge(*dd_ready(l, w - 1 + d))
                            for c in range(CH):
                                ins = mm(ps[:, 2 + d, c * P:(c + 1) * P], mb[:, d, c, 0, :], dd[:, d, c, 0, :])
                            ins.then_inc(f_done.sem, 1)
                        for d in range(2):
                            pe.wait_ge(*e_ready(l, w + d + 1))
                            for c in range(CH):
                                if k < LV - 1:
                                    mm(ps[:, 4 + 2 * d, c * P:(c + 1) * P], dd[:, d, c, 1, :], ee[:, d, c, :])
                                ins = mm(ps[:, 5 + 2 * d, c * P:(c + 1) * P], ee[:, d, c, :], dd[:, d, c, 1, :])
                            ins.then_inc(de_done.sem, 1)
                    pe.wait_ge(*dd_ready(l, (p + 1) * 2 * LV))
                    def values_share(o, weights, c, start, stop):
                        return mm(o, weights, vtm[:, c, :], start, stop)

                    pe.wait_ge(*gate_kept(l, p + 1))
                    for d in range(2):
                        c = chunk(d, 0)
                        ins = values_share(ps[:, 4, d * L:(d + 1) * L], mk[:, d, c, 0, :], c, True, True)
                    ins.then_inc(r_done.sem, 1)
                    for j in range(CH):
                        if j:
                            pe.wait_ge(*s_evac(l, 3 * p + j))
                            for d in range(2):
                                c = chunk(d, j)
                                ins = mm(ps[:, 4, d * L:(d + 1) * L], flat(arX[:, d, c, 0, :, :]), st8[:, j, d, :], False, d == 1)
                            ins.then_inc(r_done.sem, 1)
                            for d in range(2):
                                c = chunk(d, j)
                                mm(ps[:, 7, c * L:(c + 1) * L], flat(arX[:, d, c, 1, :, :]), st8[:, j, d, :], False, False)
                        else:
                            for c in range(CH):
                                values_share(ps[:, 7, c * L:(c + 1) * L], mk[:, 0, c, 1, :], c, c == 0, False)
                        pe.wait_ge(*r_evac(l, 4 * p + j + 1))
                        for d in range(2):
                            ins = mm(ps[:, 5, d * L:(d + 1) * L], dd[:, d, chunk(d, j), 1, :], rs[:, d, :])
                        ins.then_inc(u_done.sem, 1)
                        if j < CH - 1:
                            for d in range(2):
                                c = chunk(d, j + 1)
                                values_share(ps[:, 4, d * L:(d + 1) * L], mk[:, d, c, 0, :], c, d == 0, False)
                            for d in range(2):
                                c = chunk(d, j)
                                values_share(ps[:, 6, d * L:(d + 1) * L], ktm[:, d, c, :], c, d == 0, False)
                        pe.wait_ge(*u_evac(l, 4 * p + j + 1))
                        if j < CH - 1:
                            for d in range(2):
                                ins = mm(ps[:, 6, d * L:(d + 1) * L], btm[:, d, chunk(d, j), :], us[:, j, d, :], False, d == 1)
                            ins.then_inc(s_done.sem, 1)
                        if j == 0:
                            for c in range(CH):
                                values_share(ps[:, 7, c * L:(c + 1) * L], mk[:, 1, c, 1, :], c, False, False)
                        for d in range(2):
                            c = chunk(d, j)
                            ins = mm(ps[:, 7, c * L:(c + 1) * L], mb[:, d, c, 1, :], us[:, j, d, :], False,
                                     j == CH - 1 and d == 1)
                        if j == CH - 1:
                            ins.then_inc(y_done.sem, 1)
                        if j == 0 and not last:
                            pair_lora(p + 1)
                    if not last:
                        pair_bonus(p + 1)

                pair_lora(0)
                pair_bonus(0)
                pair_body(0, True, False)
                with loop(pe, 1, 3) as p:
                    pair_body(p, False, False, "columns")
                pair_body(3, False, False, "rows")
                with loop(pe, 4, PAIRS - 1) as p:
                    pair_body(p, False, False)
                pair_body(PAIRS - 1, False, True)
                pair_turn_y(PAIRS - 1)
                pe.wait_ge(*yr_ready(l, PAIRS))

                def merge(first, yT, ks):
                    item = first
                    for h in range(2):
                        for kind in range(2):
                            g = group_of(item)
                            n = ks if kind else 1
                            for kk in range(n):
                                par = item % 2
                                pe.wait_ge(*slot_loaded[par](l, loads_before(item, par) + 1))
                                if kk == 0:
                                    bank_free(l, g)
                                if n == 1:
                                    ins = to_tokens(g % 2, slot(par), yT if kind else hT)
                                else:
                                    ins = to_tokens(g % 2, slot(par), yT, 8 * kk, KT, kk == 0, kk == n - 1)
                                item += 1
                            ins.then_inc(group_done.sem, 1)

                merge(IT_MR, rkv, 1)

                with loop(pe, 0, 2) as i:
                    for j in range(2):
                        project(IT_Z, 2 * i + j, i, j, to_tokens)

                def turn_conv(k, parity, later=None):
                    pe.wait_ge(*group_evacuated(l, group_of(IT_XBC) + k + 1))
                    if later is None:
                        pe.wait_ge(*conv_evac(l, k))
                    else:
                        with when(pe, later > 0):
                            pe.wait_ge(*conv_evac(l, k))
                    for t in range(TT):
                        for m in range(4):
                            ins = pe.transpose(ps[:, 4 + t, m * P:(m + 1) * P], cv[:, parity, m, t * P:(t + 1) * P], ident[:, :])
                    ins.then_inc(conv_turned.sem, 1)
                with loop(pe, 0, 2) as i:
                    for j in range(2):
                        project(IT_XBC, 2 * i + j, i, j, to_channels)
                        turn_conv(2 * i + j, j, None if j else i)
                project(IT_XBC, 4, 2, 0, to_channels)
                turn_conv(4, 0)
                project(IT_XBC, 5, 2, 1, to_channels)
                pe.wait_ge(*mamba_w_loaded(l, 4))
                for t in range(TT):
                    for k in range(KT):
                        ins = mm(ps[:, 6, t * 64:(t + 1) * 64], hT[:, k, t * P:(t + 1) * P], wdt[:, k, :], k == 0, k == KT - 1)
                ins.then_inc(dt_done.sem, 1)
                pe.wait_ge(*da_ready(l, 1))
                for c in range(TT):
                    for d in range(2):
                        mm(ps[d * 32:d * 32 + 32, 7, c * P:(c + 1) * P], dts[:, 6, c, d * 32:d * 32 + 32], tri[:, d, :])
                for c in range(TT):
                    ins = mm(ps[:, 6, c * 64:(c + 1) * 64], ones[:, :], dts[:, 6, c, :])
                ins.then_inc(acs_done.sem, 1)
                pe.wait_ge(*acs_evac(l, 1))
                settle(pe)
                for c in range(TT):
                    ins = pe.transpose(ps[:, 7, 256 + c * 64:256 + (c + 1) * 64], acsT[:, c * P:(c + 1) * P], ident[0:64, 0:64])
                ins.then_inc(acs_turned.sem, 1)
                pe.wait_ge(*acs_exp(l, 1))
                pe.wait_ge(*group_evacuated(l, group_of(IT_MM)))

                with loop(pe, 0, 4) as g:
                    pe.wait_ge(*group_staged(l, g + 1))
                    with when(pe, g > 0):
                        pe.wait_ge(*ymT_ready(l, g))
                    for c in range(TT):
                        ins = mm(ps[:, 4, c * P:(c + 1) * P], bg[:, c * P:(c + 1) * P], cgm[:, c * P:(c + 1) * P])
                    ins.then_inc(cb_done.sem, 1)
                    for d in range(2):
                        pe.wait_ge(*xs_ready(l, 2 * g + d + 1))
                        mm(ps[:, 7, :], btg[:, d, :], xs[:, :, :].rearrange("p a b -> p (a b)")).then_inc(state_done.sem, 1)
                        pe.wait_ge(*state_evac(l, 2 * g + d + 1))
                        if d:
                            pe.wait_ge(*yoff_evac(l, 2 * g + 1))
                        else:
                            pe.wait_ge(*cb_evac(l, g + 1))
                        mm(ps[:, 4, :], cgm[:, (1 - d) * P:(2 - d) * P], h0[:, :]).then_inc(yoff_done.sem, 1)
                    for c in range(TT):
                        pe.wait_ge(*wx_ready(l, 2 * g + c + 1))
                        for h in range(8):
                            for d in range(2):
                                ins = mm(ps[:, 5 + c, h * 64:(h + 1) * 64], wx[:, 2 * c + d, h, :], xdt[:, 2 * c + d, h, :],
                                         d == 0, d == 1)
                        ins.then_inc(ydiag_done.sem, 1)
                    pe.wait_ge(*ym_ready(l, g + 1))
                    for m in range(4):
                        for c in range(TT):
                            o = ps[:, 5 + m // 2, (m % 2) * S + c * P:(m % 2) * S + (c + 1) * P]
                            ins = pe.transpose(o, ym[:, c, m * P:(m + 1) * P], ident[:, :])
                    ins.then_inc(ym_turned.sem, 1)
                pe.wait_ge(*ymT_ready(l, 4))
                merge(IT_MM, zy.rearrange("p g t c -> p (g t c)").rearrange("p (k s) -> p k s", s=S), 2)

                with loop(pe, 0, 2) as i:
                    for j in range(2):
                        project(IT_DF, 2 * i + j, i, j, to_channels)
                for j in range(2):
                    project(IT_DF, 4 + j, 2, j, to_tokens)
                pe.wait_ge(*group_evacuated(l, group_of(IT_DF) + 6))
                def head_scores(h):
                    pe.wait_ge(*qx_ready(l, h + 1))
                    for t in range(TT):
                        for m in range(2):
                            ins = mm(ps[:, 4 + t, m * S:(m + 1) * S], qX[:, m, t * P:(t + 1) * P], qkT[:, ds(h + 8, 1), :])
                    ins.then_inc(sc_done.sem, 1)

                def head_body(h, last):
                    if not last:
                        pe.wait_ge(*smax_ready(l, h + 1))
                        head_scores(h + 1)
                    pe.wait_ge(*am_ready(l, h + 1))
                    for kt in range(TT):
                        for t in range(TT):
                            ins = pe.transpose(ps[:, 6, kt * S + t * P:kt * S + (t + 1) * P], am[:, t, kt * P:(kt + 1) * P], ident[:, :])
                    ins.then_inc(am_turned.sem, 1)
                    pe.wait_ge(*amT_ready(l, h + 1))
                    for t in range(TT):
                        for kt in range(TT):
                            ins = mm(ps[:, 7, t * P:(t + 1) * P], amT[:, kt, t * P:(t + 1) * P], vdm[:, kt, ds(h * P, P)],
                                     kt == 0, kt == 1)
                    ins.then_inc(o_done.sem, 1)
                    pe.wait_ge(*on_ready(l, h + 1))
                    for t in range(TT):
                        ins = pe.transpose(ps[:, 6, t * P:(t + 1) * P], on[:, t, :], ident[:, :])
                    ins.then_inc(on_turned.sem, 1)

                head_scores(0)
                with loop(pe, 0, HEADS - 1) as h:
                    head_body(h, False)
                head_body(HEADS - 1, True)
                pe.wait_ge(*yd_ready(l, 8))
                merge(IT_MD, ydT, 1)

                pe.wait_ge(*group_evacuated(l, group_of(IT_OUT)))
                for kt in range(KT):
                    for t in range(TT):
                        o = ps[:, 4 + kt // 2, (kt % 2) * S + t * P:(kt % 2) * S + (t + 1) * P]
                        ins = pe.transpose(o, merged[:, t, kt * P:(kt + 1) * P], ident[:, :])
                ins.then_inc(merged_turned.sem, 1)
                pe.wait_ge(*hT_ready(l, 3))
                for h in range(2):
                    item = IT_OUT + h
                    par = item % 2
                    pe.wait_ge(*slot_loaded[par](l, loads_before(item, par) + 1))
                    bank_free(l, group_of(item))
                    to_tokens(group_of(item) % 2, slot(par), hT).then_inc(group_done.sem, 1)
                turn_norm(l, 3)
                feed_forward(l, 1, IT_FFB)

        @block.scalar
        def _(act):
            own = Serial(act, act_own, settled)

            def sumsq(l, k, src, into):
                for t in range(TT):
                    own.step(act.activation(yt[:, :], src[t], ACT.Square, accum_out=stat[:, t:t + 1]))
                act.sem_inc(sumsq_done.sem, 1)

            def ffn(l, f, first):
                g0 = group_of(first)

                def gate_of(j, parity):
                    act.wait_ge(*group_done(l, g0 + j + 1))
                    pair = (g0 + parity) % 2
                    act.activation(sgm[:, parity, :], ps[:, 2 * pair, :], ACT.Sigmoid).then_inc(ffn_sig.sem, 1)
                for j in range(2):
                    gate_of(j, j)
                with loop(act, 0, 4) as i:
                    for j in range(2):
                        act.wait_ge(*group_evacuated(l, g0 + 2 * i + 1 + j))
                        gate_of(2 * i + 2 + j, j)
                act.wait_ge(*group_evacuated(l, g0 + 9))
                gate_of(10, 0)
                act.wait_ge(*down_done(l, (f + 1) * FJ))

            act.wait_ge(*c_turned(0, 1))
            act.activation(stat[:, 8:16], ps[:, 4, 0:8], ACT.Sigmoid).then_inc(c_sig.sem, 1)
            act.wait_ge(*x_loaded(0, 1))
            own.restart()
            with loop(act, 0, DEPTH) as l:
                act.wait_ge(*layer_open(l, 1))
                xs_ = [x[:, t, :] for t in range(TT)]
                sumsq(l, 1, xs_, 0)
                ffn(l, 0, IT_FFA)
                sumsq(l, 2, [ps[:, 4 + 2 * t:6 + 2 * t, :] for t in range(TT)], 0)
                act.wait_ge(*x_updated(l, 1))
                sumsq(l, 3, xs_, 0)

                act.wait_ge(*hT_ready(l, 2))

                def scaled(g, pair, mt0, n, last=P):
                    act.wait_ge(*group_done(l, g + 1))
                    for m in range(n):
                        cols = last if m == n - 1 else P
                        dst, mcol = mt0(m)
                        own.step(act.activation(dst, ps[0:cols, 2 * pair + m // 2, (m % 2) * S:(m % 2 + 1) * S],
                                                ACT.Identity, scale=der[0:cols, ds(mcol, 1)]))
                    act.sem_inc(shift_scaled.sem, 1)
                own.restart()
                with loop(act, 0, 3) as i:
                    for j in range(2):
                        g = group_of(IT_RW)
                        scaled(g + 2 * i + j, (g + j) % 2,
                               lambda m: (rkv[:, ds(i * 8 + j * 4 + m, 1), :], i * 8 + j * 4 + m + E_OMU), 4)
                    own.restart()
                g = group_of(IT_RW)
                scaled(g + 6, g % 2, lambda m: ((cw, ca)[m], 24 + m + E_OMU), 2)
                scaled(g + 7, (g + 1) % 2, lambda m: ((cg, cg2)[m], 26 + m + E_OMU), 2, 32)
                act.wait_ge(*group_evacuated(l, g + 8))
                own.step(act.activation(cw, cw, ACT.Tanh))
                own.step(act.activation(cg, cg, ACT.Sigmoid))
                act.activation(cg2, cg2, ACT.Sigmoid).then_inc(lora_act.sem, 1)
                act.wait_ge(*vlow_done(l, 1))
                act.activation(vrs, ps[0:32, 4, 0:S], ACT.Identity).then_inc(vlow_evac.sem, 1)
                for n in range(4):
                    act.wait_ge(*vmix_done(l, n + 1))
                    if n:
                        act.wait_ge(*v_final(l, n))
                    for m in range(2):
                        own.step(act.activation(vtmp[:, m * S:(m + 1) * S], ps[:, 4 + n % 2, m * S:(m + 1) * S], ACT.Sigmoid,
                                                bias=prm[:, C_V0 + 2 * n + m:C_V0 + 2 * n + m + 1]))
                    act.sem_inc(vmix_sig.sem, 1)
                act.wait_ge(*kk_eps(l, 1))
                act.activation(kk_sq_buf, kk_sq_buf, ACT.Sqrt).then_inc(kk_root.sem, 1)
                own.restart()
                def pair_decay(q):
                    act.wait_ge(*lora_done(l, q + 1))
                    for d in range(2):
                        own.step(act.activation(lwb[:, d, :, :], ps[:, 2 + d, 0:S], ACT.Tanh, scale=0.5,
                                                bias=der[:, ds(q + E_W0H + 8 * d, 1)]))
                        ins = act.activation(icl[:, d, :, :], ps[:, 2 + d, S:2 * S], ACT.Tanh, scale=0.5,
                                             bias=der[:, ds(q + E_A0H + 8 * d, 1)])
                        if d == 0:
                            own.step(ins)
                    ins.then_inc(lora_evac.sem, 1)
                    act.wait_ge(*cum_ready(l, q + 1))
                    own.step(act.activation(ege, ge, ACT.Exp))
                    own.step(act.activation(eni, gi, ACT.Exp, scale=-1.0))
                    act.activation(egi, gi, ACT.Exp).then_inc(exps_ready.sem, 1)

                def pair_body(p, last):
                    for d in range(2):
                        u = 2 * p + d
                        act.wait_ge(*turned_done(l, u + 1))
                        own.step(act.activation(btm[:, d], ps[:, 2, :], ACT.Identity))
                        act.activation(ktm[:, d], ps[:, 3, :], ACT.Identity).then_inc(turned_evac.sem, 1)
                    own.step(act.activation(etot[:, 0, :], egi[:, 0, :, L - 1], ACT.Identity))
                    act.activation(etot[:, 1, :], egi[:, 1, :, 0], ACT.Identity).then_inc(etot_ready.sem, 1)
                    act.wait_ge(*bonus_evac(l, p + 1))
                    act.activation(gate, ps[:, 0, 0:S], ACT.Identity).then_inc(gate_kept.sem, 1)
                    if not last:
                        pair_decay(p + 1)
                    own.restart()

                pair_decay(0)
                pair_body(0, False)
                with loop(act, 1, PAIRS - 1) as p:
                    pair_body(p, False)
                pair_body(PAIRS - 1, True)

                def gates(first):
                    for item in (first, first + (3 if first == IT_MM else 2)):
                        g = group_of(item)
                        act.wait_ge(*group_done(l, g + 1))
                        act.wait_ge(*group_evacuated(l, g))
                        act.activation(sg, halves(g % 2), ACT.Sigmoid).then_inc(gate_sig.sem, 1)

                act.wait_ge(*yr_ready(l, PAIRS))
                gates(IT_MR)

                g = group_of(IT_Z)
                act.wait_ge(*group_evacuated(l, g))
                with loop(act, 0, 2) as i:
                    for j in range(2):
                        act.wait_ge(*group_done(l, g + 2 * i + j + 1))
                        act.activation(zy[:, ds(2 * i + j, 1), :, :], halves((g + j) % 2), ACT.Sigmoid).then_inc(z_sig.sem, 1)
                g = group_of(IT_XBC)

                def conv(k, parity, turned_free, to_tok):
                    act.wait_ge(*group_done(l, g + k + 1))
                    if turned_free is not None:
                        act.wait_ge(*conv_turned(l, turned_free))
                    for m in range(4):
                        own.step(act.activation(cv[:, parity, m, :], ps[:, 2 * ((g + parity) % 2) + m // 2, (m % 2) * S:(m % 2 + 1) * S],
                                                ACT.Identity, scale=prm[:, ds(k * 4 + m + C_CONVW + 48, 1)],
                                                bias=prm[:, ds(k * 4 + m + C_CONVB, 1)]))
                    act.sem_inc(conv_scaled.sem, 1)
                    act.wait_ge(*conv_raw(l, k + 1))
                    act.activation(cvs, cv[:, parity, :, :], ACT.Sigmoid).then_inc(conv_sig.sem, 1)
                    if to_tok:
                        act.wait_ge(*conv_turned(l, k + 1))
                        for t in range(TT):
                            dst = xtm[:, t, ds(k * 512, 512)] if to_tok == 1 else btk[:, t, :]
                            own.step(act.activation(dst, ps[:, 4 + t, :], ACT.Identity))
                        act.sem_inc(conv_evac.sem, 1)
                own.restart()
                with loop(act, 0, 2) as i:
                    for j in range(2):
                        conv(2 * i + j, j, None, 1)
                    own.restart()
                conv(4, 0, None, 2)
                conv(5, 1, None, 0)
                act.wait_ge(*dt_raw(l, 1))
                own.step(act.activation(alog, alog, ACT.Exp))
                act.activation(dts[:, 1, :, :], dts[:, 1, :, :], ACT.Exp).then_inc(dt_exp.sem, 1)
                act.wait_ge(*acs_diff(l, 1))
                own.step(act.activation(dts[:, 4, :, :], dts[:, 4, :, :], ACT.Exp))
                act.activation(dts[:, 5, :, :], dts[:, 3, :, :], ACT.Exp).then_inc(acs_exp.sem, 1)
                with loop(act, 0, 4) as gg:
                    for n in range(4):
                        act.wait_ge(*seg_ready(l, 4 * gg + n + 1))
                        act.activation(wx[:, n, :, :], wx[:, n, :, :], ACT.Exp).then_inc(seg_exp.sem, 1)
                        if n % 2 == 0:
                            d = n // 2
                            act.wait_ge(*state_done(l, 2 * gg + d + 1))
                            with when(act, gg * 2 + d > 0):
                                act.wait_ge(*yoff_done(l, 2 * gg + d))
                            act.activation(h0, ps[:, 7, :], ACT.Identity).then_inc(state_evac.sem, 1)
                act.wait_ge(*ymT_ready(l, 4))
                gates(IT_MM)

                own.restart()
                act.wait_ge(*lam_raw(l, 1))
                act.activation(dstat[:, 26:28], dstat[:, 24:26], ACT.Exp).then_inc(lam_exp.sem, 1)
                def head_exp(h):
                    act.wait_ge(*smax_ready(l, h + 1))
                    for t in range(TT):
                        for m in range(2):
                            own.step(act.activation(pr[:, t, m, :], sc[:, t, m, :], ACT.Exp, scale=0.125,
                                                    bias=dstat[:, 4 + 2 * t + m:5 + 2 * t + m],
                                                    accum_out=dstat[:, 8 + 2 * t + m:9 + 2 * t + m]))
                    act.sem_inc(p_ready.sem, 1)

                def head_body(h, last):
                    act.wait_ge(*o_done(l, h + 1))
                    for t in range(TT):
                        own.step(act.activation(on[:, t, :], ps[:, 7, t * P:(t + 1) * P], ACT.Square,
                                                accum_out=dstat[:, 16 + t:17 + t]))
                    act.sem_inc(o_sq.sem, 1)
                    if not last:
                        head_exp(h + 1)
                    own.restart()

                head_exp(0)
                own.restart()
                with loop(act, 0, HEADS - 1) as h:
                    head_body(h, False)
                head_body(HEADS - 1, True)
                gates(IT_MD)
                act.wait_ge(*group_evacuated(l, group_of(IT_OUT) + 2))
                sumsq(l, 4, [merged[:, t, :] for t in range(TT)], 0)
                act.wait_ge(*x_updated(l, 2))
                sumsq(l, 5, xs_, 0)
                ffn(l, 1, IT_FFB)
                sumsq(l, 6, [ps[:, 4 + 2 * t:6 + 2 * t, :] for t in range(TT)], 0)
                own.restart()

        @block.vector
        def _(dve):
            own = Serial(dve, dve_own, settled)

            def tt(o, i0, i1, op):
                return dve.tensor_tensor(o, i0, i1, op)

            def ts(o, i0, s1, s2, op0, op1=ALU.bypass):
                return dve.tensor_scalar(o, i0, s1, s2, op0, op1)

            def stt(o, i0, s, i1, op0, op1):
                return dve.scalar_tensor_tensor(out=o, in0=i0, scalar=s, in1=i1, op0=op0, op1=op1)

            def evacuated(l, ins, group):
                own.raise_(ins, *group_evacuated(l, group + 1))

            def raised(ins, pair):
                own.raise_(ins, *pair)

            def make_rstd(l, k):
                dve.wait_ge(*sumsq_done(l, k))
                raised(ts(stat[:, 2:4], stat[:, 0:2], 1.0 / D, 1e-6, ALU.mult, ALU.add), mean_ready(l, k))
                dve.wait_ge(*rstd_ready(l, k))

            def norm_in(l, k, n, i):
                make_rstd(l, k)
                own.step(ts(xn[:, 0, :], x[:, 0, :], stat[:, 4:5], None, ALU.mult))
                raised(ts(xn[:, 1, :], x[:, 1, :], stat[:, 5:6], None, ALU.mult), xn_ready(l, n))
                dve.wait_ge(*xn_turned(l, n))
                for kt in range(KT):
                    ins = ts(hT[:, kt, :], ps[:, 4 + kt // 2, (kt % 2) * S:(kt % 2 + 1) * S],
                             modc[:, 16 * i + 8 + kt:16 * i + 9 + kt], modc[:, 16 * i + kt:16 * i + kt + 1],
                             ALU.mult, ALU.add)
                    if kt < KT - 1:
                        own.step(ins)
                raised(ins, hT_ready(l, n if n < 3 else 4))

            def residual(l, k, src, i, n):
                make_rstd(l, k)
                for t in range(TT):
                    own.step(stt(yt, src[t], stat[:, 4 + t:5 + t], gbc[:, i, :], ALU.mult, ALU.mult))
                    ins = tt(x[:, t, :], x[:, t, :], yt, ALU.add)
                    if t == 0:
                        own.step(ins)
                raised(ins, x_updated(l, n))

            def ffn(l, f, first):
                g0 = group_of(first)

                def hidden(j, parity, down_free):
                    pair = (g0 + parity) % 2
                    dve.wait_ge(*ffn_sig(l, f * FJ + j + 1))
                    own.step(tt(sgm[:, parity, :], sgm[:, parity, :], ps[:, 2 * pair, :], ALU.mult))
                    if down_free:
                        dve.wait_ge(*down_done(l, f * FJ + j - 1))
                    evacuated(l, tt(actT[:, parity, :, :], sgm[:, parity, :], ps[:, 2 * pair + 1, :], ALU.mult), g0 + j)
                hidden(0, 0, False)
                hidden(1, 1, False)
                own.restart()
                with loop(dve, 0, 4) as i:
                    hidden(2 * i + 2, 0, True)
                    hidden(2 * i + 3, 1, True)
                    own.restart()
                hidden(10, 0, True)

            dve.wait_ge(*consts_ready(0, 1))
            own.step(ts(sc_const, dist[:, :, :], -1.0, None, ALU.mult))
            own.step(tt(dist[:, :, :], dist[:, :, :], sc_const, ALU.max))
            dve.wait_ge(*c_sig(0, 1))
            raised(tt(ccol[:, :], stat[:, 8:16], ps[:, 4, 0:8], ALU.mult), c_ready(0, 1))
            own.restart()
            dve.wait_ge(*x_loaded(0, 1))
            dve.sem_inc(layer_open.sem, 1)

            with loop(dve, 0, DEPTH) as l:
                dve.wait_ge(*params_turned(l, 1))
                own.step(dve.tensor_copy(prm[:, :], ps[:, 4, :]))
                own.step(ts(der[:, E_OMU:E_OMU + 28], prm[:, C_MU:C_MU + 28], -1.0, 1.0, ALU.mult, ALU.add))
                own.step(ts(der[:, E_HMU:E_HMU + 28], prm[:, C_MU:C_MU + 28], 0.5, None, ALU.mult))
                own.step(ts(der[:, E_W0H:E_W0H + 32], prm[:, C_W0:C_W0 + 32], 0.5, None, ALU.mult))
                own.step(ts(der[:, E_KA1:E_KA1 + 8], prm[:, C_KA:C_KA + 8], -1.0, 1.0, ALU.mult, ALU.add))
                own.step(tt(der[:, E_SUB:E_SUB + 1], prm[:, C_SUB:C_SUB + 1],
                            laminit[:, ds(l, 1), 1:2].rearrange("p a b -> p (a b)"), ALU.mult))
                own.restart()
                def columns_of(first, n, bank):
                    return tt(modc[:, ds(first, 4)], ps[:, bank, 0:4], prm[:, ds(n + C_ADAB, 4)], ALU.add)

                def rows_of(i, half, bank):
                    o = gbc[:, ds(i, 1), half * 512:(half + 1) * 512]
                    return tt(o, o, ps[:, bank:bank + 1, :], ALU.add)

                def with_norm_weights(i, weights):
                    own.step(stt(modc[:, 16 * i + 8:16 * i + 16], modc[:, 16 * i + 8:16 * i + 16], 1.0,
                                 prm[:, C_NORM + 16 * i:C_NORM + 16 * i + 8], ALU.add, ALU.mult))
                    own.step(stt(gbc[:, i, :], gbc[:, i, :], halfc[:, i:i + 1], weights, ALU.mult, ALU.mult))

                with loop(dve, 0, 2) as i:
                    for b in range(6):
                        dve.wait_ge(*group_done(l, i * 6 + b + 1))
                        bank = 2 * (b % 2)
                        ins = columns_of(i * 16 + b * 4, i * 24 + b * 4, bank) if b < 4 else rows_of(i, b - 4, bank)
                        evacuated(l, ins, i * 6 + b)
                for i in range(2):
                    with_norm_weights(i, nbc[:, i, :])

                norm_in(l, 1, 1, 0)
                ffn(l, 0, IT_FFA)
                dve.wait_ge(*down_done(l, FJ))
                residual(l, 2, [ps[:, 4 + 2 * t:6 + 2 * t, :].rearrange("p a b -> p (a b)") for t in range(TT)], 0, 1)
                norm_in(l, 3, 2, 1)

                own.restart()
                g = group_of(IT_RW)

                def neighbours(gi_, pair, where, n, last=P):
                    dve.wait_ge(*shift_scaled(l, gi_ - g + 1))
                    for m in range(n):
                        cols = last if m == n - 1 else P
                        dst, mcol = where(m)
                        src = ps[0:cols, 2 * pair + m // 2, (m % 2) * S:(m % 2 + 1) * S]
                        h = der[0:cols, ds(mcol, 1)]
                        own.step(stt(dst[..., 1:S], src[:, 0:S - 1], h, dst[..., 1:S], ALU.mult, ALU.add))
                        ins = stt(dst[..., 0:S - 1], src[:, 1:S], h, dst[..., 0:S - 1], ALU.mult, ALU.add)
                        if m < n - 1:
                            own.step(ins)
                    evacuated(l, ins, gi_)
                with loop(dve, 0, 3) as i:
                    for j in range(2):
                        neighbours(g + 2 * i + j, (g + j) % 2,
                                   lambda m: (rkv[:, ds(i * 8 + j * 4 + m, 1), :].rearrange("p a s -> p (a s)"),
                                              i * 8 + j * 4 + m + E_HMU), 4)
                    own.restart()
                neighbours(g + 6, g % 2, lambda m: ((cw, ca)[m], 24 + m + E_HMU), 2)
                neighbours(g + 7, (g + 1) % 2, lambda m: ((cg, cg2)[m], 26 + m + E_HMU), 2, 32)

                with when(dve, l < 1):
                    dve.tensor_copy(vfirst[:, :, :], rkv[:, 16:24, :]).then_inc(vfirst_kept.sem, 1)
                    dve.wait_ge(*vfirst_kept(0, 1))
                own.step(tt(vfd, vfirst[:, :, :], rkv[:, 16:24, :], ALU.subtract))
                for kt in range(KT):
                    own.step(ts(kkT[:, kt, :], rkv[:, 8 + kt, :], prm[:, C_KK + kt:C_KK + kt + 1], None, ALU.mult))
                raised(tt(kk_sq_buf, kkT, kkT, ALU.mult), kk_sq(l, 1))
                for n in range(4):
                    dve.wait_ge(*vmix_sig(l, n + 1))
                    d2 = vfd[:, 2 * n:2 * n + 2, :]
                    own.step(tt(d2, d2, vtmp.rearrange("p (a s) -> p a s", a=2), ALU.mult))
                    v2 = rkv[:, 16 + 2 * n:18 + 2 * n, :]
                    raised(tt(v2, v2, d2, ALU.add), v_final(l, n + 1))
                dve.wait_ge(*kk_sum(l, 1))
                raised(ts(kk_sq_buf, ps[:, 4:8, :], 1e-12, None, ALU.add), kk_eps(l, 1))
                dve.wait_ge(*kk_root(l, 1))
                own.step(dve.reciprocal(kk_sq_buf, kk_sq_buf))
                own.step(stt(kkT, kkT, -1.0, kk_sq_buf, ALU.mult, ALU.mult))
                own.restart()

                f512 = "p d c t -> p (d c t)"
                ic2 = icl.rearrange("p d c t -> p d (c t)")

                def pair_rates(q):
                    dve.wait_ge(*lora_evac(l, q + 1))
                    own.step(ts(lwb, lwb, 1.0, NEG_EXP_HALF, ALU.add, ALU.mult))

                def pair_scan(q):
                    own.step(dve.tensor_tensor_scan(gi.rearrange(f512), reset[:, :, :].rearrange("p a b -> p (a b)"),
                                                    lwb.rearrange(f512), 0.0, ALU.mult, ALU.add))

                def pair_exclusive(q):
                    own.step(tt(ge[:, 0], gi[:, 0], lwb[:, 0], ALU.subtract))

                def pair_backward(q):
                    own.step(tt(ge[:, 1], gi[:, 1, :, L - 1:L].to_broadcast([P, CH, L]), gi[:, 1], ALU.subtract))

                def pair_backward_inclusive(q):
                    raised(tt(gi[:, 1], ge[:, 1], lwb[:, 1], ALU.add), cum_ready(l, q + 1))

                def pair_iclr(q):
                    own.step(ts(icl, icl, 1.0, 0.5, ALU.add, ALU.mult))

                def pair_key_factor(q):
                    own.step(ts(kdir, ic2, prm[:, ds(q + C_KA, 1)], der[:, ds(q + E_KA1, 1)], ALU.mult, ALU.add))

                def pair_keys(q):
                    own.step(tt(kdir, kdir, rkv[:, ds(q + 8, 1), :].to_broadcast([P, 2, S]), ALU.mult))

                def pair_key_sum(q):
                    own.step(tt(bprod, kdir[:, 0, :], kdir[:, 1, :], ALU.add))

                def pair_bonus_product(q):
                    raised(stt(bprod, bprod, prm[:, ds(q + C_RK, 1)], rkv[:, ds(q, 1), :].rearrange("p a s -> p (a s)"), ALU.mult, ALU.mult),
                           decay_ready(l, q + 1))

                def pair_removal(q):
                    own.step(stt(kb.rearrange("p d c t -> p d (c t)"), ic2, -1.0, kkT[:, ds(q, 1), :].to_broadcast([P, 2, S]),
                                 ALU.mult, ALU.mult))

                def pair_ops(p, d):
                    for h in range(2):
                        hh = slice(64 * h, 64 * h + 64)

                        def chunks(t, q):
                            return t[hh, ds(q, 1), :].rearrange("p a (c t) -> p (a c) t", c=CH)
                        own.step(tt(arX[hh, d, :, 0, h, :], chunks(kkT, p), ege[hh, d], ALU.mult))
                        own.step(tt(arX[hh, d, :, 1, h, :], chunks(rkv, p), egi[hh, d], ALU.mult))
                        own.step(tt(btX[hh, d, :, h, :], kb[hh, d], eni[hh, d], ALU.mult))
                        ins = tt(ktX[hh, d, :, h, :], kdir[hh, d, :].rearrange("p (c t) -> p c t", c=CH), eni[hh, d], ALU.mult)
                        if h == 0:
                            own.step(ins)
                    raised(ins, ops_ready(l, 2 * p + d + 1))

                def pair_norm(q):
                    dve.wait_ge(*y_done(l, q + 1))
                    yps = ps[:, 7, 0:S].rearrange("p (c t) -> p c t", c=CH)
                    own.step(dve.tensor_reduce(out=gstat[:, 0, :], in_=yps, op=ALU.add, axis=AX))
                    own.step(ts(gstat[:, 0, :], gstat[:, 0, :], 1.0 / L, None, ALU.mult))
                    own.step(tt(yy, yps, gstat[:, 0, :].rearrange("p (c a) -> p c a", a=1).to_broadcast([P, CH, L]), ALU.subtract))
                    own.step(tt(ysq, yy, yy, ALU.mult))
                    own.step(dve.tensor_reduce(out=gstat[:, 1, :], in_=ysq, op=ALU.add, axis=AX))
                    raised(ts(gstat[:, 2, :], gstat[:, 1, :], 1.0 / L, 64e-5, ALU.mult, ALU.add), gn_var(l, q + 1))

                def pair_scale(q):
                    dve.wait_ge(*gn_rstd(l, q + 1))
                    for h in range(2):
                        hh = slice(64 * h, 64 * h + 64)
                        ins = tt(yX[hh, :, h, :], yy[hh], gstat[hh, 3, :].rearrange("p (c a) -> p c a", a=1).to_broadcast([64, CH, L]), ALU.mult)
                        if h == 0:
                            own.step(ins)
                    raised(ins, yx_ready(l, q + 1))

                def pair_finish(q):
                    yf = ysq.rearrange("p c t -> p (c t)")
                    dve.wait_ge(*yt_done(l, q + 1))
                    own.step(ts(yf, ps[:, 1, S:2 * S], prm[:, ds(q + C_LNW, 1)], prm[:, ds(q + C_LNB, 1)], ALU.mult, ALU.add))
                    own.step(tt(yf, yf, bonus, ALU.add))
                    raised(tt(rkv[:, ds(q, 1), :].rearrange("p a s -> p (a s)"), yf, gate, ALU.mult), yr_ready(l, q + 1))

                def late_modulation(p, j, bank, columns):
                    g = group_of(IT_LATE) + 2 * (p - 1) + j
                    dve.wait_ge(*group_done(l, g + 1))
                    n = 8 * (p - 1) + 4 * j
                    evacuated(l, columns_of(n + 32, n + 48, bank) if columns else rows_of(2, j, bank), g)

                def pair_body(p, first, last, late=None):
                    if not first:
                        pair_norm(p - 1)
                    dve.wait_ge(*bonus_done(l, p + 1))
                    raised(dve.tensor_copy(vtm, ps[:, 1, 0:S]), vtm_ready(l, p + 1))
                    dve.wait_ge(*exps_ready(l, p + 1))
                    pair_ops(p, 0)
                    if late:
                        late_modulation(p, 0, 6, late == "columns")
                    if not first:
                        pair_scale(p - 1)
                    pair_ops(p, 1)
                    if not first:
                        pair_finish(p - 1)
                    raised(tt(bonus, ps[:, 0, S:2 * S], rkv[:, ds(p + 16, 1), :].rearrange("p a s -> p (a s)"), ALU.mult),
                           bonus_evac(l, p + 1))
                    b4 = [P, CH, P]
                    eye = ident[:, :].rearrange("p (a b) -> p a b", a=1).to_broadcast(b4)
                    for d in range(2):
                        u = 2 * p + d
                        dve.wait_ge(*m1_done(l, u + 1))
                        ddn = dd[:, d, :, 0, :]
                        ddt = dd[:, d, :, 1, :]
                        lm, lt = lvl[:, d], lvl[:, 1 - d]
                        rm = rmask[:, d, :, :].rearrange("p u t -> p (u t)").rearrange("p (a t) -> p a t", a=1).to_broadcast([P, 2, 2 * P])

                        def two(t, c):
                            return t[:, d, c:c + 2, :, :].rearrange("p c u t -> p c (u t)")
                        own.step(tt(ddn, ps[:, 4, :].rearrange("p (c t) -> p c t", c=CH), lm[:, 0:1, :].to_broadcast(b4), ALU.mult))
                        own.step(tt(two(mb, 0), ps[:, 5, :].rearrange("p (c t) -> p c t", c=2), rm, ALU.mult))
                        own.step(tt(two(mb, 2), ps[:, 6, :].rearrange("p (c t) -> p c t", c=2), rm, ALU.mult))
                        own.step(tt(ddn, ddn, eye, ALU.add))
                        own.step(tt(ddt, mb[:, d, :, 0, :], lt[:, 0:1, :].to_broadcast(b4), ALU.mult))
                        own.step(tt(ddt, ddt, eye, ALU.add))
                        dve.wait_ge(*m2_done(l, u + 1))
                        own.step(tt(two(mk, 0), ps[:, 7, :].rearrange("p (c t) -> p c t", c=2), rm, ALU.mult))
                        raised(tt(two(mk, 2), ps[:, 2, :].rearrange("p (c t) -> p c t", c=2), rm, ALU.mult), m2_evac(l, u + 1))
                        if late and d == 0:
                            late_modulation(p, 1, 3, late == "columns")
                    for k in range(LV):
                        w = p * 2 * LV + 2 * k
                        for d in range(2):
                            dve.wait_ge(*f_done(l, w + d + 1))
                            raised(tt(ee[:, d], ps[:, 2 + d, :].rearrange("p (c t) -> p c t", c=CH),
                                      lvl[:, d, k + 1:k + 2, :].to_broadcast(b4), ALU.mult), e_ready(l, w + d + 1))
                        for d in range(2):
                            dve.wait_ge(*de_done(l, w + d + 1))
                            if k < LV - 1:
                                src = ps[:, 4 + 2 * d:6 + 2 * d, :].rearrange("p u (c t) -> p u c t", c=CH)
                                dst = dd[:, d].rearrange("p c u t -> p u c t")
                            else:
                                src = ps[:, 5 + 2 * d, :].rearrange("p (c t) -> p c t", c=CH)
                                dst = dd[:, d, :, 1, :]
                            raised(tt(dst, dst, src, ALU.add), dd_ready(l, w + d + 1))
                    for j in range(CH):
                        dve.wait_ge(*r_done(l, 4 * p + j + 1))
                        raised(dve.tensor_copy(rs, ps[:, 4, 0:2 * L].rearrange("p (d v) -> p d v", d=2)), r_evac(l, 4 * p + j + 1))
                        if not last and j == 2:
                            pair_backward(p + 1)
                            pair_backward_inclusive(p + 1)
                        if not last and j == 3:
                            pair_keys(p + 1)
                        dve.wait_ge(*u_done(l, 4 * p + j + 1))
                        raised(dve.tensor_copy(us[:, j, :, :], ps[:, 5, 0:2 * L].rearrange("p (d v) -> p d v", d=2)), u_evac(l, 4 * p + j + 1))
                        if not last and j == 1:
                            pair_rates(p + 1)
                            pair_scan(p + 1)
                        if not last and j == 2:
                            pair_iclr(p + 1)
                        if j < CH - 1:
                            dve.wait_ge(*s_done(l, 3 * p + j + 1))
                            src = ps[:, 6, 0:2 * L].rearrange("p (d v) -> p d v", d=2)
                            if j:
                                own.step(tt(st8[:, j + 1, :, :], st8[:, j, :, :], src, ALU.add))
                                src = st8[:, j + 1, :, :]
                            else:
                                dve.wait_ge(*etot_ready(l, p + 1))
                            own.step(ts(st8[:, j + 1, 0, :], src[:, 0, :], etot[:, 0, j:j + 1], None, ALU.mult))
                            raised(ts(st8[:, j + 1, 1, :], src[:, 1, :], etot[:, 1, CH - 1 - j:CH - j], None, ALU.mult), s_evac(l, 3 * p + j + 1))
                        if not last and j == 1:
                            pair_exclusive(p + 1)
                        if not last and j == 2:
                            pair_key_factor(p + 1)
                        if not last and j == 3:
                            pair_key_sum(p + 1)
                            pair_bonus_product(p + 1)
                            pair_removal(p + 1)
                    own.restart()

                def pair_first():
                    pair_rates(0)
                    pair_scan(0)
                    pair_exclusive(0)
                    pair_backward(0)
                    pair_backward_inclusive(0)
                    pair_iclr(0)
                    pair_key_factor(0)
                    pair_keys(0)
                    pair_key_sum(0)
                    pair_bonus_product(0)
                    pair_removal(0)

                pair_first()
                pair_body(0, True, False)
                with loop(dve, 1, 3) as p:
                    pair_body(p, False, False, "columns")
                pair_body(3, False, False, "rows")
                with loop(dve, 4, PAIRS - 1) as p:
                    pair_body(p, False, False)
                pair_body(PAIRS - 1, False, True)
                dve.wait_ge(*late_weights_loaded(l, 1))
                with_norm_weights(2, merged[:, 0, :])
                pair_norm(PAIRS - 1)
                pair_scale(PAIRS - 1)
                pair_finish(PAIRS - 1)
                own.restart()

                def merge(first, b, ks, n0):
                    for h in range(2):
                        gg = group_of(first + h * (1 + ks))
                        dve.wait_ge(*gate_sig(l, n0 + h + 1))
                        dve.sem_inc(group_evacuated.sem, 1)
                        dve.wait_ge(*group_done(l, gg + 2))
                        dst = merged[:, :, h * 512:(h + 1) * 512]
                        if b == 0:
                            evacuated(l, tt(dst, sg, halves((gg + 1) % 2), ALU.mult), gg + 1)
                        else:
                            own.step(tt(sg, sg, halves((gg + 1) % 2), ALU.mult))
                            evacuated(l, tt(dst, dst, sg, ALU.add), gg + 1)

                merge(IT_MR, 0, 1, 0)

                g = group_of(IT_Z)
                with loop(dve, 0, 2) as i:
                    for j in range(2):
                        dve.wait_ge(*z_sig(l, 2 * i + j + 1))
                        zz = zy[:, ds(2 * i + j, 1), :, :].rearrange("p a t c -> p (a t) c")
                        evacuated(l, tt(zz, zz, halves((g + j) % 2), ALU.mult), g + 2 * i + j)
                gx = group_of(IT_XBC)

                def conv(k, parity, dst, copy_to=None):
                    dve.wait_ge(*conv_scaled(l, k + 1))
                    for m in range(4):
                        src = ps[:, 2 * ((gx + parity) % 2) + m // 2, (m % 2) * S:(m % 2 + 1) * S]
                        c = cv[:, parity, m, :]
                        for tap in (0, 1, 3, 4):
                            s = tap - 2
                            w = prm[:, ds(k * 4 + m + C_CONVW + 24 * tap, 1)]
                            o = c[:, -s:S] if s < 0 else c[:, 0:S - s]
                            i0 = src[:, 0:S + s] if s < 0 else src[:, s:S]
                            ins = stt(o, i0, w, o, ALU.mult, ALU.add)
                            if m < 3 or tap < 4:
                                own.step(ins)
                    raised(ins, conv_raw(l, k + 1))
                    dve.wait_ge(*conv_sig(l, k + 1))
                    sig = cvs.rearrange("p (a s) -> p a s", a=4)
                    if copy_to is not None:
                        own.step(tt(copy_to, cv[:, parity, :, :], sig, ALU.mult))
                    evacuated(l, tt(dst, cv[:, parity, :, :], sig, ALU.mult), gx + k)
                own.restart()
                with loop(dve, 0, 2) as i:
                    for j in range(2):
                        conv(2 * i + j, j, cv[:, j, :, :])
                    own.restart()
                conv(4, 0, cv[:, 0, :, :], bcT[:, 0:4, :])
                conv(5, 1, bcT[:, 4:8, :])

                T0, T1, T2, T3, T4, T5, T6, T7 = (dts[:, n, :, :] for n in range(8))
                b64 = [P, TT, 64]

                def rowbc(v):
                    return v.rearrange("p (a b) -> p a b", a=1).to_broadcast(b64)
                dve.wait_ge(*dt_done(l, 1))
                own.step(tt(T0, ps[:, 6, 0:128].rearrange("p (a b) -> p a b", a=TT), rowbc(dtb), ALU.add))
                own.step(ts(T1, T0, -1.0, None, ALU.mult))
                raised(tt(T1, T0, T1, ALU.min), dt_raw(l, 1))
                dve.wait_ge(*dt_exp(l, 1))
                own.step(ts(T2, T1, 2.0, None, ALU.add))
                own.step(dve.reciprocal(T2, T2))
                own.step(tt(T1, T1, T2, ALU.mult))
                own.step(tt(T2, T1, T1, ALU.mult))
                own.step(ts(T7, T2, 1.0 / 15, None, ALU.mult))
                for n in (13, 11, 9, 7, 5, 3):
                    own.step(stt(T7, T7, 1.0 / n, T2, ALU.add, ALU.mult))
                own.step(stt(T7, T7, 1.0, T1, ALU.add, ALU.mult))
                own.step(ts(T0, T0, 0.0, None, ALU.max))
                own.step(stt(T0, T7, 2.0, T0, ALU.mult, ALU.add))
                raised(stt(T6, T0, -1.0, rowbc(alog), ALU.mult, ALU.mult), da_ready(l, 1))
                dve.wait_ge(*acs_done(l, 1))
                own.step(dve.tensor_copy(T4, ps[:, 6, 0:128].rearrange("p (a b) -> p a b", a=TT)))
                raised(dve.tensor_copy(acsT, ps[0:64, 7, 0:S]), acs_evac(l, 1))
                dve.wait_ge(*acs_turned(l, 1))
                own.step(dve.tensor_copy(T3, ps[:, 7, 256:384].rearrange("p (a b) -> p a b", a=TT)))
                raised(tt(T4, T4, T3, ALU.subtract), acs_diff(l, 1))
                dve.wait_ge(*acs_exp(l, 1))
                own.restart()

                def heads(t, c, h0):
                    return t[:, c, h0].rearrange("p (h a) -> p h a", a=1).to_broadcast([P, 8, 64])

                with loop(dve, 0, 4) as gg:
                    dve.wait_ge(*cb_done(l, gg + 1))
                    for d in range(2):
                        ins = tt(cbm[:, d, :, :], ps[:, 4, 0:256].rearrange("p (c t) -> p c t", c=TT),
                                 tri[:, d:d + 1, :].to_broadcast([P, TT, P]), ALU.mult)
                        if d == 0:
                            own.step(ins)
                    raised(ins, cb_evac(l, gg + 1))
                    xg = [xtm[:, c, ds(gg * 512, 512)].rearrange("p (h q) -> p h q", h=8) for c in range(TT)]

                    def decay_differences(n):
                        c, d = n // 2, n % 2
                        dve.wait_ge(*acs_bc[n % 2](l, 2 * gg + n // 2 + 1))
                        a_s = dts[:, 3, c, ds(gg * 8 + d * 32, 8)].rearrange("p (h a) -> p h a", a=1).to_broadcast([P, 8, P])
                        own.step(tt(wx[:, n, :, :], bca[:, n % 2, :, :], a_s, ALU.subtract))
                        raised(ts(wx[:, n, :, :], wx[:, n, :, :], 0.0, None, ALU.min), seg_ready(l, 4 * gg + n + 1))

                    def scaled_inputs(n):
                        c, d = n // 2, n % 2
                        own.step(tt(xdt[:, n, :, :], xg[c], heads(dts[:, 0], c, ds(gg * 8 + d * 32, 8)), ALU.mult))

                    def weights(n):
                        c, d = n // 2, n % 2
                        dve.wait_ge(*seg_exp(l, 4 * gg + n + 1))
                        ins = tt(wx[:, n, :, :], wx[:, n, :, :], cbm[:, d, c:c + 1, :].to_broadcast([P, 8, P]), ALU.mult)
                        if d == 0:
                            own.step(ins)
                        else:
                            raised(ins, wx_ready(l, 2 * gg + c + 1))

                    def state_inputs(d):
                        raised(tt(xs, xdt[:, 3 * d, :, :], heads(dts[:, 4], d, ds(gg * 8 + d * 32, 8)), ALU.mult),
                               xs_ready(l, 2 * gg + d + 1))

                    def from_neighbour(d):
                        dve.wait_ge(*yoff_done(l, 2 * gg + d + 1))
                        raised(tt(ym[:, 1 - d, :].rearrange("p (h q) -> p h q", h=8), ps[:, 4, :].rearrange("p (h q) -> p h q", h=8),
                                  heads(dts[:, 5], 1 - d, ds(gg * 8 + d * 32, 8)), ALU.mult), yoff_evac(l, 2 * gg + d + 1))

                    scaled_inputs(0)
                    state_inputs(0)
                    decay_differences(0)
                    decay_differences(1)
                    scaled_inputs(3)
                    dve.wait_ge(*state_done(l, 2 * gg + 1))
                    state_inputs(1)
                    decay_differences(2)
                    from_neighbour(0)
                    decay_differences(3)
                    weights(0)
                    scaled_inputs(1)
                    weights(1)
                    from_neighbour(1)
                    scaled_inputs(2)
                    weights(2)
                    weights(3)
                    for c in range(TT):
                        dsk = dskip[:, ds(gg * 8, 8)].rearrange("p (h a) -> p h a", a=1).to_broadcast([P, 8, 64])
                        own.step(tt(ytmp.rearrange("p (h q) -> p h q", h=8), xg[c], dsk, ALU.mult))
                        own.step(tt(ym[:, c, :], ym[:, c, :], ytmp, ALU.add))
                    for c in range(TT):
                        dve.wait_ge(*ydiag_done(l, 2 * gg + c + 1))
                        raised(tt(ym[:, c, :], ym[:, c, :], ps[:, 5 + c, :], ALU.add), ydiag_evac(l, 2 * gg + c + 1))
                    zz = zy[:, ds(gg, 1), :, :].rearrange("p a t c -> p (a t) c")
                    own.step(tt(ym, ym, zz, ALU.mult))
                    for c in range(TT):
                        own.step(tt(ytmp, ym[:, c, :], ym[:, c, :], ALU.mult))
                        own.step(dve.tensor_reduce(out=mstat[:, c:c + 1], in_=ytmp, op=ALU.add, axis=AX))
                    raised(ts(mstat[:, 2:4], mstat[:, 0:2], 1.0 / 512, 1e-5, ALU.mult, ALU.add), msq_ready(l, gg + 1))
                    dve.wait_ge(*mrstd_ready(l, gg + 1))
                    own.step(ts(ym[:, 0, :], ym[:, 0, :], mstat[:, 4:5], None, ALU.mult))
                    raised(ts(ym[:, 1, :], ym[:, 1, :], mstat[:, 5:6], None, ALU.mult), ym_ready(l, gg + 1))
                    dve.wait_ge(*ym_turned(l, gg + 1))
                    for m in range(4):
                        dst = zy[:, ds(gg, 1), m // 2, (m % 2) * S:(m % 2 + 1) * S]
                        ins = ts(dst, ps[:, 5 + m // 2:6 + m // 2, (m % 2) * S:(m % 2 + 1) * S], prm[:, ds(gg * 4 + m + C_MNW, 1)], None, ALU.mult)
                        if m < 3:
                            own.step(ins)
                    raised(ins, ymT_ready(l, gg + 1))
                    own.restart()
                merge(IT_MM, 1, 2, 2)

                g = group_of(IT_DF)
                own.restart()
                with loop(dve, 0, 2) as i:
                    for j in range(2):
                        dve.wait_ge(*group_done(l, g + 2 * i + j + 1))
                        evacuated(l, dve.tensor_copy(qkT[:, ds(i * 8 + j * 4, 4), :].rearrange("p a s -> p (a s)"),
                                                     halves((g + j) % 2).rearrange("p a s -> p (a s)")), g + 2 * i + j)
                for j in range(2):
                    dve.wait_ge(*group_done(l, g + 4 + j + 1))
                    evacuated(l, dve.tensor_copy(vdm[:, :, j * 512:(j + 1) * 512], halves((g + j) % 2)), g + 4 + j)
                dve.wait_ge(*diff_w_loaded(l, 1))
                for n in range(2):
                    own.step(tt(dlam[:, 2 * n, :], dlam[:, 2 * n, :], dlam[:, 2 * n + 1, :], ALU.mult))
                    ins = dve.tensor_reduce(out=dstat[:, 24 + n:25 + n], in_=dlam[:, 2 * n, :], op=ALU.add, axis=AX)
                    if n == 0:
                        own.step(ins)
                raised(ins, lam_raw(l, 1))
                dve.wait_ge(*lam_exp(l, 1))
                own.step(tt(dstat[:, 28:29], dstat[:, 27:28], dstat[:, 26:27], ALU.subtract))
                own.step(tt(dstat[:, 28:29], dstat[:, 28:29], laminit[:, ds(l, 1), 0:1].rearrange("p a b -> p (a b)"), ALU.subtract))
                own.restart()
                def head_bias(h):
                    dve.wait_ge(*sc_done(l, h + 1))
                    for t in range(TT):
                        own.step(stt(sc[:, t, :, :], dist[:, t:t + 1, :].to_broadcast([P, 2, S]), slopes[:, ds(h, 1)],
                                     ps[:, 4 + t, :].rearrange("p (m s) -> p m s", m=2), ALU.mult, ALU.add))

                def head_max(h):
                    own.step(dve.tensor_reduce(out=dstat[:, 0:4], in_=sc.rearrange("p t m s -> p (t m) s"), op=ALU.max, axis=AX))
                    raised(ts(dstat[:, 4:8], dstat[:, 0:4], -0.125, None, ALU.mult), smax_ready(l, h + 1))

                def head_body(h, last):
                    dve.wait_ge(*p_ready(l, h + 1))
                    own.step(dve.reciprocal(dstat[:, 12:16], dstat[:, 8:12]))
                    for t in range(TT):
                        own.step(tt(dstat[:, 13 + 2 * t:14 + 2 * t], dstat[:, 13 + 2 * t:14 + 2 * t], dstat[:, 28:29], ALU.mult))
                        own.step(ts(am[:, t, :], pr[:, t, 0, :], dstat[:, 12 + 2 * t:13 + 2 * t], None, ALU.mult))
                        ins = stt(am[:, t, :], pr[:, t, 1, :], dstat[:, 13 + 2 * t:14 + 2 * t], am[:, t, :], ALU.mult, ALU.add)
                        if t == 0:
                            own.step(ins)
                    raised(ins, am_ready(l, h + 1))
                    if not last:
                        head_bias(h + 1)
                    dve.wait_ge(*am_turned(l, h + 1))
                    raised(dve.tensor_copy(amT.rearrange("p a s -> p (a s)"), ps[:, 6, :]), amT_ready(l, h + 1))
                    if not last:
                        head_max(h + 1)
                    dve.wait_ge(*o_sq(l, h + 1))
                    raised(ts(dstat[:, 18:20], dstat[:, 16:18], 1.0 / P, 1e-5, ALU.mult, ALU.add), o_mean(l, h + 1))
                    dve.wait_ge(*o_rstd(l, h + 1))
                    own.step(ts(on[:, 0, :], ps[:, 7, 0:P], dstat[:, 20:21], None, ALU.mult))
                    raised(ts(on[:, 1, :], ps[:, 7, P:2 * P], dstat[:, 21:22], None, ALU.mult), on_ready(l, h + 1))
                    dve.wait_ge(*on_turned(l, h + 1))
                    raised(ts(ydT[:, ds(h, 1), :].rearrange("p a s -> p (a s)"), ps[:, 6, 0:S], der[:, E_SUB:E_SUB + 1], None, ALU.mult), yd_ready(l, h + 1))
                    own.restart()

                head_bias(0)
                head_max(0)
                own.restart()
                with loop(dve, 0, HEADS - 1) as h:
                    head_body(h, False)
                head_body(HEADS - 1, True)
                merge(IT_MD, 2, 1, 4)

                dve.wait_ge(*merged_turned(l, 1))
                raised(dve.tensor_copy(hT[:, :, :].rearrange("p a s -> p (a s)"), ps[:, 4:8, :].rearrange("p a s -> p (a s)")), hT_ready(l, 3))
                for h in range(2):
                    g = group_of(IT_OUT + h)
                    dve.wait_ge(*group_done(l, g + 1))
                    evacuated(l, dve.tensor_copy(merged[:, :, h * 512:(h + 1) * 512], halves(g % 2)), g)
                residual(l, 4, [merged[:, t, :] for t in range(TT)], 1, 2)
                norm_in(l, 5, 3, 2)
                ffn(l, 1, IT_FFB)
                dve.wait_ge(*down_done(l, 2 * FJ))
                residual(l, 6, [ps[:, 4 + 2 * t:6 + 2 * t, :].rearrange("p a b -> p (a b)") for t in range(TT)], 2, 3)
                own.restart()
                dve.sem_inc(layer_open.sem, 1)


INPUTS = ["x", "c", "ada_w", "ada_b", "norm_w", "ffn_w13", "ffn_w2", "w_in", "rwkv_mu", "rwkv_w0", "rwkv_w2",
          "rwkv_a0", "rwkv_a2", "rwkv_g2", "rwkv_k_k", "rwkv_k_a", "rwkv_r_k", "rwkv_ln_w", "rwkv_ln_b", "rwkv_v0",
          "rwkv_v1", "rwkv_v2", "mamba_conv_w", "mamba_conv_b", "mamba_dt_bias", "mamba_a_log", "mamba_d",
          "mamba_norm_w", "diff_lambda", "diff_subln_w", "w_branch_rwkv", "w_branch_mamba", "w_branch_diff", "w_out"]


def kernel(**inputs):
    import numpy as np
    import concourse.bacc as bacc
    from concourse.bass_utils import run_bass_kernel_spmd

    nc = bacc.Bacc("TRN2", target_bir_lowering=False, num_devices=1)
    arrays, args = {}, {}
    for name in INPUTS:
        v = np.ascontiguousarray(inputs[name])
        arrays[f"in_{name}"] = v
        args[name] = nc.dram_tensor(f"in_{name}", v.shape, mybir.dt.from_np(v.dtype), kind="ExternalInput").ap()
    out = nc.dram_tensor("out", (1, S, D), F32, kind="ExternalOutput").ap()
    build(nc, args, out)
    return run_bass_kernel_spmd(nc, [arrays], core_ids=[0]).results[0]["out"]
```
